# Optimizing a Trainium2 kernel written in Bass

```python
import functools
import jax, jax.numpy as jnp
from jax import lax
import numpy as np

D_MODEL = 1024
BATCH = 1
SEQ = 128
DEPTH = 2
DEC_BATCH = 1
DEC_SEQ = 512
PAST_LEN = 128

GRID_W = 64
MIX_W = D_MODEL
N_GROUPS = 4
GW = MIX_W // N_GROUPS
CONV_K = 31
GLA_HEADS = 4
GLA_DK = GW // GLA_HEADS
GLA_DV = GW // GLA_HEADS
GLA_LR = 16
GLA_TAU = 16.0
GDN_HEADS = 4
GDN_DK = GW // GDN_HEADS
GDN_DV = GW // GDN_HEADS
GDN_CONV_K = 3
SC_K = 3
CHUNK = 64
D_FF = 2816
N_EXPERTS = 8
TOP_K = 2
D_FF_EXPERT = 1408
N_DENSE = (DEPTH + 1) // 2
N_MOE = DEPTH // 2
ALPHA = (2 * DEPTH) ** 0.25
BETA_INIT = (8 * DEPTH) ** -0.25
EPS = 1e-5
IN_SIZES = (GW, GW,
            GW, GW, GW, GW,
            2 * GLA_LR,
            GW, GW, GW, GW,
            GDN_HEADS,
            2 * GDN_HEADS,
            GW, GW, GW)
N_IN = 13 * GW + 2 * GLA_LR + 3 * GDN_HEADS

kernel_name = "hybrid_bidir_diffusion_trunk_step"

def _layer_norm(x, g, b):
    xf = x.astype(jnp.float32)
    xc = xf - jnp.mean(xf, -1, keepdims=True)
    var = jnp.mean(xc * xc, -1, keepdims=True)
    return (xc * lax.rsqrt(var + EPS)).astype(x.dtype) * g + b

def _rms(x):
    return x * lax.rsqrt(jnp.mean(x * x, -1, keepdims=True) + EPS)

def _l2norm(x):
    return x * lax.rsqrt(jnp.sum(x * x, -1, keepdims=True) + 1e-6)

def _heads(x, n):
    b, t, _ = x.shape
    return x.reshape(b, t, n, -1).transpose(0, 2, 1, 3)

def _unheads(x):
    b, n, t, d = x.shape
    return x.transpose(0, 2, 1, 3).reshape(b, t, n * d)

def _to_cols(x):
    b, t, ch = x.shape
    rows = t // GRID_W
    return x.reshape(b, rows, GRID_W, ch).transpose(0, 2, 1, 3).reshape(b, t, ch)

def _from_cols(x):
    b, t, ch = x.shape
    rows = t // GRID_W
    return x.reshape(b, GRID_W, rows, ch).transpose(0, 2, 1, 3).reshape(b, t, ch)

def _flip(a):
    return jnp.flip(a, axis=2)

def _dwconv(x, w):
    k = w.shape[0]
    return lax.conv_general_dilated(x, w[:, None, :].astype(x.dtype), (1,), [(k // 2, k // 2)],
                                    dimension_numbers=('NWC', 'WIO', 'NWC'),
                                    feature_group_count=x.shape[-1])

def _gla_chunk(q, k, v, log_a, s0):
    b, h, t, _ = q.shape
    n = t // CHUNK
    ch = lambda a: a.reshape(b, h, n, CHUNK, a.shape[-1])
    q, k, v, log_a = ch(q), ch(k), ch(v), ch(log_a)
    cum = jnp.cumsum(log_a, axis=3)
    tot = cum[:, :, :, -1]
    qe = q * jnp.exp(cum)
    ke = k * jnp.exp(-cum)
    kd = k * jnp.exp(tot[:, :, :, None] - cum)
    mask = jnp.tril(jnp.ones((CHUNK, CHUNK), bool))
    att = jnp.where(mask, jnp.einsum('bhncd,bhnsd->bhncs', qe, ke), 0.0)
    o = jnp.einsum('bhncs,bhnse->bhnce', att, v)
    upd = jnp.einsum('bhncd,bhnce->bhnde', kd, v)

    def step(s, inp):
        dec, u = inp
        return dec[..., None] * s + u, s

    s_fin, s_in = lax.scan(step, s0, (jnp.moveaxis(jnp.exp(tot), 2, 0), jnp.moveaxis(upd, 2, 0)))
    o = o + jnp.einsum('bhncd,nbhde->bhnce', qe, s_in)
    return o.reshape(b, h, t, -1), s_fin

def _gdn_chunk(q, k, v, beta, log_a, s0):
    b, h, t, _ = q.shape
    n = t // CHUNK
    ch = lambda a: a.reshape(b, h, n, CHUNK, a.shape[-1])
    q, k, v = ch(q), ch(k), ch(v)
    beta = beta.reshape(b, h, n, CHUNK)
    g = jnp.cumsum(log_a.reshape(b, h, n, CHUNK), axis=-1)
    incl = jnp.tril(jnp.ones((CHUNK, CHUNK), bool))
    strict = jnp.tril(jnp.ones((CHUNK, CHUNK), bool), -1)
    diff = g[..., :, None] - g[..., None, :]
    decay = jnp.where(incl, jnp.exp(jnp.where(incl, diff, 0.0)), 0.0)
    kb = k * beta[..., None]
    eye = jnp.eye(CHUNK, dtype=jnp.float32)
    lmat = jnp.where(strict, jnp.einsum('bhncd,bhnsd->bhncs', kb, k) * decay, 0.0)
    tinv = lax.linalg.triangular_solve(eye + lmat, jnp.broadcast_to(eye, lmat.shape),
                                       left_side=True, lower=True)
    u = jnp.einsum('bhncs,bhnse->bhnce', tinv, v * beta[..., None])
    w = jnp.einsum('bhncs,bhnsd->bhncd', tinv, kb * jnp.exp(g)[..., None])
    qk = jnp.einsum('bhncd,bhnsd->bhncs', q, k) * decay
    qg = q * jnp.exp(g)[..., None]
    kd = k * jnp.exp(g[..., -1:] - g)[..., None]
    gl = jnp.exp(g[..., -1])

    def step(s, inp):
        u_n, w_n, qk_n, qg_n, kd_n, gl_n = inp
        v_new = u_n - jnp.einsum('bhcd,bhde->bhce', w_n, s)
        o_n = jnp.einsum('bhcd,bhde->bhce', qg_n, s) + jnp.einsum('bhcs,bhse->bhce', qk_n, v_new)
        s = gl_n[..., None, None] * s + jnp.einsum('bhcd,bhce->bhde', kd_n, v_new)
        return s, o_n

    xs = (jnp.moveaxis(u, 2, 0), jnp.moveaxis(w, 2, 0), jnp.moveaxis(qk, 2, 0),
          jnp.moveaxis(qg, 2, 0), jnp.moveaxis(kd, 2, 0), jnp.moveaxis(gl, 2, 0))
    s_fin, o = lax.scan(step, s0, xs)
    return jnp.moveaxis(o, 0, 2).reshape(b, h, t, -1), s_fin

def _gla_mixer(q, k, v, gate, lr, w_lr, b_lr, norm_g, s0):
    b, t, _ = q.shape
    f32 = jnp.float32
    qh = _heads(q, GLA_HEADS).astype(f32) * GLA_DK ** -0.5
    kh = _heads(k, GLA_HEADS).astype(f32)
    vh = _heads(v, GLA_HEADS).astype(f32)
    z = jnp.einsum('btzr,zrc->btzc', lr.reshape(b, t, 2, GLA_LR), w_lr) + b_lr
    la = jax.nn.log_sigmoid(z.astype(f32)) / GLA_TAU
    la_f = _heads(la[:, :, 0], GLA_HEADS)
    la_b = _heads(la[:, :, 1], GLA_HEADS)
    o_f, s_f = _gla_chunk(qh, kh, vh, la_f, s0[:, 0])
    o_b, s_b = _gla_chunk(_flip(qh), _flip(kh), _flip(vh), _flip(la_b), s0[:, 1])
    o = _unheads(_rms(o_f + _flip(o_b))).astype(q.dtype)
    return o * norm_g * jax.nn.silu(gate), jnp.stack([s_f, s_b], axis=1)

def _gdn_mixer(q, k, v, gate, beta, dec, conv_w, a_log, dt_bias, norm_g, s0, latent):
    f32 = jnp.float32
    qkv = jnp.concatenate([q, k, v], axis=-1)
    bd = jnp.concatenate([beta, dec], axis=-1)
    if latent:
        qkv, bd = _to_cols(qkv), _to_cols(bd)
    b, t, _ = qkv.shape
    qkv = jax.nn.silu(_dwconv(qkv, conv_w))
    q, k, v = jnp.split(qkv, 3, axis=-1)
    qh = _l2norm(_heads(q, GDN_HEADS).astype(f32)) * GDN_DK ** -0.5
    kh = _l2norm(_heads(k, GDN_HEADS).astype(f32))
    vh = _heads(v, GDN_HEADS).astype(f32)
    bd = bd.astype(f32)
    bt = jax.nn.sigmoid(bd[..., :GDN_HEADS]).transpose(0, 2, 1)
    dd = bd[..., GDN_HEADS:].reshape(b, t, 2, GDN_HEADS)
    la = -jnp.exp(a_log.astype(f32)) * jax.nn.softplus(dd + dt_bias.astype(f32))
    la_f = la[:, :, 0].transpose(0, 2, 1)
    la_b = la[:, :, 1].transpose(0, 2, 1)
    o_f, s_f = _gdn_chunk(qh, kh, vh, bt, la_f, s0[:, 0])
    o_b, s_b = _gdn_chunk(_flip(qh), _flip(kh), _flip(vh), _flip(bt), _flip(la_b), s0[:, 1])
    o = _unheads(_rms(o_f + _flip(o_b))).astype(gate.dtype)
    if latent:
        o = _from_cols(o)
    return o * norm_g * jax.nn.silu(gate), jnp.stack([s_f, s_b], axis=1)

def _mixer(h, p, s0_gla, s0_gdn, latent):
    u = h @ p['w_in']
    idx = np.cumsum(IN_SIZES)[:-1].tolist()
    (a_val, a_gate, gq, gk, gv, gg, glr, dq, dk, dv, dgate, dbeta, ddec, sb, sc, sx) = jnp.split(u, idx, axis=-1)
    a = a_val * jax.nn.sigmoid(a_gate)
    a = _dwconv(a, p['conv_w']) + p['conv_b']
    a = jax.nn.silu(_layer_norm(a, p['conv_ln_g'], p['conv_ln_b'])) @ p['conv_pw']
    y_gla, st_gla = _gla_mixer(gq, gk, gv, gg, glr, p['gla_w_lr'], p['gla_b_lr'], p['gla_norm_g'], s0_gla)
    y_gdn, st_gdn = _gdn_mixer(dq, dk, dv, dgate, dbeta, ddec, p['gdn_conv_w'], p['gdn_a_log'],
                               p['gdn_dt_bias'], p['gdn_norm_g'], s0_gdn, latent)
    y_sc = sb * _dwconv(sc * sx, p['sc_conv_w'])
    y = jnp.concatenate([a, y_gla, y_gdn, y_sc], axis=-1) @ p['w_out']
    return y, st_gla, st_gdn

def _swiglu(h, w_gate, w_up, w_down):
    return (jax.nn.silu(h @ w_gate) * (h @ w_up)) @ w_down

def _moe(h, router, w_gate, w_up, w_down):
    b, t, d = h.shape
    xt = h.reshape(b * t, d)
    logits = (xt @ router).astype(jnp.float32)
    top_v, top_i = lax.top_k(logits, TOP_K)
    probs = jax.nn.softmax(top_v, axis=-1)
    combine = jnp.einsum('nk,nke->ne', probs,
                         jax.nn.one_hot(top_i, N_EXPERTS, dtype=jnp.float32)).astype(h.dtype)
    out = jnp.zeros_like(xt)
    for e in range(N_EXPERTS):
        out = out + combine[:, e:e + 1] * _swiglu(xt, w_gate[e], w_up[e], w_down[e])
    return out.reshape(b, t, d)

def _layer(x, mod, p, ffn, s0_gla, s0_gdn, latent):
    sh1, sc1, g1, sh2, sc2, g2 = jnp.split(mod, 6, axis=-1)
    m, st_gla, st_gdn = _mixer(x * (1 + sc1) + sh1, p, s0_gla, s0_gdn, latent)
    x = _layer_norm(ALPHA * x + g1 * m, p['ln1_g'], p['ln1_b'])
    f = ffn(x * (1 + sc2) + sh2)
    x = _layer_norm(ALPHA * x + g2 * f, p['ln2_g'], p['ln2_b'])
    return x, st_gla, st_gdn

def setup_inputs(seed: int = 0) -> dict:
    key = jax.random.key(seed)
    ks = list(jax.random.split(key, 40))
    f32 = jnp.float32
    nrm = lambda i, shape, s: jax.random.normal(ks[i], shape, f32) * s
    D = D_MODEL
    dt = jnp.exp(jax.random.uniform(ks[30], (DEPTH, 2, GDN_HEADS), f32, np.log(1e-3), np.log(1e-1)))
    return {
        'x_prompt': nrm(0, (BATCH, SEQ, D), 1.0),
        'x_sample': nrm(1, (DEC_BATCH, DEC_SEQ, D), 1.0),
        'c': nrm(2, (DEC_BATCH, D), 1.0),
        'state_gla': nrm(3, (DEC_BATCH, DEPTH, 2, GLA_HEADS, GLA_DK, GLA_DV), 1.0),
        'state_gdn': nrm(4, (DEC_BATCH, DEPTH, 2, GDN_HEADS, GDN_DK, GDN_DV), 0.5),
        'c_ctx': nrm(5, (D,), 1.0),
        'w_ada': nrm(6, (DEPTH, D, 6 * D), 0.5 * D ** -0.5),
        'b_ada': nrm(7, (DEPTH, 6 * D), 0.02),
        'w_in': nrm(8, (DEPTH, D, N_IN), D ** -0.5),
        'w_out': nrm(9, (DEPTH, MIX_W, D), BETA_INIT * MIX_W ** -0.5),
        'conv_w': nrm(10, (DEPTH, CONV_K, GW), CONV_K ** -0.5),
        'conv_b': nrm(11, (DEPTH, GW), 0.02),
        'conv_ln_g': 1.0 + nrm(12, (DEPTH, GW), 0.02),
        'conv_ln_b': nrm(13, (DEPTH, GW), 0.02),
        'conv_pw': nrm(14, (DEPTH, GW, GW), GW ** -0.5),
        'gla_w_lr': nrm(15, (DEPTH, 2, GLA_LR, GW), GLA_LR ** -0.5),
        'gla_b_lr': nrm(16, (DEPTH, 2, GW), 0.1),
        'gla_norm_g': 1.0 + nrm(17, (DEPTH, GW), 0.02),
        'gdn_conv_w': nrm(18, (DEPTH, GDN_CONV_K, 3 * GW), GDN_CONV_K ** -0.5),
        'gdn_a_log': jnp.log(jax.random.uniform(ks[19], (DEPTH, 2, GDN_HEADS), f32, 1.0, 16.0)),
        'gdn_dt_bias': jnp.log(jnp.expm1(dt)),
        'gdn_norm_g': 1.0 + nrm(20, (DEPTH, GW), 0.02),
        'sc_conv_w': nrm(21, (DEPTH, SC_K, GW), SC_K ** -0.5),
        'ln1_g': 1.0 + nrm(22, (DEPTH, D), 0.02),
        'ln1_b': nrm(23, (DEPTH, D), 0.02),
        'ln2_g': 1.0 + nrm(24, (DEPTH, D), 0.02),
        'ln2_b': nrm(25, (DEPTH, D), 0.02),
        'ffn_w_gate': nrm(26, (N_DENSE, D, D_FF), D ** -0.5),
        'ffn_w_up': nrm(27, (N_DENSE, D, D_FF), D ** -0.5),
        'ffn_w_down': nrm(28, (N_DENSE, D_FF, D), BETA_INIT * D_FF ** -0.5),
        'moe_router': nrm(29, (N_MOE, D, N_EXPERTS), D ** -0.5),
        'moe_w_gate': nrm(31, (N_MOE, N_EXPERTS, D, D_FF_EXPERT), D ** -0.5),
        'moe_w_up': nrm(32, (N_MOE, N_EXPERTS, D, D_FF_EXPERT), D ** -0.5),
        'moe_w_down': nrm(33, (N_MOE, N_EXPERTS, D_FF_EXPERT, D), BETA_INIT * D_FF_EXPERT ** -0.5),
    }

def reference(x_prompt, x_sample, c, state_gla, state_gdn, c_ctx, w_ada, b_ada, w_in, w_out,
              conv_w, conv_b, conv_ln_g, conv_ln_b, conv_pw, gla_w_lr, gla_b_lr, gla_norm_g,
              gdn_conv_w, gdn_a_log, gdn_dt_bias, gdn_norm_g, sc_conv_w, ln1_g, ln1_b, ln2_g, ln2_b,
              ffn_w_gate, ffn_w_up, ffn_w_down, moe_router, moe_w_gate, moe_w_up, moe_w_down):
    f32 = jnp.float32
    nb = x_prompt.shape[0]
    zero_gla = jnp.zeros((nb, 2, GLA_HEADS, GLA_DK, GLA_DV), f32)
    zero_gdn = jnp.zeros((nb, 2, GDN_HEADS, GDN_DK, GDN_DV), f32)
    y_p, y_s = x_prompt, x_sample
    gla_states, gdn_states = [], []
    for l in range(DEPTH):
        p = dict(w_in=w_in[l], w_out=w_out[l], conv_w=conv_w[l], conv_b=conv_b[l],
                 conv_ln_g=conv_ln_g[l], conv_ln_b=conv_ln_b[l], conv_pw=conv_pw[l],
                 gla_w_lr=gla_w_lr[l], gla_b_lr=gla_b_lr[l], gla_norm_g=gla_norm_g[l],
                 gdn_conv_w=gdn_conv_w[l], gdn_a_log=gdn_a_log[l], gdn_dt_bias=gdn_dt_bias[l],
                 gdn_norm_g=gdn_norm_g[l], sc_conv_w=sc_conv_w[l],
                 ln1_g=ln1_g[l], ln1_b=ln1_b[l], ln2_g=ln2_g[l], ln2_b=ln2_b[l])
        j = l // 2
        if l % 2 == 0:
            ffn = functools.partial(_swiglu, w_gate=ffn_w_gate[j], w_up=ffn_w_up[j], w_down=ffn_w_down[j])
        else:
            ffn = functools.partial(_moe, router=moe_router[j], w_gate=moe_w_gate[j],
                                    w_up=moe_w_up[j], w_down=moe_w_down[j])
        mod_ctx = (jax.nn.silu(c_ctx) @ w_ada[l] + b_ada[l])[None, None, :]
        mod_lat = (jax.nn.silu(c) @ w_ada[l] + b_ada[l])[:, None, :]
        y_p, s_gla, s_gdn = _layer(y_p, mod_ctx, p, ffn, zero_gla, zero_gdn, False)
        gla_states.append(s_gla.astype(x_prompt.dtype))
        gdn_states.append(s_gdn.astype(x_prompt.dtype))
        y_s, _, _ = _layer(y_s, mod_lat, p, ffn, state_gla[:, l].astype(f32), state_gdn[:, l].astype(f32), True)
    new_state_gla = jnp.stack(gla_states, axis=1)
    new_state_gdn = jnp.stack(gdn_states, axis=1)
    return (y_p, y_s, new_state_gla, new_state_gdn)


_drawn_inputs = setup_inputs


def setup_inputs(seed=0):
    import zlib

    import numpy as np

    out = dict(_drawn_inputs(seed))
    spreads = {}
    factors = {'state_gla': 8.0,
     'state_gdn': 4.674,
     'conv_b': 8.0,
     'conv_ln_g': 50.13,
     'conv_ln_b': 47.595,
     'gla_norm_g': 54.628,
     'gdn_norm_g': 56.307}
    for name, (base, spread) in spreads.items():
        noise = np.random.default_rng([zlib.crc32(name.encode()), seed]).standard_normal(out[name].shape)
        drawn = base * np.exp(spread * noise) if base else spread * noise
        out[name] = __import__('jax').numpy.asarray(drawn.astype(out[name].dtype))
    for name, factor in factors.items():
        out[name] = (out[name] * factor).astype(out[name].dtype)
    return out
```

```python
from contextlib import ExitStack

import concourse.bass as bass
from concourse import mybir

F32 = mybir.dt.float32
U32 = mybir.dt.uint32
ALU = mybir.AluOpType
ACT = mybir.ActivationFunctionType
AX = mybir.AxisListType

P = 128


class Signal:

    def __init__(self, sem):
        self.sem = sem
        self.n = 0
        self.base = 0

    def up(self, k=1):
        self.n += k
        return k

    def at(self, value):
        return self.base + value


def trunk_kernel(nc, a, out):
    DEPTH, D, N_IN = a["w_in"].shape
    CTX = a["x_prompt"].shape[1]
    LAT = a["x_sample"].shape[1]
    T = CTX + LAT
    TT = T // P
    KD = D // P
    GRID_W = 64
    ROWS = LAT // GRID_W
    CONV_K, GW = a["conv_w"].shape[1:]
    J = GW // P
    H = a["state_gla"].shape[3]
    DK = a["state_gla"].shape[4]
    LR = a["gla_w_lr"].shape[2]
    GLA_TAU = 16.0
    CHUNK = 64
    NCH = T // CHUNK
    NE = a["moe_w_gate"].shape[1]
    FE = a["moe_w_gate"].shape[3]
    FT = FE // P
    DENSE = a["ffn_w_gate"].shape[2] // FE
    ALPHA = (2 * DEPTH) ** 0.25
    EPS = 1e-5
    QSCALE = DK ** -0.5
    SEQS = ((0, CTX), (CTX, T))
    SHORT = ((0, 512), (512, T))
    assert D == 1024 and J == 2 and H == 4 and DK == 64 and CTX == P and T == 640 and FE == 11 * P

    UW = T + 4
    names = ["aval", "agate", "gq", "gk", "gv", "gg", "lr", "dq", "dk", "dv", "dgate", "bd", "sb", "sc", "sx"]
    widths = {n: GW for n in names} | {"lr": 2 * LR, "bd": 3 * H}
    in_tiles, slot, col = [], {}, 0
    for n in names:
        slot[n] = len(in_tiles)
        for c in range(0, widths[n], P):
            in_tiles.append((n, len(in_tiles), col + c, min(P, widths[n] - c)))
        col += widths[n]
    assert col == N_IN
    PADDED = ("dq", "dk", "dv", "sx")
    PERMUTED = ("dq", "dk", "dv", "bd")
    U = len(in_tiles)
    PW = T + 5

    rows_a = [("b_ada", 6 * KD), ("ln1_g", KD), ("ln1_b", KD), ("ln2_g", KD), ("ln2_b", KD), ("conv_b", J),
              ("conv_ln_g", J), ("conv_ln_b", J), ("gla_norm_g", J), ("gdn_norm_g", J), ("gla_b_lr", 2 * J),
              ("sc_conv_w", 3 * J), ("gdn_conv_w", 9 * J)]
    rows_b = [("conv_w", CONV_K * J), ("c", KD), ("c_ctx", KD)]

    def offsets(rows):
        at, o = {}, 0
        for n, k in rows:
            at[n] = o
            o += k
        assert o <= P
        return at, o
    at_a, n_a = offsets(rows_a)
    at_b, n_b = offsets(rows_b)

    RING = 10
    RW = FT * P
    PER_EXPERT = 2 * FT + KD
    assert PER_EXPERT % RING == 0

    ctx = ExitStack()
    with ctx:
        def sb(name, shape, dt=F32):
            return ctx.enter_context(nc.sbuf_tensor(name, shape, dt))

        signals = {}

        def sem(name, l=None):
            if l is None or name not in signals:
                signals[name] = Signal(ctx.enter_context(nc.semaphore(name)))
            signals[name].base = signals[name].n
            return signals[name]

        x = sb("x", [P, KD, T])
        h = sb("h", [P, KD, T])
        ring = sb("ring", [P, RING, RW])
        u = sb("u", [P, U, UW])
        tmp = sb("tmp", [P, 4, T])
        wide = sb("wide", [P, 4, 688])
        mod = sb("mod", [P, 6 * KD, 2])
        cond = sb("cond", [P, KD, 2])
        pa = sb("pa", [P, DEPTH, P])
        pb = sb("pb", [P, DEPTH, P])
        ident = sb("ident", [P, P])
        mean_d = sb("mean_d", [P, P])
        mean_g = sb("mean_g", [P, P])
        head_sum = sb("head_sum", [P, P])
        until = sb("until", [P, 2, P])
        before = sb("before", [P, 2, P])
        chunk_until = sb("chunk_until", [P, 2, P])
        level = sb("level", [P, 7, 2, P], mybir.dt.bfloat16)
        level0t = sb("level0t", [P, 2, P])
        w_lr = sb("w_lr", [2 * LR, 2 * GW])
        pw = sb("pw", [P, J, GW])
        router = sb("router", [P, KD, NE])
        dtb = sb("dtb", [P, 2 * H])
        nega = sb("nega", [P, 2 * H])
        eps_col = sb("eps_col", [P, 2])
        resets = sb("resets", [P, 2, T])
        psum = ctx.enter_context(nc.psum_tensor("psum", [P, 4, 1024], F32))

        def bank(n):
            return psum[:, n // 2, (n % 2) * 512:(n % 2) * 512 + 512]

        ctx.enter_context(nc.allow_non_contiguous_dma(reason="small loads"))

        ring_loaded = [sem(f"ring_loaded{s}") for s in range(RING)]
        ring_used = sem("ring_used")

        def column_block(w, c, n=P):
            return w[:, c:c + n].rearrange("(k p) n -> p k n", p=P)

        def ring_view(s, k, n=P):
            return ring[:, s, 0:k * n].rearrange("p (k n) -> p k n", n=n)

        stream = []
        parts = {}
        for l in range(DEPTH):
            blocks = [(a["w_ada"][l], m * P, P, KD) for m in range(6 * KD)]
            parts["ada", l] = (sum(map(len, stream)), len(blocks))
            stream.append(blocks)
            blocks = [(a["w_in"][l], c, n, KD) for _, _, c, n in in_tiles]
            parts["in", l] = (sum(map(len, stream)), len(blocks))
            stream.append(blocks)
            blocks = [(a["w_out"][l], m * P, P, KD) for m in range(KD)]
            parts["out", l] = (sum(map(len, stream)), len(blocks))
            stream.append(blocks)
            count = (DENSE if l % 2 == 0 else NE) * PER_EXPERT
            parts["ffn", l] = (sum(map(len, stream)), count)
            stream.append([None] * count)
        flat = [b for part in stream for b in part]

        def expert_block(l, e, i):
            if l % 2 == 0:
                wg, wu, wd = a["ffn_w_gate"][l // 2], a["ffn_w_up"][l // 2], a["ffn_w_down"][l // 2]
                if i < 2 * FT:
                    w = (wg, wu)[i % 2]
                    cols = w[:, bass.ds(e * FE + (i // 2) * P, P)]
                    return cols.rearrange("(k p) n -> p k n", p=P), KD
                rows = wd[bass.ds(e * FE, FE), (i - 2 * FT) * P:(i - 2 * FT + 1) * P]
                return rows.rearrange("(k p) n -> p k n", p=P), FT
            wg, wu, wd = a["moe_w_gate"][l // 2], a["moe_w_up"][l // 2], a["moe_w_down"][l // 2]
            if i < 2 * FT:
                w = (wg, wu)[i % 2]
                c = (i // 2) * P
                return w[bass.ds(e, 1), :, c:c + P].rearrange("a (k p) n -> p (a k) n", p=P), KD
            c = (i - 2 * FT) * P
            return wd[bass.ds(e, 1), :, c:c + P].rearrange("a (k p) n -> p (a k) n", p=P), FT

        def load_block(eng, n):
            if n >= RING:
                eng.wait_ge(ring_used.sem, ring_used.at(n - RING + 1))
            s = n % RING
            if flat[n] is None:
                l = next(l for l in range(DEPTH) if parts["ffn", l][0] <= n < sum(parts["ffn", l]))
                i = n - parts["ffn", l][0]
                src, k = expert_block(l, i // PER_EXPERT, i % PER_EXPERT)
                dst = ring_view(s, k)
            else:
                w, c, m, k = flat[n]
                src, dst = column_block(w, c, m), ring_view(s, k, m)
            eng.dma_start(dst, src).then_inc(ring_loaded[s].sem, 16)

        def load_ahead(eng, part):
            base, count = parts[part]
            for n in range(base + RING, base + count + RING):
                if n < len(flat):
                    load_block(eng, n)

        def block_landed(eng, n):
            eng.wait_ge(ring_loaded[n % RING].sem, ring_loaded[n % RING].at(16 * (n // RING + 1)))

        def start():
            small = sem("small_loaded")
            stage_in = sem("stage_loaded")
            x_in = sem("x_loaded")
            consts = sem("consts_built")
            turned = sem("start_turned")
            copied = sem("start_copied")
            act_copied = sem("start_act_copied")
            stage = wide[:, :, 0:P]
            x_rows = [u[:, 2 * t:2 * t + 2, :].rearrange("p s w -> p (s w)")[:, 0:D] for t in range(TT)]
            with nc.Block() as block:
                n_stage = 0

                @block.sync
                def _(sp):
                    for t in range(TT):
                        src = a["x_prompt"][0] if t == 0 else a["x_sample"][0, (t - 1) * P:t * P, :]
                        sp.dma_start(x_rows[t], src).then_inc(x_in.sem, x_in.up(16))
                    for n in range(RING):
                        load_block(sp, n)

                @block.gpsimd
                def _(pool):
                    def built(ins):
                        ins.then_inc(consts.sem, consts.up())
                        pool.wait_ge(consts.sem, consts.n)

                    def keep(v, pattern, base, mult):
                        built(nc.gpsimd.affine_select(out=v, in_=v, compare_op=ALU.is_ge, fill=0.0, base=base,
                                                      pattern=pattern, channel_multiplier=mult))
                    for v, value in ((ident, 0.0), (mean_d, 1.0 / D), (mean_g, 1.0 / GW), (head_sum, 1.0),
                                     (until, 1.0), (before, 1.0), (level, 1.0), (level0t, 1.0), (resets, 1.0)):
                        built(nc.gpsimd.memset(v[:], value))
                    built(nc.gpsimd.memset(w_lr[:], 0.0))
                    for t in range(0, T, CHUNK):
                        built(nc.gpsimd.memset(resets[:, 0, t:t + 1], 0.0))
                        built(nc.gpsimd.memset(resets[:, 1, t + CHUNK - 1:t + CHUNK], 0.0))
                    built(nc.gpsimd.memset(eps_col[:, 0:1], EPS))
                    built(nc.gpsimd.memset(eps_col[:, 1:2], 1e-6))
                    built(nc.gpsimd.affine_select(out=ident[:], in_=ident[:], compare_op=ALU.not_equal, fill=1.0,
                                                  base=0, pattern=[[-1, P]], channel_multiplier=1))

                    def same_block(v, size, dims):
                        n = P // size
                        v = v.rearrange("p (g c) -> p g c", c=size)
                        keep(v, [[-size, n], [0, size]], 0, 1)
                        keep(v, [[size, n], [0, size]], size - 1, -1)
                    same_block(head_sum[:], DK, 0)
                    for z, sign in ((0, 1), (1, -1)):
                        keep(until[:, z, :], [[sign, P]], 0, -sign)
                        keep(before[:, z, :], [[sign, P]], -1, -sign)
                        built(nc.gpsimd.tensor_copy(chunk_until[:, z, :], until[:, z, :]))
                        same_block(chunk_until[:, z, :], CHUNK, 0)
                        for b in range(7):
                            v = level[:, b, z, :]
                            size = 2 << b
                            if size < P:
                                same_block(v, size, 0)
                            w = v.rearrange("p (g i c) -> p g i c", i=2, c=size // 2)
                            own, other = w[:, :, z, :], w[:, :, 1 - z, :]
                            built(nc.gpsimd.memset(own, 0.0))
                            n = P // size
                            if z == 0:
                                keep(other, [[size, n], [0, size // 2]], size // 2 - 1, -1)
                            else:
                                keep(other, [[-size, n], [0, size // 2]], -(size // 2), 1)
                        built(nc.gpsimd.tensor_copy(level0t[:, 1 - z, :], level[:, 0, z, :]))

                @block.scalar
                def _(act):
                    k = 0
                    for l in range(DEPTH):
                        for rows, at, half in ((rows_a, at_a, 0), (rows_b, at_b, 1)):
                            for n, count in rows:
                                if n == "c":
                                    src = a["c"].rearrange("b (k p) -> (b k) p", p=P)
                                elif n == "c_ctx":
                                    src = a["c_ctx"].rearrange("(k p) -> k p", p=P)
                                else:
                                    w = a[n][l]
                                    if len(w.shape) == 2:
                                        w = w.rearrange("a b -> (a b)")
                                    src = w.rearrange("(k p) -> k p", p=P)
                                act.dma_start(stage[at[n]:at[n] + count, 2 * l + half, :], src).then_inc(stage_in.sem, stage_in.up(16))
                                k += 1
                    assert k == DEPTH * (len(rows_a) + len(rows_b))

                @block.tensor
                def _(pe):
                    pe.wait_ge(consts.sem, consts.at(consts.n))
                    pe.wait_ge(stage_in.sem, stage_in.at(stage_in.n))
                    for l in range(DEPTH):
                        nc.tensor.transpose(psum[:, 0, (2 * l) * P:(2 * l) * P + n_a], stage[0:n_a, 2 * l, :],
                                            ident[0:n_a, 0:n_a])
                        nc.tensor.transpose(psum[:, 0, (2 * l + 1) * P:(2 * l + 1) * P + n_b],
                                                      stage[0:n_b, 2 * l + 1, :], ident[0:n_b, 0:n_b]).then_inc(turned.sem, turned.up())
                    for t in range(TT):
                        pe.wait_ge(x_in.sem, x_in.at(16 * TT))
                        if t >= 3:
                            pe.wait_ge(copied.sem, copied.at(DEPTH * 2 + t - 2))
                        for k in range(KD):
                            ins = nc.tensor.transpose(psum[:, 1 + t % 3, k * P:(k + 1) * P],
                                                      x_rows[t][:, k * P:(k + 1) * P], ident[:])
                        ins.then_inc(turned.sem, turned.up())

                @block.vector
                def _(dve):
                    dve.wait_ge(turned.sem, turned.at(DEPTH))
                    for l in range(DEPTH):
                        nc.vector.tensor_copy(pa[:, l, 0:n_a], psum[:, 0, 2 * l * P:2 * l * P + n_a]).then_inc(copied.sem, copied.up())
                        nc.vector.tensor_copy(pb[:, l, 0:n_b],
                                                        psum[:, 0, (2 * l + 1) * P:(2 * l + 1) * P + n_b]).then_inc(copied.sem, copied.up())
                    for t in range(TT):
                        dve.wait_ge(turned.sem, turned.at(DEPTH + t + 1))
                        nc.vector.tensor_copy(
                            x[:, :, t * P:(t + 1) * P], psum[:, 1 + t % 3, :].rearrange("p (k n) -> p k n", n=P)).then_inc(copied.sem, copied.up())
            with nc.Block() as block:
                @block.scalar
                def _(act):
                    for s, n in ((0, "c_ctx"), (1, "c")):
                        nc.scalar.activation(cond[:, :, s], pb[:, 0, at_b[n]:at_b[n] + KD], ACT.Silu)

        def modulation(l):
            landed = sem("small_weights_landed", l)
            products = sem("ada_products", l)
            added = sem("ada_added", l)
            base, count = parts["ada", l]
            with nc.Block() as block:
                @block.sync
                def _(sp):
                    load_ahead(sp, ("ada", l))

                @block.gpsimd
                def _(pool):
                    for z in range(2):
                        pool.dma_start(w_lr[z * LR:(z + 1) * LR, z * GW:(z + 1) * GW], a["gla_w_lr"][l, z]).then_inc(landed.sem, landed.up(16))
                    pool.dma_start(pw[:], a["conv_pw"][l].rearrange("(k p) n -> p k n", p=P)).then_inc(landed.sem, landed.up(16))
                    pool.dma_start(dtb[:], a["gdn_dt_bias"][l].rearrange("a h -> (a h)").partition_broadcast(P)).then_inc(landed.sem, landed.up(16))
                    pool.dma_start(nega[:], a["gdn_a_log"][l].rearrange("a h -> (a h)").partition_broadcast(P)).then_inc(landed.sem, landed.up(16))
                    n = 5
                    if l % 2 == 1:
                        pool.dma_start(router[:], a["moe_router"][l // 2].rearrange("(k p) n -> p k n", p=P)).then_inc(landed.sem, landed.up(16))
                        n += 1
                    pool.wait_ge(landed.sem, landed.at(16 * n))

                @block.tensor
                def _(pe):
                    for m in range(count):
                        block_landed(pe, base + m)
                        w = ring_view((base + m) % RING, KD)
                        for k in range(KD):
                            ins = nc.tensor.matmul(psum[:, 0, 2 * m:2 * m + 2], w[:, k, :], cond[:, k, :],
                                                   start=(k == 0), stop=(k == KD - 1))
                        ins.then_inc(ring_used.sem, ring_used.up())

                @block.vector
                def _(dve):
                    dve.wait_ge(ring_used.sem, ring_used.at(base + count))
                    nc.vector.tensor_tensor(
                        mod[:], psum[:, 0, 0:2 * count].rearrange("p (m s) -> p m s", s=2),
                        pa[:, l, 0:count].unsqueeze(2).to_broadcast([P, count, 2]), ALU.add).then_inc(added.sem, added.up())
                    dve.wait_ge(added.sem, added.n)
                    for c in (1, 4):
                        v = mod[:, c * KD:(c + 1) * KD, :]
                        nc.vector.tensor_scalar(v, v, 1.0, None, ALU.add).then_inc(added.sem, added.up())

        def modulate(c):
            with nc.Block() as block:
                @block.vector
                def _(dve):
                    for k in range(0, KD, 2):
                        for s, (t0, t1) in enumerate(SEQS):
                            nc.vector.tensor_scalar(h[:, k, t0:t1], x[:, k, t0:t1], mod[:, (c + 1) * KD + k, s:s + 1],
                                                    mod[:, c * KD + k, s:s + 1], ALU.mult, ALU.add)

                @block.scalar
                def _(act):
                    for k in range(1, KD, 2):
                        for s, (t0, t1) in enumerate(SEQS):
                            nc.scalar.activation(h[:, k, t0:t1], x[:, k, t0:t1], ACT.Identity,
                                                 scale=mod[:, (c + 1) * KD + k, s:s + 1],
                                                 bias=mod[:, c * KD + k, s:s + 1])

        def project_in(l):
            products = ring_used
            base, count = parts["in", l]
            freed = [sem(f"in_tiles_copied_by_{e}", l) for e in ("scalar", "vector")]

            def copies(n, i):
                s, m = in_tiles[i][1], in_tiles[i][3]
                src = psum[0:m, i % 4, :]
                pad = 1 if n in PADDED else 0
                if n in PERMUTED:
                    lat = u[0:m, s, CTX + 2 * pad:T + 2 * pad].rearrange("p (c r) -> p c r", r=ROWS)
                    return [(u[0:m, s, pad:CTX + pad], src[:, 0:CTX]),
                            (lat, src[:, CTX:T].rearrange("p (r c) -> p c r", c=GRID_W))]
                if pad:
                    return [(u[0:m, s, pad:CTX + pad], src[:, 0:CTX]),
                            (u[0:m, s, CTX + 2 * pad:T + 2 * pad], src[:, CTX:T])]
                return [(u[0:m, s, 0:T], src[:, 0:T])]

            with nc.Block() as block:
                @block.sync
                def _(sp):
                    load_ahead(sp, ("in", l))

                @block.tensor
                def _(pe):
                    for i, (n, s, c, m) in enumerate(in_tiles):
                        block_landed(pe, base + i)
                        if i >= 4:
                            pe.wait_ge(freed[i % 2].sem, freed[i % 2].at((i - 4) // 2 + 1))
                        w = ring_view((base + i) % RING, KD, m)
                        for k in range(KD):
                            for c0, c1 in SHORT:
                                ins = nc.tensor.matmul(psum[0:m, i % 4, c0:c1], w[:, k, :], h[:, k, c0:c1],
                                                       start=(k == 0), stop=(k == KD - 1))
                        ins.then_inc(ring_used.sem, ring_used.up())

                @block.scalar
                def _(act):
                    for i in range(0, count, 2):
                        act.wait_ge(ring_used.sem, ring_used.at(base + i + 1))
                        for d, s in copies(in_tiles[i][0], i):
                            ins = nc.scalar.activation(d, s, ACT.Copy)
                        ins.then_inc(freed[0].sem, freed[0].up())

                @block.vector
                def _(dve):
                    for i in range(1, count, 2):
                        dve.wait_ge(ring_used.sem, ring_used.at(base + i + 1))
                        for d, s in copies(in_tiles[i][0], i):
                            ins = nc.vector.tensor_copy(d, s)
                        ins.then_inc(freed[1].sem, freed[1].up())

                @block.gpsimd
                def _(pool):
                    for n in PADDED:
                        for j in range(J):
                            for c in (0, CTX + 1, T + 2):
                                nc.gpsimd.memset(u[:, slot[n] + j, c:c + 1], 0.0)

        def conformer(l):
            PADC = CONV_K // 2
            CW = T + PADC
            ends = ((0, CTX), (CTX + PADC, CW))
            banks = ((0, 512), (512, CW))
            gate_done = sem("conf_gate", l)
            vector_done = sem("conf_vector", l)
            scalar_done = sem("conf_scalar", l)
            pool_done = sem("conf_pool", l)
            tensor_done = sem("conf_products", l)
            padded, conv = wide[:, 0:J, :], wide[:, J:2 * J, :]
            sg = [u[:, slot["agate"] + j, 0:T] for j in range(J)]
            sq = [u[:, slot["aval"] + j, 0:T] for j in range(J)]
            sq = tmp[:, :, :].rearrange("p a t -> p (a t)")
            sq = [sq[:, j * CW:(j + 1) * CW] for j in range(J)]
            std = tmp[:, :, :].rearrange("p a t -> p (a t)")[:, J * CW:(J + 1) * CW]
            with nc.Block() as block:
                @block.gpsimd
                def _(pool):
                    for j in range(J):
                        for c0, c1 in ((0, PADC), (CTX + PADC, CTX + 2 * PADC), (T + 2 * PADC, T + 3 * PADC)):
                            ins = nc.gpsimd.memset(padded[:, j, c0:c1], 0.0)
                            ins.then_inc(pool_done.sem, pool_done.up())

                @block.scalar
                def _(act):
                    for j in range(J):
                        nc.scalar.activation(sg[j], sg[j], ACT.Sigmoid).then_inc(scalar_done.sem, scalar_done.up())
                    for j in range(J):
                        act.wait_ge(vector_done.sem, vector_done.at(J * (CONV_K + 3) + j + 1))
                        nc.scalar.activation(sq[j], conv[:, j, 0:CW], ACT.Square).then_inc(scalar_done.sem, scalar_done.up())
                    act.wait_ge(tensor_done.sem, tensor_done.at(2))
                    nc.scalar.activation(std, psum[:, 1, 0:CW], ACT.Ln, bias=eps_col[:, 0:1]).then_inc(scalar_done.sem, scalar_done.up())
                    act.wait_ge(scalar_done.sem, scalar_done.n)
                    nc.scalar.activation(std, std, ACT.Exp, scale=-0.5).then_inc(scalar_done.sem, scalar_done.up())
                    for j in range(J):
                        act.wait_ge(vector_done.sem, vector_done.at(J * (CONV_K + 5) + j + 1))
                        nc.scalar.activation(conv[:, j, 0:CW], conv[:, j, 0:CW], ACT.Silu,
                                                  scale=pa[:, l, at_a["conv_ln_g"] + j:at_a["conv_ln_g"] + j + 1],
                                                  bias=pa[:, l, at_a["conv_ln_b"] + j:at_a["conv_ln_b"] + j + 1]).then_inc(scalar_done.sem, scalar_done.up())
                    act.wait_ge(tensor_done.sem, tensor_done.at(3))
                    for (t0, t1), (c0, c1) in zip(SEQS, ends):
                        nc.scalar.activation(h[:, 0, t0:t1], psum[:, 2, c0:c1], ACT.Copy).then_inc(scalar_done.sem, scalar_done.up())

                @block.vector
                def _(dve):
                    dve.wait_ge(pool_done.sem, pool_done.at(3 * J))
                    for j in range(J):
                        dve.wait_ge(scalar_done.sem, scalar_done.at(j + 1))
                        for s, (t0, t1) in enumerate(SEQS):
                            o = PADC * (s + 1)
                            nc.vector.tensor_tensor(padded[:, j, t0 + o:t1 + o], u[:, slot["aval"] + j, t0:t1],
                                                         sg[j][:, t0:t1], ALU.mult).then_inc(vector_done.sem, vector_done.up())
                    dve.wait_ge(vector_done.sem, vector_done.n)
                    for k in range(CONV_K):
                        for j in range(J):
                            w = pb[:, l, at_b["conv_w"] + k * J + j:at_b["conv_w"] + k * J + j + 1]
                            if k == 0:
                                b = pa[:, l, at_a["conv_b"] + j:at_a["conv_b"] + j + 1]
                                ins = nc.vector.tensor_scalar(conv[:, j, 0:CW], padded[:, j, 0:CW], w, b,
                                                              ALU.mult, ALU.add)
                            else:
                                dve.wait_ge(vector_done.sem, vector_done.n - 1)
                                ins = nc.vector.scalar_tensor_tensor(out=conv[:, j, 0:CW], in0=padded[:, j, k:k + CW],
                                                                     scalar=w, in1=conv[:, j, 0:CW],
                                                                     op0=ALU.mult, op1=ALU.add)
                            ins.then_inc(vector_done.sem, vector_done.up())
                    for j in range(J):
                        dve.wait_ge(vector_done.sem, vector_done.n)
                        nc.vector.memset(wide[:, 0, 0:1], 0.0).then_inc(vector_done.sem, vector_done.up())
                    dve.wait_ge(tensor_done.sem, tensor_done.at(1))
                    for j in range(J):
                        nc.vector.tensor_tensor(conv[:, j, 0:CW], conv[:, j, 0:CW], psum[:, 0, 0:CW], ALU.subtract).then_inc(vector_done.sem, vector_done.up())
                    dve.wait_ge(scalar_done.sem, scalar_done.at(J + J + 2))
                    for j in range(J):
                        nc.vector.memset(wide[:, 0, 0:1], 0.0).then_inc(vector_done.sem, vector_done.up())
                        dve.wait_ge(vector_done.sem, vector_done.n)
                    for j in range(J):
                        nc.vector.tensor_tensor(conv[:, j, 0:CW], conv[:, j, 0:CW], std, ALU.mult).then_inc(vector_done.sem, vector_done.up())
                    dve.wait_ge(tensor_done.sem, tensor_done.at(4))
                    for (t0, t1), (c0, c1) in zip(SEQS, ends):
                        nc.vector.tensor_copy(h[:, 1, t0:t1], psum[:, 3, c0:c1]).then_inc(vector_done.sem, vector_done.up())

                @block.tensor
                def _(pe):
                    pe.wait_ge(vector_done.sem, vector_done.at(J * (CONV_K + 2)))
                    for j in range(J):
                        for c0, c1 in banks:
                            ins = nc.tensor.matmul(psum[:, 0, c0:c1], mean_g[:], conv[:, j, c0:c1],
                                                   start=(j == 0), stop=(j == J - 1))
                    ins.then_inc(tensor_done.sem, tensor_done.up())
                    pe.wait_ge(scalar_done.sem, scalar_done.at(2 * J))
                    for j in range(J):
                        for c0, c1 in banks:
                            ins = nc.tensor.matmul(psum[:, 1, c0:c1], mean_g[:], sq[j][:, c0:c1],
                                                   start=(j == 0), stop=(j == J - 1))
                    ins.then_inc(tensor_done.sem, tensor_done.up())
                    pe.wait_ge(scalar_done.sem, scalar_done.at(2 * J + 2 + J))
                    for m in range(J):
                        for k in range(J):
                            for c0, c1 in banks:
                                ins = nc.tensor.matmul(psum[:, 2 + m, c0:c1], pw[:, k, m * P:(m + 1) * P],
                                                       conv[:, k, c0:c1], start=(k == 0), stop=(k == J - 1))
                        ins.then_inc(tensor_done.sem, tensor_done.up())

        def conv3(dve, vector_done, dst, src, w, width):
            nc.vector.tensor_scalar(dst, src[:, 0:width], w(0), None, ALU.mult).then_inc(vector_done.sem, vector_done.up())
            for k in (1, 2):
                dve.wait_ge(vector_done.sem, vector_done.n)
                nc.vector.scalar_tensor_tensor(out=dst, in0=src[:, k:k + width], scalar=w(k), in1=dst,
                                                    op0=ALU.mult, op1=ALU.add).then_inc(vector_done.sem, vector_done.up())

        def short_conv(l):
            vector_done = sem("short_vector", l)
            with nc.Block() as block:
                @block.vector
                def _(dve):
                    for j in range(J):
                        sx, sc, sbt = (u[:, slot[n] + j, :] for n in ("sx", "sc", "sb"))
                        for s, (t0, t1) in enumerate(SEQS):
                            v = sx[:, t0 + 1 + s:t1 + 1 + s]
                            nc.vector.tensor_tensor(v, v, sc[:, t0:t1], ALU.mult).then_inc(vector_done.sem, vector_done.up())
                        dve.wait_ge(vector_done.sem, vector_done.n)
                        cv = wide[:, j, 0:T + 1]
                        o = at_a["sc_conv_w"] + j
                        conv3(dve, vector_done, cv, sx, lambda k: pa[:, l, o + k * J:o + k * J + 1], T + 1)
                        dve.wait_ge(vector_done.sem, vector_done.n)
                        for s, (t0, t1) in enumerate(SEQS):
                            nc.vector.tensor_tensor(h[:, 3 * J + j, t0:t1], cv[:, t0 + s:t1 + s], sbt[:, t0:t1],
                                                         ALU.mult).then_inc(vector_done.sem, vector_done.up())

        def gla(l):
            q = [u[:, slot["gq"] + j, 0:T] for j in range(J)]
            k = [u[:, slot["gk"] + j, 0:T] for j in range(J)]
            v = [u[:, slot["gv"] + j, 0:T] for j in range(J)]
            gate = [u[:, slot["gg"] + j, 0:T] for j in range(J)]
            qe = [[u[:, j, 0:T] for j in range(J)], q]
            ke = [[u[:, J + j, 0:T] for j in range(J)], k]
            kd = [[wide[:, j, 0:T] for j in range(J)], [wide[:, J + j, 0:T] for j in range(J)]]
            free = slot["sb"]
            kd_tok = u[:, free:free + 4, :].rearrange("p s w -> p (s w)")[:, 0:TT * 2 * GW]\
                .rearrange("p (t z f) -> p t z f", t=TT, z=2)
            v_tok = u[:, free + 4:free + 6, :].rearrange("p s w -> p (s w)")[:, 0:TT * GW]\
                .rearrange("p (t f) -> p t f", t=TT)
            PAIRS = [(z, j) for z in range(2) for j in range(J)]
            dec = u[:, slot["lr"], 0:2 * J * NCH].rearrange("p (z j n) -> p z j n", z=2, j=J)
            vector_done = sem("gla_vector", l)
            scalar_done = sem("gla_scalar", l)
            tensor_done = sem("gla_products", l)
            VEC, SCA = 6, 8
            with nc.Block() as block:
                @block.tensor
                def _(pe):
                    for i, (z, j) in enumerate(PAIRS):
                        for c0, c1 in SHORT:
                            ins = nc.tensor.matmul(psum[:, i, c0:c1], w_lr[:, z * GW + j * P:z * GW + (j + 1) * P],
                                                   u[0:2 * LR, slot["lr"], c0:c1], start=True, stop=True)
                        ins.then_inc(tensor_done.sem, tensor_done.up())

                @block.scalar
                def _(act):
                    for i, (z, j) in enumerate(PAIRS):
                        o = at_a["gla_b_lr"] + z * J + j
                        b = pa[:, l, o:o + 1]
                        act.wait_ge(tensor_done.sem, tensor_done.at(i + 1))
                        if i:
                            act.wait_ge(vector_done.sem, vector_done.at(VEC * i))
                        nc.scalar.activation(tmp[:, 0, :], psum[:, i, 0:T], ACT.Identity, bias=b).then_inc(scalar_done.sem, scalar_done.up())
                        act.wait_ge(scalar_done.sem, scalar_done.n)
                        nc.scalar.activation(tmp[:, 1, :], tmp[:, 0, :], ACT.Abs).then_inc(scalar_done.sem, scalar_done.up())
                        act.wait_ge(scalar_done.sem, scalar_done.n)
                        nc.scalar.activation(tmp[:, 1, :], tmp[:, 1, :], ACT.Exp, scale=-1.0).then_inc(scalar_done.sem, scalar_done.up())
                        act.wait_ge(scalar_done.sem, scalar_done.n)
                        nc.scalar.activation(tmp[:, 1, :], tmp[:, 1, :], ACT.Ln, bias=1.0).then_inc(scalar_done.sem, scalar_done.up())
                        act.wait_ge(vector_done.sem, vector_done.at(VEC * i + 3))
                        nc.scalar.activation(tmp[:, 0, :], tmp[:, 2, :], ACT.Exp, scale=1.0 / GLA_TAU).then_inc(scalar_done.sem, scalar_done.up())
                        nc.scalar.activation(tmp[:, 3, :], tmp[:, 2, :], ACT.Exp, scale=-1.0 / GLA_TAU).then_inc(scalar_done.sem, scalar_done.up())
                        last = tmp[:, 2, :].rearrange("p (n c) -> p n c", c=CHUNK)
                        last = last[:, :, CHUNK - 1] if z == 0 else last[:, :, 0]
                        act.wait_ge(tensor_done.sem, tensor_done.at(len(PAIRS)))
                        nc.scalar.activation(dec[:, z, j, :], last, ACT.Exp, scale=1.0 / GLA_TAU).then_inc(scalar_done.sem, scalar_done.up())
                        act.wait_ge(vector_done.sem, vector_done.at(VEC * i + 5))
                        nc.scalar.activation(kd[z][j], tmp[:, 1, :], ACT.Exp, scale=1.0 / GLA_TAU).then_inc(scalar_done.sem, scalar_done.up())

                @block.vector
                def _(dve):
                    for i, (z, j) in enumerate(PAIRS):
                        dve.wait_ge(scalar_done.sem, scalar_done.at(SCA * i + 2))
                        nc.vector.tensor_scalar(tmp[:, 0, :], tmp[:, 0, :], 0.0, None, ALU.min).then_inc(vector_done.sem, vector_done.up())
                        dve.wait_ge(vector_done.sem, vector_done.n)
                        dve.wait_ge(scalar_done.sem, scalar_done.at(SCA * i + 4))
                        nc.vector.tensor_tensor(tmp[:, 0, :], tmp[:, 0, :], tmp[:, 1, :], ALU.subtract).then_inc(vector_done.sem, vector_done.up())
                        dve.wait_ge(vector_done.sem, vector_done.n)
                        cum, la, r = tmp[:, 2, :], tmp[:, 0, :], resets[:, z, :]
                        if z == 1:
                            cum, la, r = cum[:, ::-1], la[:, ::-1], r[:, ::-1]
                        nc.vector.tensor_tensor_scan(cum, r, la, 0.0, ALU.mult, ALU.add).then_inc(vector_done.sem, vector_done.up())
                        dve.wait_ge(scalar_done.sem, scalar_done.at(SCA * i + 6))
                        nc.vector.scalar_tensor_tensor(out=qe[z][j], in0=q[j], scalar=QSCALE, in1=tmp[:, 0, :],
                                                            op0=ALU.mult, op1=ALU.mult).then_inc(vector_done.sem, vector_done.up())
                        cums = tmp[:, 2, :].rearrange("p (n c) -> p n c", c=CHUNK)
                        last = cums[:, :, CHUNK - 1:CHUNK] if z == 0 else cums[:, :, 0:1]
                        dve.wait_ge(vector_done.sem, vector_done.n)
                        nc.vector.tensor_tensor(tmp[:, 1, :].rearrange("p (n c) -> p n c", c=CHUNK),
                                                     last.to_broadcast([P, NCH, CHUNK]), cums, ALU.subtract).then_inc(vector_done.sem, vector_done.up())
                        dve.wait_ge(scalar_done.sem, scalar_done.at(SCA * i + 8))
                        nc.vector.tensor_tensor(kd[z][j], kd[z][j], k[j], ALU.mult)
                        nc.vector.tensor_tensor(ke[z][j], k[j], tmp[:, 3, :], ALU.mult).then_inc(vector_done.sem, vector_done.up())

            copied_d, copied_e = sem("gla_turned_vector", l), sem("gla_turned_scalar", l)
            turned = sem("gla_turned", l)
            jobs = [(v[j], lambda j=j: v_tok[:, :, j * P:(j + 1) * P]) for j in range(J)] + \
                   [(kd[z][j], lambda z=z, j=j: kd_tok[:, :, z, j * P:(j + 1) * P]) for z, j in PAIRS]
            with nc.Block() as block:
                @block.tensor
                def _(pe):
                    for i, (src, _) in enumerate(jobs):
                        if i >= 4:
                            pe.wait_ge((copied_d, copied_e)[i % 2].sem, (copied_d, copied_e)[i % 2].at((i - 4) // 2 + 1))
                        for t in range(TT):
                            ins = nc.tensor.transpose(psum[:, i % 4, t * P:(t + 1) * P], src[:, t * P:(t + 1) * P],
                                                      ident[:])
                        ins.then_inc(turned.sem, turned.up())

                @block.vector
                def _(dve):
                    for i in range(0, len(jobs), 2):
                        dve.wait_ge(turned.sem, turned.at(i + 1))
                        nc.vector.tensor_copy(jobs[i][1](), psum[:, i % 4, 0:T].rearrange("p (t n) -> p t n", n=P)).then_inc(copied_d.sem, copied_d.up())

                @block.scalar
                def _(act):
                    for i in range(1, len(jobs), 2):
                        act.wait_ge(turned.sem, turned.at(i + 1))
                        nc.scalar.activation(jobs[i][1](), psum[:, i % 4, 0:T].rearrange("p (t n) -> p t n", n=P),
                                                         ACT.Copy).then_inc(copied_e.sem, copied_e.up())

            updates, states = sem("gla_updates", l), sem("gla_states", l)
            state_in, state_out = sem("gla_state_in", l), sem("gla_state_out", l)
            S = tmp[:].rearrange("p a t -> p (a t)").rearrange("p (z j n e) -> p z j n e", z=2, j=J, e=DK)
            final = wide[:, 0, 0:2 * J * DK].rearrange("p (z j e) -> p z j e", z=2, e=DK)
            CC = CTX // CHUNK

            def update(i, n):
                c = (n % 2) * 512 + (n // 2) * DK
                return psum[:, i, c:c + DK]
            orders = {0: (list(range(CC)), list(range(CC, NCH))), 1: (list(range(CC))[::-1], list(range(CC, NCH))[::-1])}
            with nc.Block() as block:
                @block.sync
                def _(sp):
                    for z, j in PAIRS:
                        sp.dma_start(S[:, z, j, orders[z][1][0], :],
                                     a["state_gla"][0, l, z, 2 * j:2 * j + 2].rearrange("h d e -> (h d) e")).then_inc(state_in.sem, state_in.up(16))
                    sp.wait_ge(states.sem, states.at(4 + 4 * NCH - 4))
                    for z, j in PAIRS:
                        sp.dma_start(out["gla"][0, l, z, 2 * j:2 * j + 2].rearrange("h d e -> (h d) e"),
                                     final[:, z, j, :]).then_inc(state_out.sem, state_out.up(16))
                    sp.wait_ge(state_out.sem, state_out.at(64))

                @block.tensor
                def _(pe):
                    for i, (z, j) in enumerate(PAIRS):
                        for n in range(NCH):
                            r0 = (n % 2) * CHUNK
                            for hp in range(2):
                                c = j * P + hp * DK
                                ins = nc.tensor.matmul(update(i, n)[hp * DK:(hp + 1) * DK, :],
                                                       kd_tok[r0:r0 + CHUNK, n // 2, z, c:c + DK],
                                                       v_tok[r0:r0 + CHUNK, n // 2, c:c + DK], start=True, stop=True)
                        ins.then_inc(updates.sem, updates.up())

                @block.vector
                def _(dve):
                    for z, j in PAIRS:
                        nc.vector.memset(S[:, z, j, orders[z][0][0], :], 0.0).then_inc(states.sem, states.up())
                    dve.wait_ge(states.sem, states.n)
                    dve.wait_ge(state_in.sem, state_in.at(64))
                    dve.wait_ge(updates.sem, updates.at(4))
                    for step in range(NCH - CC):
                        for seq in range(2):
                            for i, (z, j) in enumerate(PAIRS):
                                order = orders[z][seq]
                                if step >= len(order) or (seq == 1 and step == len(order) - 1):
                                    continue
                                n = order[step]
                                to = S[:, z, j, order[step + 1], :] if step + 1 < len(order) else final[:, z, j, :]
                                ins = nc.vector.scalar_tensor_tensor(
                                    out=to, in0=S[:, z, j, n, :], scalar=dec[:, z, j, n:n + 1],
                                    in1=update(i, n), op0=ALU.mult, op1=ALU.add)
                                ins.then_inc(states.sem, states.up())
                        dve.wait_ge(states.sem, states.n)

            scores, masked, outs, kept = (sem(f"gla_{n}", l) for n in ("scores", "masked", "outs", "kept"))
            att = u[:, free:free + 4, :].rearrange("p s w -> p (s w)")
            att = att[:, 0:4 * 512].rearrange("p (b h c) -> p b h c", b=4, h=H)
            o = [v[j] for j in range(J)]
            with nc.Block() as block:
                @block.tensor
                def _(pe):
                    def attend(t):
                        for z in range(2):
                            i = 2 * t + z
                            if i >= 3:
                                pe.wait_ge(masked.sem, masked.at(i - 2))
                            for hd in range(H):
                                r0 = (hd % 2) * DK
                                c = (hd % 2) * 512 + (hd // 2) * P
                                ins = nc.tensor.matmul(psum[:, i % 3, c:c + P],
                                                       ke[z][hd // 2][r0:r0 + DK, t * P:(t + 1) * P],
                                                       qe[z][hd // 2][r0:r0 + DK, t * P:(t + 1) * P],
                                                       start=True, stop=True)
                            ins.then_inc(scores.sem, scores.up())
                    attend(0)
                    for t in range(TT):
                        if t + 1 < TT:
                            attend(t + 1)
                        pe.wait_ge(masked.sem, masked.at(2 * t + 2))
                        if t >= 2:
                            pe.wait_ge(kept.sem, kept.at(t - 1))
                        for hd in range(H):
                            r0, j = (hd % 2) * DK, hd // 2
                            o_ps = bank(6 + t % 2)[r0:r0 + DK, j * P:(j + 1) * P]
                            for z in range(2):
                                nc.tensor.matmul(o_ps, v_tok[:, t, hd * DK:(hd + 1) * DK], att[:, (2 * t + z) % 4, hd, :],
                                                 start=(z == 0), stop=False, skip_group_check=True)
                            for z in range(2):
                                for c in range(2):
                                    n = 2 * t + c
                                    ins = nc.tensor.matmul(o_ps[:, c * CHUNK:(c + 1) * CHUNK],
                                                           S[r0:r0 + DK, z, j, n, :],
                                                           qe[z][j][r0:r0 + DK, n * CHUNK:(n + 1) * CHUNK],
                                                           start=False, stop=(z == 1), skip_group_check=True)
                        ins.then_inc(outs.sem, outs.up())

                @block.vector
                def _(dve):
                    for t in range(TT):
                        for z in range(2):
                            i = 2 * t + z
                            dve.wait_ge(scores.sem, scores.at(i + 1))
                            if i >= 4:
                                dve.wait_ge(outs.sem, outs.at(i // 2 - 1))
                            nc.vector.tensor_tensor(
                                att[:, i % 4, :, :].rearrange("p (j i) c -> p i j c", i=2),
                                psum[:, i % 3, :].rearrange("p (i r) -> p i r", i=2)[:, :, 0:J * P]
                                .rearrange("p i (j c) -> p i j c", j=J),
                                chunk_until[:, z, :].unsqueeze(1).unsqueeze(1).to_broadcast([P, 2, J, P]), ALU.mult).then_inc(masked.sem, masked.up())

                @block.scalar
                def _(act):
                    for t in range(TT):
                        act.wait_ge(outs.sem, outs.at(t + 1))
                        dst = u[:, slot["gv"]:slot["gv"] + J, t * P:(t + 1) * P]
                        nc.scalar.activation(dst, bank(6 + t % 2)[:, 0:J * P].rearrange("p (j c) -> p j c", j=J),
                                                     ACT.Copy).then_inc(kept.sem, kept.up())
            gated_norm(l, "gla", slot["gv"], slot["gg"], J, at_a["gla_norm_g"], permuted=False)

        def gated_norm(l, name, o_slot, gate_slot, mix, norm, permuted):
            scalar_done, tensor_done, vector_done = (sem(f"{name}_norm_{n}", l) for n in ("scalar", "products", "vector"))
            with nc.Block() as block:
                @block.scalar
                def _(act):
                    for j in range(J):
                        nc.scalar.activation(tmp[:, j, :], u[:, o_slot + j, 0:T], ACT.Square).then_inc(scalar_done.sem, scalar_done.up())
                    for j in range(J):
                        nc.scalar.activation(u[:, gate_slot + j, 0:T], u[:, gate_slot + j, 0:T], ACT.Silu).then_inc(scalar_done.sem, scalar_done.up())
                    for j in range(J):
                        act.wait_ge(tensor_done.sem, tensor_done.at(j + 1))
                        nc.scalar.activation(tmp[:, J + j, :], psum[:, j, 0:T], ACT.Ln, bias=eps_col[:, 0:1],
                                                  scale=1.0 / DK).then_inc(scalar_done.sem, scalar_done.up())
                    act.wait_ge(scalar_done.sem, scalar_done.n)
                    for j in range(J):
                        nc.scalar.activation(tmp[:, J + j, :], tmp[:, J + j, :], ACT.Exp, scale=-0.5).then_inc(scalar_done.sem, scalar_done.up())

                @block.tensor
                def _(pe):
                    for j in range(J):
                        pe.wait_ge(scalar_done.sem, scalar_done.at(j + 1))
                        for c0, c1 in SHORT:
                            ins = nc.tensor.matmul(psum[:, j, c0:c1], head_sum[:], tmp[:, j, c0:c1], start=True, stop=True)
                        ins.then_inc(tensor_done.sem, tensor_done.up())

                @block.vector
                def _(dve):
                    for j in range(J):
                        dve.wait_ge(scalar_done.sem, scalar_done.at(3 * J + j + 1))
                        o = u[:, o_slot + j, :]
                        nc.vector.tensor_tensor(o[:, 0:T], o[:, 0:T], tmp[:, J + j, :], ALU.mult).then_inc(vector_done.sem, vector_done.up())
                        dve.wait_ge(vector_done.sem, vector_done.n)
                        for t0, t1 in SEQS:
                            src, gt, dst = o[:, t0:t1], u[:, gate_slot + j, t0:t1], h[:, mix + j, t0:t1]
                            if permuted and t0:
                                src = src.rearrange("p (c r) -> p r c", r=ROWS)
                                gt, dst = (w.rearrange("p (r c) -> p r c", r=ROWS) for w in (gt, dst))
                            nc.vector.scalar_tensor_tensor(out=dst, in0=src, scalar=pa[:, l, norm + j:norm + j + 1],
                                                                in1=gt, op0=ALU.mult, op1=ALU.mult).then_inc(vector_done.sem, vector_done.up())

        def gdn(l):
            feat = [u[:, slot["dq"] + i, 0:T] for i in range(3 * J)]
            cv = [u[:, i, 0:T + 1] for i in range(3 * J)]

            def area(first, n, size):
                return u[:, first:first + n, :].rearrange("p s w -> p (s w)")[:, 0:size]
            k_tok = area(6, 2, TT * GW).rearrange("p (t f) -> p t f", t=TT)
            v_tok = area(8, 2, TT * GW).rearrange("p (t f) -> p t f", t=TT)
            o_acc = [u[:, 10 + j, 0:T] for j in range(J)]
            col = u[:, 12, :]
            beta = col[:, 0:TT * H].rearrange("p (t h) -> p t h", t=TT)
            dd = col[:, 20:20 + TT * 2 * H].rearrange("p (t z) -> p t z", t=TT)
            la = col[:, 60:60 + TT * 2 * H].rearrange("p (t z) -> p t z", t=TT)
            g = col[:, 100:100 + TT * 2 * H].rearrange("p (t z) -> p t z", t=TT)
            eg = col[:, 140:140 + TT * 2 * H].rearrange("p (t z) -> p t z", t=TT)
            t0c = col[:, 180:180 + TT * 2 * H].rearrange("p (t z) -> p t z", t=TT)
            vector_done, scalar_done, tensor_done = (sem(f"gdn_{n}", l) for n in ("vector", "scalar", "products"))
            with nc.Block() as block:
                @block.vector
                def _(dve):
                    for i in range(3 * J):
                        o = at_a["gdn_conv_w"] + i
                        conv3(dve, vector_done, cv[i], u[:, slot["dq"] + i, :], lambda k: pa[:, l, o + k * 3 * J:o + k * 3 * J + 1], T + 1)

                @block.scalar
                def _(act):
                    for i in range(3 * J):
                        act.wait_ge(vector_done.sem, vector_done.at(3 * (i + 1)))
                        for s, (a0, a1) in enumerate(SEQS):
                            nc.scalar.activation(feat[i][:, a0:a1], cv[i][:, a0 + s:a1 + s], ACT.Silu).then_inc(scalar_done.sem, scalar_done.up())
                    nc.scalar.activation(nega[:], nega[:], ACT.Exp).then_inc(scalar_done.sem, scalar_done.up())
            vector_done2, scalar_done2, tensor_done2 = (sem(f"gdn_norm_{n}", l) for n in ("vector2", "scalar2", "products2"))
            with nc.Block() as block:
                @block.scalar
                def _(act):
                    for i in range(2 * J):
                        nc.scalar.activation(tmp[:, i, :], feat[i], ACT.Square).then_inc(scalar_done2.sem, scalar_done2.up())
                    act.wait_ge(vector_done2.sem, vector_done2.at(2))
                    nc.scalar.activation(beta, beta, ACT.Sigmoid).then_inc(scalar_done2.sem, scalar_done2.up())
                    for i in range(2 * J):
                        act.wait_ge(tensor_done2.sem, tensor_done2.at(2 + i))
                        nc.scalar.activation(tmp[:, i, :], psum[:, i, 0:T], ACT.Ln, bias=eps_col[:, 1:2]).then_inc(scalar_done2.sem, scalar_done2.up())
                    act.wait_ge(scalar_done2.sem, scalar_done2.n)
                    for i in range(2 * J):
                        nc.scalar.activation(tmp[:, i, :], tmp[:, i, :], ACT.Exp, scale=-0.5).then_inc(scalar_done2.sem, scalar_done2.up())
                    act.wait_ge(vector_done2.sem, vector_done2.at(1))
                    nc.scalar.activation(t0c, dd, ACT.Abs).then_inc(scalar_done2.sem, scalar_done2.up())
                    act.wait_ge(scalar_done2.sem, scalar_done2.n)
                    nc.scalar.activation(t0c, t0c, ACT.Exp, scale=-1.0).then_inc(scalar_done2.sem, scalar_done2.up())
                    act.wait_ge(scalar_done2.sem, scalar_done2.n)
                    nc.scalar.activation(t0c, t0c, ACT.Ln, bias=1.0).then_inc(scalar_done2.sem, scalar_done2.up())

                @block.tensor
                def _(pe):
                    bdt = u[0:3 * H, slot["bd"], :]
                    for t in range(TT):
                        ins = nc.tensor.transpose(psum[:, 3, 768 + 16 * t:768 + 16 * t + 3 * H],
                                                  bdt[:, t * P:(t + 1) * P], ident[0:3 * H, 0:3 * H])
                    ins.then_inc(tensor_done2.sem, tensor_done2.up())
                    for i in range(2 * J):
                        pe.wait_ge(scalar_done2.sem, scalar_done2.at(i + 1))
                        for c0, c1 in SHORT:
                            if i == 3 and c0:
                                pe.wait_ge(vector_done2.sem, vector_done2.at(2))
                            ins = nc.tensor.matmul(psum[:, i, c0:c1], head_sum[:], tmp[:, i, c0:c1], start=True, stop=True)
                        ins.then_inc(tensor_done2.sem, tensor_done2.up())

                @block.vector
                def _(dve):
                    dve.wait_ge(tensor_done2.sem, tensor_done2.at(1))
                    nc.vector.tensor_tensor(
                        dd, psum[:, 3, 768:768 + TT * 16].rearrange("p (t c) -> p t c", c=16)[:, :, H:3 * H],
                        dtb[:].unsqueeze(1).to_broadcast([P, TT, 2 * H]), ALU.add).then_inc(vector_done2.sem, vector_done2.up())
                    nc.vector.tensor_copy(
                        beta, psum[:, 3, 768:768 + TT * 16].rearrange("p (t c) -> p t c", c=16)[:, :, 0:H]).then_inc(vector_done2.sem, vector_done2.up())
                    for i in range(2 * J):
                        dve.wait_ge(scalar_done2.sem, scalar_done2.at(10 + i))
                        if i < J:
                            nc.vector.scalar_tensor_tensor(out=feat[i], in0=feat[i], scalar=QSCALE,
                                                                 in1=tmp[:, i, :], op0=ALU.mult, op1=ALU.mult).then_inc(vector_done2.sem, vector_done2.up())
                        else:
                            nc.vector.tensor_tensor(feat[i], feat[i], tmp[:, i, :], ALU.mult).then_inc(vector_done2.sem, vector_done2.up())
                    dve.wait_ge(scalar_done2.sem, scalar_done2.at(16))
                    nc.vector.scalar_tensor_tensor(out=la, in0=dd, scalar=0.0, in1=t0c, op0=ALU.max, op1=ALU.add).then_inc(vector_done2.sem, vector_done2.up())
                    dve.wait_ge(vector_done2.sem, vector_done2.n)
                    nc.vector.scalar_tensor_tensor(out=la, in0=la, scalar=-1.0,
                                                         in1=nega[:].unsqueeze(1).to_broadcast([P, TT, 2 * H]),
                                                         op0=ALU.mult, op1=ALU.mult).then_inc(vector_done2.sem, vector_done2.up())
            scalar_done3, tensor_done3, vector_done3 = (sem(f"gdn_turn_{n}", l) for n in ("scalar3", "products3", "vector3"))
            with nc.Block() as block:
                @block.tensor
                def _(pe):
                    for i in range(4):
                        for t in range(TT):
                            ins = nc.tensor.transpose(psum[:, i, t * P:(t + 1) * P], feat[J + i][:, t * P:(t + 1) * P],
                                                      ident[:])
                        ins.then_inc(tensor_done3.sem, tensor_done3.up())
                    pe.wait_ge(vector_done3.sem, vector_done3.at(1))
                    for z in range(2):
                        ins = nc.tensor.matmul(psum[:, 0, z * TT * H:(z + 1) * TT * H], until[:, z, :],
                                               la[:, :, z * H:(z + 1) * H], start=True, stop=True)
                    ins.then_inc(tensor_done3.sem, tensor_done3.up())

                @block.vector
                def _(dve):
                    for i in (0, 2):
                        dve.wait_ge(tensor_done3.sem, tensor_done3.at(i + 1))
                        dst = (k_tok, v_tok)[i // 2][:, :, 0:P]
                        nc.vector.tensor_copy(dst, psum[:, i, 0:T].rearrange("p (t n) -> p t n", n=P)).then_inc(vector_done3.sem, vector_done3.up())
                    dve.wait_ge(tensor_done3.sem, tensor_done3.at(5))
                    nc.vector.tensor_copy(g.rearrange("p t (z h) -> p z t h", z=2),
                                                psum[:, 0, 0:2 * TT * H].rearrange("p (z t h) -> p z t h", z=2, t=TT)).then_inc(vector_done3.sem, vector_done3.up())

                @block.scalar
                def _(act):
                    for i in (1, 3):
                        act.wait_ge(tensor_done3.sem, tensor_done3.at(i + 1))
                        dst = (k_tok, v_tok)[i // 2][:, :, P:2 * P]
                        nc.scalar.activation(dst, psum[:, i, 0:T].rearrange("p (t n) -> p t n", n=P), ACT.Copy).then_inc(scalar_done3.sem, scalar_done3.up())
                    act.wait_ge(vector_done3.sem, vector_done3.at(3))
                    nc.scalar.activation(eg, g, ACT.Exp).then_inc(scalar_done3.sem, scalar_done3.up())
            gdn_chunks(l, feat, k_tok, v_tok, o_acc, beta, la, g, eg)
            gated_norm(l, "gdn", 10, slot["dgate"], 2 * J, at_a["gdn_norm_g"], permuted=True)

        def gdn_chunks(l, feat, k_tok, v_tok, o_acc, beta, la, g, eg):
            qf, kf = feat[0:J], feat[J:2 * J]
            rounds = [(0, 0)] + [(1 + i, TT - 1 - i) for i in range(TT - 1)]
            seen = set()
            first_visit = []
            for r in rounds:
                pair = []
                for t in r:
                    pair.append(t not in seen)
                    seen.add(t)
                first_visit.append(pair)
            flat_a = u[:, 0:6, :].rearrange("p s w -> p (s w)")
            flat_b = u[:, slot["sb"]:slot["sb"] + 6, :].rearrange("p s w -> p (s w)")
            flat_t = tmp[:].rearrange("p a t -> p (a t)")
            flat_w = wide[:].rearrange("p a t -> p (a t)")

            def bufs(f, n):
                return [f[:, i * 512:(i + 1) * 512].rearrange("p (h c) -> p h c", h=H) for i in range(n)]
            ba, bb, bt, bw = bufs(flat_a, 7), bufs(flat_b, 7), bufs(flat_t, 5), bufs(flat_w, 5)
            side_bufs = []
            for s, own, more in ((0, ba, bt), (1, bb, bw)):
                side_bufs.append(dict(D=own[0], LT=own[1], QK=own[2], Ti=own[3], TiT=own[4], X=own[5], M=own[6],
                                      EG=more[0], VB=more[1][:, :, 0:DK], KB=more[1][:, :, DK:2 * DK],
                                      KD=more[2][:, :, 0:DK], VN=more[2][:, :, DK:2 * DK],
                                      QG=more[3].rearrange("p h c -> p (h c)")[:, 0:J * P].rearrange("p (j c) -> p j c", j=J),
                                      WT=more[3].rearrange("p h c -> p (h c)")[:, J * P:2 * J * P].rearrange("p (j c) -> p j c", j=J),
                                      S=more[4].rearrange("p h c -> p (h c)")[:, 0:J * DK].rearrange("p (j e) -> p j e", j=J),
                                      EL=more[4].rearrange("p h c -> p (h c)")[:, 200:200 + H],
                                      EK=more[4].rearrange("p h c -> p (h c)")[:, 208:208 + H]))
            LV = 6
            names_ = ["decay_rows", "kk_qk", "turned_l", "x", "tx", "wt", "vn", "out", "upd"]
            tensor_done = {n: sem(f"gdnc_pe_{n}", l) for n in names_}
            vector_done = sem("gdnc_vector", l)
            scalar_done = sem("gdnc_scalar", l)
            pool_done = sem("gdnc_pool", l)
            st_in, st_out = sem("gdn_state_in", l), sem("gdn_state_out", l)

            DV = {n: i for i, n in enumerate(
                ["state", "dm", "dmin", "ek", "qg0", "qg1", "qkm", "ltb", "lt", "vb", "kd", "kb0", "kb", "ti0", "tit0"] +
                [f"{n}{b}" for b in range(LV) for n in ("t", "tt")] + ["vn", "oacc", "s0", "s1", "s2", "s3"])}
            AC = {n: i for i, n in enumerate(["exp", "eg", "el", "ekx"] + [f"x{b}" for b in range(LV)] + ["wt"])}
            PO = {n: i for i, n in enumerate(["strict"] + [f"m{b}" for b in range(LV)])}

            def dn(r, n, s):
                return (r * len(DV) + DV[n]) * 2 + s + 1

            def an(r, n, s):
                return (r * len(AC) + AC[n]) * 2 + s + 1

            def pn(r, n, s):
                return (r * len(PO) + PO[n]) * 2 + s + 1

            def en(r, s, per=1, i=0):
                return (r * per + i) * 2 + s + 1

            R = len(rounds)
            with nc.Block() as block:
                @block.sync
                def _(sp):
                    for s in range(2):
                        sp.wait_ge(vector_done.sem, vector_done.at(dn(0, "s3", s)))
                        for j in range(J):
                            sp.dma_start(out["gdn"][0, l, s, 2 * j:2 * j + 2].rearrange("h d e -> (h d) e"),
                                         side_bufs[s]["S"][:, j, :]).then_inc(st_out.sem, st_out.up(16))
                    for n in ("out",):
                        sp.wait_ge(tensor_done[n].sem, tensor_done[n].at(en(0, 1)))
                    sp.wait_ge(st_out.sem, st_out.at(64))
                    for s in range(2):
                        for j in range(J):
                            sp.dma_start(side_bufs[s]["S"][:, j, :],
                                         a["state_gdn"][0, l, s, 2 * j:2 * j + 2].rearrange("h d e -> (h d) e")).then_inc(st_in.sem, st_in.up(16))

                @block.tensor
                def _(pe):
                    for r, tiles in enumerate(rounds):
                        for s, t in enumerate(tiles):
                            B = side_bufs[s]
                            b0, b1, b2, b3 = (bank(4 * s + i) for i in range(4))
                            if r:
                                pe.wait_ge(vector_done.sem, vector_done.at(dn(r - 1, "s3", s)))
                            for hd in range(H):
                                nc.tensor.matmul(b0[:, hd * P:(hd + 1) * P],
                                                 la[:, t, s * H + hd:s * H + hd + 1].to_broadcast([P, P]),
                                                 until[:, s, :], start=True, stop=True)
                            for hd in range(H):
                                ins = nc.tensor.matmul(b3[:, hd * P:(hd + 1) * P],
                                                       beta[:, t, hd:hd + 1].to_broadcast([P, P]), ident[:],
                                                       start=True, stop=True)
                            ins.then_inc(tensor_done["decay_rows"].sem, tensor_done["decay_rows"].up())
                        for hp, (s, t) in ((i, side) for i in range(2) for side in enumerate(tiles)):
                            b0, b1, b2, b3 = (bank(4 * s + i) for i in range(4))
                            if hp == 1:
                                pe.wait_ge(tensor_done["kk_qk"].sem, tensor_done["kk_qk"].at((r * 2) * 2 + s + 1))
                            for hd in range(hp, H, 2):
                                r0, j = (hd % 2) * DK, hd // 2
                                ks = kf[j][r0:r0 + DK, t * P:(t + 1) * P]
                                nc.tensor.matmul(b1[:, hd * P:(hd + 1) * P], ks, ks, start=True, stop=True)
                                ins = nc.tensor.matmul(b2[:, hd * P:(hd + 1) * P], ks,
                                                       qf[j][r0:r0 + DK, t * P:(t + 1) * P], start=True, stop=True)
                            ins.then_inc(tensor_done["kk_qk"].sem, tensor_done["kk_qk"].up())
                        for s, t in enumerate(tiles):
                            B = side_bufs[s]
                            pe.wait_ge(vector_done.sem, vector_done.at(dn(r, "lt", s)))
                            for hd in range(H):
                                ins = nc.tensor.transpose(bank(4 * s + 3)[:, hd * P:(hd + 1) * P], B["LT"][:, hd, :], ident[:])
                            ins.then_inc(tensor_done["turned_l"].sem, tensor_done["turned_l"].up())
                        for b in range(LV):
                            for s, t in enumerate(tiles):
                                B = side_bufs[s]
                                b0 = bank(4 * s)
                                pe.wait_ge(pool_done.sem, pool_done.at(pn(r, f"m{b}", s)))
                                pe.wait_ge(vector_done.sem, vector_done.at(dn(r, "ti0" if b == 0 else f"tt{b - 1}", s)))
                                if b == 0:
                                    pe.wait_ge(scalar_done.sem, scalar_done.at(an(r, "ekx", s)))
                                else:
                                    pe.wait_ge(scalar_done.sem, scalar_done.at(an(r, f"x{b - 1}", s)))
                                for hd in range(H):
                                    ins = nc.tensor.matmul(b0[:, hd * P:(hd + 1) * P], B["M"][:, hd, :], B["Ti"][:, hd, :],
                                                           start=True, stop=True)
                                ins.then_inc(tensor_done["x"].sem, tensor_done["x"].up())
                            for s, t in enumerate(tiles):
                                B = side_bufs[s]
                                b1, b2 = bank(4 * s + 1), bank(4 * s + 2)
                                pe.wait_ge(scalar_done.sem, scalar_done.at(an(r, f"x{b}", s)))
                                pe.wait_ge(vector_done.sem, vector_done.at(dn(r, "tit0" if b == 0 else f"tt{b - 1}", s)))
                                for hd in range(H):
                                    if b < LV - 1:
                                        nc.tensor.matmul(b1[:, hd * P:(hd + 1) * P], B["TiT"][:, hd, :], B["X"][:, hd, :],
                                                         start=True, stop=True)
                                    ins = nc.tensor.matmul(b2[:, hd * P:(hd + 1) * P], B["X"][:, hd, :], B["TiT"][:, hd, :],
                                                           start=True, stop=True)
                                ins.then_inc(tensor_done["tx"].sem, tensor_done["tx"].up())
                        for s, t in enumerate(tiles):
                            B = side_bufs[s]
                            b3 = bank(4 * s + 3)
                            pe.wait_ge(vector_done.sem, vector_done.at(dn(r, f"tt{LV - 1}", s)))
                            for hd in range(H):
                                r0, j = (hd % 2) * DK, hd // 2
                                ins = nc.tensor.matmul(b3[r0:r0 + DK, j * P:(j + 1) * P], B["KB"][:, hd, :], B["TiT"][:, hd, :],
                                                       start=True, stop=True)
                            ins.then_inc(tensor_done["wt"].sem, tensor_done["wt"].up())
                        for s, t in enumerate(tiles):
                            B = side_bufs[s]
                            pe.wait_ge(scalar_done.sem, scalar_done.at(an(r, "wt", s)))
                            for hd in range(H):
                                r0, j = (hd % 2) * DK, hd // 2
                                vn = bank(4 * s + hd % 2)[:, j * DK:(j + 1) * DK]
                                nc.tensor.matmul(vn, B["TiT"][:, hd, :], B["VB"][:, hd, :], start=True, stop=False)
                                ins = nc.tensor.matmul(vn, B["WT"][r0:r0 + DK, j, :], B["S"][r0:r0 + DK, j, :],
                                                       start=False, stop=True)
                            ins.then_inc(tensor_done["vn"].sem, tensor_done["vn"].up())
                        for s, t in enumerate(tiles):
                            B = side_bufs[s]
                            b2, b3 = bank(4 * s + 2), bank(4 * s + 3)
                            pe.wait_ge(vector_done.sem, vector_done.at(dn(r, "vn", s)))
                            for hd in range(H):
                                r0, j = (hd % 2) * DK, hd // 2
                                o = b3[r0:r0 + DK, j * P:(j + 1) * P]
                                nc.tensor.matmul(o, B["VN"][:, hd, :], B["QK"][:, hd, :], start=True, stop=False)
                                ins = nc.tensor.matmul(o, B["S"][r0:r0 + DK, j, :], B["QG"][r0:r0 + DK, j, :],
                                                       start=False, stop=True)
                            ins.then_inc(tensor_done["out"].sem, tensor_done["out"].up())
                            for hd in range(H):
                                r0, j = (hd % 2) * DK, hd // 2
                                ins = nc.tensor.matmul(b2[r0:r0 + DK, j * DK:(j + 1) * DK], B["KD"][:, hd, :],
                                                       B["VN"][:, hd, :], start=True, stop=True)
                            ins.then_inc(tensor_done["upd"].sem, tensor_done["upd"].up())

                @block.scalar
                def _(act):
                    for r, tiles in enumerate(rounds):
                        def both(step):
                            for s, t in enumerate(tiles):
                                step(s, t, side_bufs[s])

                        def exp(s, t, B):
                            act.wait_ge(vector_done.sem, vector_done.at(dn(r, "dmin", s)))
                            nc.scalar.activation(B["D"], B["D"], ACT.Exp).then_inc(scalar_done.sem, scalar_done.up())

                        def egr(s, t, B):
                            act.wait_ge(vector_done.sem, vector_done.at(dn(r, "ek", s)))
                            if r:
                                act.wait_ge(vector_done.sem, vector_done.at(dn(r - 1, "qg1", s)))
                            nc.scalar.activation(B["EG"], bank(4 * s).rearrange("p (h c) -> p h c", h=H), ACT.Exp).then_inc(scalar_done.sem, scalar_done.up())

                        def el(s, t, B):
                            last = bank(4 * s).rearrange("p (h c) -> p h c", h=H)[:, :, (P - 1) if s == 0 else 0]
                            if r:
                                act.wait_ge(vector_done.sem, vector_done.at(dn(r - 1, "s3", s)))
                            nc.scalar.activation(B["EL"], last, ACT.Exp).then_inc(scalar_done.sem, scalar_done.up())

                        def ekx(s, t, B):
                            act.wait_ge(vector_done.sem, vector_done.at(dn(r, "ek", s)))
                            nc.scalar.activation(B["EK"], B["EK"], ACT.Exp).then_inc(scalar_done.sem, scalar_done.up())
                        for f in (exp, egr, el, ekx):
                            both(f)
                        for b in range(LV):
                            def xcopy(s, t, B):
                                act.wait_ge(tensor_done["x"].sem, tensor_done["x"].at(en(r, s, LV, b)))
                                if b:
                                    act.wait_ge(tensor_done["tx"].sem, tensor_done["tx"].at(en(r, s, LV, b - 1)))
                                nc.scalar.activation(B["X"], bank(4 * s).rearrange("p (h c) -> p h c", h=H), ACT.Copy).then_inc(scalar_done.sem, scalar_done.up())
                            both(xcopy)

                        def wt(s, t, B):
                            act.wait_ge(tensor_done["wt"].sem, tensor_done["wt"].at(en(r, s)))
                            nc.scalar.mul(B["WT"], bank(4 * s + 3)[:, 0:J * P].rearrange("p (j c) -> p j c", j=J), -1.0).then_inc(scalar_done.sem, scalar_done.up())
                        both(wt)

                @block.gpsimd
                def _(pool):
                    for r, tiles in enumerate(rounds):
                        for s, t in enumerate(tiles):
                            B = side_bufs[s]
                            pool.wait_ge(scalar_done.sem, scalar_done.at(an(r, "exp", s)))
                            nc.gpsimd.tensor_tensor(B["D"], B["D"], until[:, s:s + 1, :].to_broadcast([P, H, P]), ALU.mult).then_inc(pool_done.sem, pool_done.up())
                        for b in range(LV):
                            for s, t in enumerate(tiles):
                                B = side_bufs[s]
                                if b == 0:
                                    pool.wait_ge(vector_done.sem, vector_done.at(dn(r, "lt", s)))
                                else:
                                    pool.wait_ge(tensor_done["x"].sem, tensor_done["x"].at(en(r, s, LV, b - 1)))
                                nc.gpsimd.tensor_tensor(B["M"], B["LT"],
                                                              level[:, b + 1, s:s + 1, :].to_broadcast([P, H, P]), ALU.mult).then_inc(pool_done.sem, pool_done.up())

                @block.vector
                def _(dve):
                    def v3(n):
                        return bank(n).rearrange("p (h c) -> p h c", h=H)

                    for r, tiles in enumerate(rounds):
                        def both(step):
                            for s, t in enumerate(tiles):
                                step(s, t, side_bufs[s])

                        def state(s, t, B):
                            if r == 0:
                                ins = nc.vector.memset(B["S"], 0.0)
                            else:
                                if r == 1:
                                    dve.wait_ge(st_in.sem, st_in.at(64))
                                ins = nc.vector.memset(B["EK"], 0.0)
                            ins.then_inc(vector_done.sem, vector_done.up())

                        def dm(s, t, B):
                            dve.wait_ge(tensor_done["decay_rows"].sem, tensor_done["decay_rows"].at(en(r, s)))
                            if r:
                                dve.wait_ge(pool_done.sem, pool_done.at(pn(r - 1, f"m{LV - 1}", s)))
                            gz = g[:, t, s * H:(s + 1) * H].unsqueeze(2).to_broadcast([P, H, P])
                            nc.vector.tensor_tensor(B["D"], v3(4 * s), gz, ALU.subtract).then_inc(vector_done.sem, vector_done.up())

                        def dmin(s, t, B):
                            dve.wait_ge(vector_done.sem, vector_done.at(dn(r, "dm", s)))
                            nc.vector.tensor_scalar(B["D"], B["D"], 0.0, None, ALU.min).then_inc(vector_done.sem, vector_done.up())

                        def ek(s, t, B):
                            last = v3(4 * s)[:, :, (P - 1) if s == 0 else 0]
                            dve.wait_ge(vector_done.sem, vector_done.at(dn(r, "state", s)))
                            nc.vector.tensor_tensor(B["EK"], last, g[:, t, s * H:(s + 1) * H], ALU.subtract).then_inc(vector_done.sem, vector_done.up())

                        def qg(s, t, B, hp):
                            dve.wait_ge(scalar_done.sem, scalar_done.at(an(r, "eg", s)))
                            r0 = hp * DK
                            egv = B["EG"].rearrange("p (j i) c -> p j i c", i=2)[r0:r0 + DK, :, hp, :]
                            qv = u[r0:r0 + DK, slot["dq"]:slot["dq"] + J, t * P:(t + 1) * P]
                            nc.vector.tensor_tensor(B["QG"][r0:r0 + DK, :, :], qv, egv, ALU.mult).then_inc(vector_done.sem, vector_done.up())

                        def qkm(s, t, B):
                            dve.wait_ge(tensor_done["kk_qk"].sem, tensor_done["kk_qk"].at(en(r, s, 2, 1)))
                            dve.wait_ge(pool_done.sem, pool_done.at(pn(r, "strict", s)))
                            nc.vector.tensor_tensor(B["QK"], v3(4 * s + 2), B["D"], ALU.mult).then_inc(vector_done.sem, vector_done.up())

                        def ltb(s, t, B):
                            nc.vector.tensor_tensor(B["LT"], v3(4 * s + 1), B["D"], ALU.mult).then_inc(vector_done.sem, vector_done.up())

                        def lt(s, t, B):
                            dve.wait_ge(vector_done.sem, vector_done.at(dn(r, "ltb", s)))
                            nc.vector.tensor_tensor(B["LT"], v3(4 * s + 3), B["LT"], ALU.mult).then_inc(vector_done.sem, vector_done.up())

                        def vb(s, t, B):
                            bt = beta[:, t, :].unsqueeze(2).to_broadcast([P, H, DK])
                            nc.vector.tensor_tensor(B["VB"], v_tok[:, t, :].rearrange("p (h e) -> p h e", h=H), bt, ALU.mult).then_inc(vector_done.sem, vector_done.up())

                        def kdec(s, t, B):
                            dve.wait_ge(scalar_done.sem, scalar_done.at(an(r, "ekx", s)))
                            bt = B["EK"].unsqueeze(2).to_broadcast([P, H, DK])
                            nc.vector.tensor_tensor(B["KD"], k_tok[:, t, :].rearrange("p (h e) -> p h e", h=H), bt, ALU.mult).then_inc(vector_done.sem, vector_done.up())

                        def kb0(s, t, B):
                            bt = beta[:, t, :].unsqueeze(2).to_broadcast([P, H, DK])
                            nc.vector.tensor_tensor(B["KB"], k_tok[:, t, :].rearrange("p (h e) -> p h e", h=H), bt, ALU.mult).then_inc(vector_done.sem, vector_done.up())

                        def kb(s, t, B):
                            dve.wait_ge(vector_done.sem, vector_done.at(dn(r, "kb0", s)))
                            bt = eg[:, t, s * H:(s + 1) * H].unsqueeze(2).to_broadcast([P, H, DK])
                            nc.vector.tensor_tensor(B["KB"], B["KB"], bt, ALU.mult).then_inc(vector_done.sem, vector_done.up())

                        def ti0(s, t, B):
                            dve.wait_ge(tensor_done["turned_l"].sem, tensor_done["turned_l"].at(en(r, s)))
                            m = level0t[:, s:s + 1, :].to_broadcast([P, H, P])
                            nc.vector.tensor_tensor(B["Ti"], v3(4 * s + 3), m, ALU.mult).then_inc(vector_inner.sem, 1)
                            vector_inner.n += 1
                            dve.wait_ge(vector_inner.sem, vector_inner.n)
                            nc.vector.scalar_tensor_tensor(out=B["Ti"], in0=B["Ti"], scalar=-1.0,
                                                                 in1=ident[:].unsqueeze(1).to_broadcast([P, H, P]),
                                                                 op0=ALU.mult, op1=ALU.add).then_inc(vector_done.sem, vector_done.up())

                        def tit0(s, t, B):
                            m = level[:, 0, s:s + 1, :].to_broadcast([P, H, P])
                            nc.vector.tensor_tensor(B["TiT"], B["LT"], m, ALU.mult).then_inc(vector_inner.sem, 1)
                            vector_inner.n += 1
                            dve.wait_ge(vector_inner.sem, vector_inner.n)
                            nc.vector.scalar_tensor_tensor(out=B["TiT"], in0=B["TiT"], scalar=-1.0,
                                                                 in1=ident[:].unsqueeze(1).to_broadcast([P, H, P]),
                                                                 op0=ALU.mult, op1=ALU.add).then_inc(vector_done.sem, vector_done.up())
                        for f in (state, dm, dmin, ek):
                            both(f)
                        both(lambda s, t, B: qg(s, t, B, 0))
                        both(lambda s, t, B: qg(s, t, B, 1))
                        for f in (qkm, ltb, lt, vb, kdec, kb0, kb, ti0, tit0):
                            both(f)
                        for b in range(LV):
                            def ti(s, t, B):
                                dve.wait_ge(tensor_done["tx"].sem, tensor_done["tx"].at(en(r, s, LV, b)))
                                if b < LV - 1:
                                    ins = nc.vector.tensor_tensor(B["Ti"], B["Ti"], v3(4 * s + 1), ALU.subtract)
                                else:
                                    ins = nc.vector.memset(B["Ti"][:, 0, 0:1], 0.0)
                                ins.then_inc(vector_done.sem, vector_done.up())

                            def tit(s, t, B):
                                nc.vector.tensor_tensor(B["TiT"], B["TiT"], v3(4 * s + 2), ALU.subtract).then_inc(vector_done.sem, vector_done.up())
                            both(ti)
                            both(tit)

                        def vn(s, t, B):
                            dve.wait_ge(tensor_done["vn"].sem, tensor_done["vn"].at(en(r, s)))
                            nc.vector.tensor_copy(B["VN"].rearrange("p (j i) e -> p i j e", i=2),
                                                        psum[:, 2 * s, :].rearrange("p (i r) -> p i r", i=2)[:, :, 0:J * DK]
                                                        .rearrange("p i (j e) -> p i j e", j=J)).then_inc(vector_done.sem, vector_done.up())

                        def oacc(s, t, B):
                            dve.wait_ge(tensor_done["out"].sem, tensor_done["out"].at(en(r, s)))
                            o = u[:, 10:10 + J, t * P:(t + 1) * P]
                            src = bank(4 * s + 3)[:, 0:J * P].rearrange("p (j c) -> p j c", j=J)
                            if first_visit[r][s]:
                                ins = nc.vector.tensor_copy(o, src)
                            else:
                                dve.wait_ge(vector_done.sem, vector_done.n)
                                ins = nc.vector.tensor_tensor(o, o, src, ALU.add)
                            ins.then_inc(vector_done.sem, vector_done.up())

                        def upd(s, t, B, hd):
                            r0, j = (hd % 2) * DK, hd // 2
                            dve.wait_ge(tensor_done["upd"].sem, tensor_done["upd"].at(en(r, s)))
                            dve.wait_ge(scalar_done.sem, scalar_done.at(an(r, "el", s)))
                            Sv = B["S"][r0:r0 + DK, j, :]
                            nc.vector.scalar_tensor_tensor(out=Sv, in0=Sv, scalar=B["EL"][r0:r0 + DK, hd:hd + 1],
                                                                 in1=bank(4 * s + 2)[r0:r0 + DK, j * DK:(j + 1) * DK],
                                                                 op0=ALU.mult, op1=ALU.add).then_inc(vector_done.sem, vector_done.up())
                        both(vn)
                        both(oacc)
                        for hd in range(H):
                            both(lambda s, t, B: upd(s, t, B, hd))
            return

        vector_inner = sem("vector_inner")

        def close(l, name, c, ln_g, ln_b):
            vector_done, scalar_done, tensor_done = (sem(f"{name}_{n}", l) for n in ("vector", "scalar", "products"))
            sq = [u[:, k, 0:T] for k in range(KD)]
            rs = tmp[:, 0, :]
            with nc.Block() as block:
                @block.tensor
                def _(pe):
                    for k in range(KD):
                        for c0, c1 in SHORT:
                            ins = nc.tensor.matmul(psum[:, 0, c0:c1], mean_d[:], x[:, k, c0:c1],
                                                   start=(k == 0), stop=(k == KD - 1))
                    ins.then_inc(tensor_done.sem, tensor_done.up())
                    for k in range(KD):
                        pe.wait_ge(scalar_done.sem, scalar_done.at(k + 1))
                        for c0, c1 in SHORT:
                            ins = nc.tensor.matmul(psum[:, 1, c0:c1], mean_d[:], sq[k][:, c0:c1],
                                                   start=(k == 0), stop=(k == KD - 1))
                    ins.then_inc(tensor_done.sem, tensor_done.up())

                @block.vector
                def _(dve):
                    dve.wait_ge(tensor_done.sem, tensor_done.at(1))
                    for k in range(KD):
                        nc.vector.tensor_tensor(x[:, k, :], x[:, k, :], psum[:, 0, 0:T], ALU.subtract).then_inc(vector_done.sem, vector_done.up())
                    dve.wait_ge(scalar_done.sem, scalar_done.at(KD + 2))
                    dve.wait_ge(vector_done.sem, vector_done.n)
                    for k in range(KD):
                        nc.vector.tensor_tensor(x[:, k, :], x[:, k, :], rs, ALU.mult).then_inc(vector_done.sem, vector_done.up())

                @block.scalar
                def _(act):
                    for k in range(KD):
                        act.wait_ge(vector_done.sem, vector_done.at(k + 1))
                        nc.scalar.activation(sq[k], x[:, k, :], ACT.Square).then_inc(scalar_done.sem, scalar_done.up())
                    act.wait_ge(tensor_done.sem, tensor_done.at(2))
                    nc.scalar.activation(rs, psum[:, 1, 0:T], ACT.Ln, bias=eps_col[:, 0:1]).then_inc(scalar_done.sem, scalar_done.up())
                    act.wait_ge(scalar_done.sem, scalar_done.n)
                    nc.scalar.activation(rs, rs, ACT.Exp, scale=-0.5).then_inc(scalar_done.sem, scalar_done.up())
                    for k in range(KD):
                        act.wait_ge(vector_done.sem, vector_done.at(KD + k + 1))
                        nc.scalar.activation(x[:, k, :], x[:, k, :], ACT.Identity,
                                                  scale=pa[:, l, ln_g + k:ln_g + k + 1],
                                                  bias=pa[:, l, ln_b + k:ln_b + k + 1]).then_inc(scalar_done.sem, scalar_done.up())

        def project_out(l):
            base, count = parts["out", l]
            vector_done, scalar_done = sem("out_added", l), sem("out_scaled", l)
            with nc.Block() as block:
                @block.sync
                def _(sp):
                    load_ahead(sp, ("out", l))

                @block.scalar
                def _(act):
                    for k in range(KD):
                        nc.scalar.mul(x[:, k, :], x[:, k, :], ALPHA).then_inc(scalar_done.sem, scalar_done.up())

                @block.tensor
                def _(pe):
                    for m in range(KD):
                        block_landed(pe, base + m)
                        if m >= 4:
                            pe.wait_ge(vector_done.sem, vector_done.at(2 * (m - 3)))
                        w = ring_view((base + m) % RING, KD)
                        for k in range(KD):
                            for c0, c1 in SHORT:
                                ins = nc.tensor.matmul(psum[:, m % 4, c0:c1], w[:, k, :], h[:, k, c0:c1],
                                                       start=(k == 0), stop=(k == KD - 1))
                        ins.then_inc(ring_used.sem, ring_used.up())

                @block.vector
                def _(dve):
                    for m in range(KD):
                        dve.wait_ge(ring_used.sem, ring_used.at(base + m + 1))
                        dve.wait_ge(scalar_done.sem, scalar_done.at(m + 1))
                        for s, (t0, t1) in enumerate(SEQS):
                            nc.vector.scalar_tensor_tensor(out=x[:, m, t0:t1], in0=psum[:, m % 4, t0:t1],
                                                                scalar=mod[:, 2 * KD + m, s:s + 1], in1=x[:, m, t0:t1],
                                                                op0=ALU.mult, op1=ALU.add).then_inc(vector_done.sem, vector_done.up())

        hidden = [u[:, f, 0:T] for f in range(FT)]
        sums = [u[:, FT + m, 0:T] for m in range(KD)]
        weight_rows = u[:, FT + KD:FT + KD + NE, 0:T]

        def route(l):
            vector_done, scalar_done, tensor_done = (sem(f"route_{n}", l) for n in ("vector", "scalar", "products"))
            area = wide[:, 0, :]
            logits = area[:, 0:TT * NE].rearrange("p (t n) -> p t n", t=TT)
            top = area[:, 40:80].rearrange("p (t n) -> p t n", t=TT)
            index = area[:, 80:120].rearrange("p (t n) -> p t n", t=TT)
            idx = area[:, 120:160].bitcast(U32).rearrange("p (t n) -> p t n", t=TT)
            share = area[:, 160:170].rearrange("p (i t) -> p i t", i=2)
            comb = area[:, 200:240].rearrange("p (t n) -> p t n", t=TT)
            part = area[:, 240:280].rearrange("p (t n) -> p t n", t=TT)
            numbers = area[:, 280:320].rearrange("p (t n) -> p t n", t=TT)
            io = sem("route_numbers", l)
            with nc.Block() as block:
                @block.gpsimd
                def _(pool):
                    for n in range(NE):
                        nc.gpsimd.memset(numbers[:, :, n], float(n)).then_inc(io.sem, io.up())

                @block.tensor
                def _(pe):
                    for t in range(TT):
                        for k in range(KD):
                            ins = nc.tensor.matmul(psum[:, 0, t * NE:(t + 1) * NE], h[:, k, t * P:(t + 1) * P],
                                                   router[:, k, :], start=(k == 0), stop=(k == KD - 1))
                    ins.then_inc(tensor_done.sem, tensor_done.up())
                    pe.wait_ge(vector_done.sem, vector_done.at(1 + TT * 2 + 1 + 2 + 2 + 1 + 3))
                    for n in range(NE):
                        if n >= 4:
                            pe.wait_ge(scalar_done.sem, scalar_done.at(1 + n - 3))
                        for t in range(TT):
                            ins = nc.tensor.matmul(psum[:, n % 4, t * P:(t + 1) * P],
                                                   comb[:, t, n:n + 1].to_broadcast([P, P]), ident[:], start=True, stop=True)
                        ins.then_inc(tensor_done.sem, tensor_done.up())

                @block.vector
                def _(dve):
                    def step(ins):
                        ins.then_inc(vector_done.sem, vector_done.up())
                        dve.wait_ge(vector_done.sem, vector_done.n)
                    dve.wait_ge(tensor_done.sem, tensor_done.at(1))
                    step(nc.vector.tensor_copy(logits, psum[:, 0, 0:TT * NE].rearrange("p (t n) -> p t n", t=TT)))
                    for t in range(TT):
                        step(nc.vector.max(top[:, t, :], logits[:, t, :]))
                        step(nc.vector.max_index(idx[:, t, :], top[:, t, :], logits[:, t, :]))
                    step(nc.vector.tensor_copy(index, idx))
                    step(nc.vector.tensor_tensor(share[:, 1, :], top[:, :, 1], top[:, :, 0], ALU.subtract))
                    dve.wait_ge(scalar_done.sem, scalar_done.at(1))
                    step(nc.vector.tensor_scalar(share[:, 0, :], share[:, 1, :], 1.0, None, ALU.add))
                    step(nc.vector.reciprocal(share[:, 0, :], share[:, 0, :]))
                    step(nc.vector.tensor_tensor(share[:, 1, :], share[:, 1, :], share[:, 0, :], ALU.mult))
                    dve.wait_ge(io.sem, io.at(NE))
                    both = [(comb, 0), (part, 1)]
                    for dst, i in both:
                        step(nc.vector.tensor_tensor(dst, numbers, index[:, :, i:i + 1].to_broadcast([P, TT, NE]),
                                                     ALU.is_equal))
                        dst_share = share[:, i, :].unsqueeze(2).to_broadcast([P, TT, NE])
                        nc.vector.tensor_tensor(dst, dst, dst_share, ALU.mult).then_inc(vector_inner.sem, 1)
                        vector_inner.n += 1
                        dve.wait_ge(vector_inner.sem, vector_inner.n)
                    step(nc.vector.tensor_tensor(comb, comb, part, ALU.add))
                    step(nc.vector.memset(part[:, 0, 0:1], 0.0))

                @block.scalar
                def _(act):
                    act.wait_ge(vector_done.sem, vector_done.at(1 + 2 * TT + 2))
                    nc.scalar.activation(share[:, 1, :], share[:, 1, :], ACT.Exp).then_inc(scalar_done.sem, scalar_done.up())
                    for n in range(NE):
                        act.wait_ge(tensor_done.sem, tensor_done.at(2 + n))
                        nc.scalar.activation(weight_rows[:, n, :], psum[:, n % 4, 0:T], ACT.Copy).then_inc(scalar_done.sem, scalar_done.up())

        def feed_forward(l):
            base, count = parts["ffn", l]
            experts = count // PER_EXPERT
            moe = l % 2 == 1
            slot_free = sem("ffn_slot_free", l)
            gates, hid, added, scaled = (sem(f"ffn_{n}_{l}") for n in ("gates", "hidden", "added", "scaled"))
            with nc.Block() as block:
                @block.sync
                def _(sp):
                    def turn(e, last):
                        for i in range(RING, PER_EXPERT + RING):
                            n = base + i
                            if i >= PER_EXPERT and last:
                                if base + count + i - PER_EXPERT < len(flat):
                                    load_block(sp, base + count + i - PER_EXPERT)
                                continue
                            src, k = expert_block(l, e + (1 if i >= PER_EXPERT else 0), i % PER_EXPERT)
                            sp.wait_ge(ring_used.sem, e * PER_EXPERT + (n - RING + 1))
                            sp.sem_inc(slot_free.sem, 1)
                            sp.dma_start(ring_view(n % RING, k), src).then_inc(ring_loaded[n % RING].sem, 16)
                    with sp.Fori(0, experts - 1) as e:
                        turn(e, False)
                    turn(experts - 1, True)

                @block.tensor
                def _(pe):
                    with pe.Fori(0, experts) as e:
                        for i in range(2 * FT):
                            n = base + i
                            pe.wait_ge(ring_loaded[n % RING].sem, (e * (PER_EXPERT // RING) + (n // RING + 1)) * 16)
                            if i >= 4:
                                pe.wait_ge(hid.sem, e * FT + ((i - 4) // 2 + 1))
                            w = ring_view(n % RING, KD)
                            for k in range(KD):
                                for c0, c1 in SHORT:
                                    ins = nc.tensor.matmul(psum[:, i % 4, c0:c1], w[:, k, :], h[:, k, c0:c1],
                                                           start=(k == 0), stop=(k == KD - 1))
                            ins.then_inc(ring_used.sem, 1)
                        for m in range(KD):
                            n = base + 2 * FT + m
                            pe.wait_ge(ring_loaded[n % RING].sem, (e * (PER_EXPERT // RING) + (n // RING + 1)) * 16)
                            if m == 0:
                                pe.wait_ge(hid.sem, e * FT + FT)
                            if m >= 4:
                                pe.wait_ge(scaled.sem, e * KD + m - 3)
                            w = ring_view(n % RING, FT)
                            for k in range(FT):
                                for c0, c1 in SHORT:
                                    ins = nc.tensor.matmul(psum[:, m % 4, c0:c1], w[:, k, :], hidden[k][:, c0:c1],
                                                           start=(k == 0), stop=(k == FT - 1))
                            ins.then_inc(ring_used.sem, 1)
                        pe.wait_ge(scaled.sem, e * KD + KD)

                @block.scalar
                def _(act):
                    with act.Fori(0, experts) as e:
                        for f in range(FT):
                            act.wait_ge(ring_used.sem, e * PER_EXPERT + (base + 2 * f + 1))
                            if f >= 2:
                                act.wait_ge(hid.sem, e * FT + (f - 1))
                            nc.scalar.activation(tmp[:, f % 2, :], psum[:, (2 * f) % 4, 0:T], ACT.Silu).then_inc(gates.sem, 1)

                @block.vector
                def _(dve):
                    nc.vector.memset(u[:, FT:FT + KD, :], 0.0).then_inc(vector_inner.sem, 1)
                    vector_inner.n += 1
                    dve.wait_ge(vector_inner.sem, vector_inner.n)
                    with dve.Fori(0, experts) as e:
                        for f in range(FT):
                            dve.wait_ge(gates.sem, e * FT + f + 1)
                            dve.wait_ge(ring_used.sem, e * PER_EXPERT + (base + 2 * f + 2))
                            nc.vector.tensor_tensor(hidden[f], tmp[:, f % 2, :], psum[:, (2 * f + 1) % 4, 0:T],
                                                    ALU.mult).then_inc(hid.sem, 1)
                        for m in range(KD):
                            dve.wait_ge(ring_used.sem, e * PER_EXPERT + (base + 2 * FT + m + 1))
                            if moe:
                                if m >= 2:
                                    dve.wait_ge(added.sem, e * KD + (m - 1))
                                nc.vector.tensor_tensor(tmp[:, 2 + m % 2, :], psum[:, m % 4, 0:T],
                                                        weight_rows[:, bass.ds(e, 1), :].rearrange("p a t -> p (a t)"),
                                                        ALU.mult).then_inc(scaled.sem, 1)
                            else:
                                nc.vector.tensor_tensor(sums[m], sums[m], psum[:, m % 4, 0:T], ALU.add)\
                                    .then_inc(scaled.sem, 1)
                        if moe:
                            dve.wait_ge(added.sem, e * KD + KD)
                        else:
                            dve.wait_ge(scaled.sem, e * KD + KD)

                if moe:
                    @block.gpsimd
                    def _(pool):
                        pool.wait_ge(vector_inner.sem, vector_inner.n)
                        with pool.Fori(0, experts) as e:
                            for m in range(KD):
                                pool.wait_ge(scaled.sem, e * KD + m + 1)
                                nc.gpsimd.tensor_tensor(sums[m], sums[m], tmp[:, 2 + m % 2, :], ALU.add)\
                                    .then_inc(added.sem, 1)
                            pool.wait_ge(added.sem, e * KD + KD)

        def residual(l):
            vector_done, scalar_done = sem("res_vector", l), sem("res_scalar", l)
            with nc.Block() as block:
                @block.scalar
                def _(act):
                    for k in range(KD):
                        nc.scalar.mul(x[:, k, :], x[:, k, :], ALPHA).then_inc(scalar_done.sem, scalar_done.up())

                @block.vector
                def _(dve):
                    for m in range(KD):
                        dve.wait_ge(scalar_done.sem, scalar_done.at(m + 1))
                        for s, (t0, t1) in enumerate(SEQS):
                            nc.vector.scalar_tensor_tensor(out=x[:, m, t0:t1], in0=sums[m][:, t0:t1],
                                                                scalar=mod[:, 5 * KD + m, s:s + 1], in1=x[:, m, t0:t1],
                                                                op0=ALU.mult, op1=ALU.add).then_inc(vector_done.sem, vector_done.up())

        def finish():
            turned, copied, stored = sem("end_turned"), sem("end_copied"), sem("end_stored")
            rows = [u[:, 2 * t:2 * t + 2, :].rearrange("p s w -> p (s w)")[:, 0:D] for t in range(TT)]
            with nc.Block() as block:
                @block.tensor
                def _(pe):
                    for t in range(TT):
                        if t >= 4:
                            pe.wait_ge(copied.sem, copied.at(t - 3))
                        for k in range(KD):
                            ins = nc.tensor.transpose(psum[:, t % 4, k * P:(k + 1) * P], x[:, k, t * P:(t + 1) * P], ident[:])
                        ins.then_inc(turned.sem, turned.up())

                @block.vector
                def _(dve):
                    for t in range(TT):
                        dve.wait_ge(turned.sem, turned.at(t + 1))
                        nc.vector.tensor_copy(rows[t], psum[:, t % 4, :]).then_inc(copied.sem, copied.up())

                @block.sync
                def _(sp):
                    for t in range(TT):
                        sp.wait_ge(copied.sem, copied.at(t + 1))
                        dst = out["yp"][0] if t == 0 else out["ys"][0, (t - 1) * P:t * P, :]
                        sp.dma_start(dst, rows[t]).then_inc(stored.sem, stored.up(16))
                    sp.wait_ge(stored.sem, stored.at(16 * TT))

        start()
        for l in range(DEPTH):
            modulation(l)
            modulate(0)
            project_in(l)
            conformer(l)
            short_conv(l)
            gla(l)
            gdn(l)
            project_out(l)
            close(l, "ln1", 0, at_a["ln1_g"], at_a["ln1_b"])
            modulate(3)
            if l % 2 == 1:
                route(l)
            feed_forward(l)
            ring_used.n = sum(parts["ffn", l])
            residual(l)
            close(l, "ln2", 0, at_a["ln2_g"], at_a["ln2_b"])
        finish()


_INS = ["x_prompt", "x_sample", "c", "state_gla", "state_gdn", "c_ctx", "w_ada", "b_ada", "w_in", "w_out", "conv_w",
        "conv_b", "conv_ln_g", "conv_ln_b", "conv_pw", "gla_w_lr", "gla_b_lr", "gla_norm_g", "gdn_conv_w",
        "gdn_a_log", "gdn_dt_bias", "gdn_norm_g", "sc_conv_w", "ln1_g", "ln1_b", "ln2_g", "ln2_b", "ffn_w_gate",
        "ffn_w_up", "ffn_w_down", "moe_router", "moe_w_gate", "moe_w_up", "moe_w_down"]


def kernel(**inputs):
    import numpy as _np
    import concourse.bacc as _bacc
    from concourse import mybir as _mybir
    from concourse.bass_utils import run_bass_kernel_spmd as _run

    nc = _bacc.Bacc("TRN2", target_bir_lowering=False, num_devices=1)
    arrays, args = {}, {}
    for name in _INS:
        v = _np.ascontiguousarray(inputs[name])
        arrays[f"in_{name}_dram"] = v
        args[name] = nc.dram_tensor(f"in_{name}_dram", v.shape, _mybir.dt.from_np(v.dtype), kind="ExternalInput").ap()
    sp, ss = inputs["x_prompt"].shape, inputs["x_sample"].shape
    outs = {"yp": sp, "ys": ss, "gla": inputs["state_gla"].shape, "gdn": inputs["state_gdn"].shape}
    handles = {n: nc.dram_tensor(f"out_{n}_dram", tuple(s), F32, kind="ExternalOutput").ap() for n, s in outs.items()}
    trunk_kernel(nc, args, handles)
    r = _run(nc, [arrays], core_ids=[0])
    return tuple(r.results[0][f"out_{n}_dram"] for n in ("yp", "ys", "gla", "gdn"))
```

```python
from contextlib import ExitStack

import concourse.bass as bass
from concourse import mybir

F32 = mybir.dt.float32
I32 = mybir.dt.int32
U32 = mybir.dt.uint32
ALU = mybir.AluOpType
ACT = mybir.ActivationFunctionType
AX = mybir.AxisListType

P = 128


class Signal:

    def __init__(self, sem):
        self.sem = sem
        self.n = 0
        self.base = 0

    def up(self, k=1):
        self.n += k
        return k

    def at(self, value):
        return self.base + value


def trunk_kernel(nc, a, out):
    DEPTH, D, N_IN = a["w_in"].shape
    CTX = a["x_prompt"].shape[1]
    LAT = a["x_sample"].shape[1]
    T = CTX + LAT
    TT = T // P
    KD = D // P
    GRID_W = 64
    ROWS = LAT // GRID_W
    CONV_K, GW = a["conv_w"].shape[1:]
    J = GW // P
    H = a["state_gla"].shape[3]
    DK = a["state_gla"].shape[4]
    LR = a["gla_w_lr"].shape[2]
    GLA_TAU = 16.0
    CHUNK = 64
    NCH = T // CHUNK
    NE = a["moe_w_gate"].shape[1]
    FE = a["moe_w_gate"].shape[3]
    FT = FE // P
    DENSE = a["ffn_w_gate"].shape[2] // FE
    ALPHA = (2 * DEPTH) ** 0.25
    EPS = 1e-5
    QSCALE = DK ** -0.5
    SEQS = ((0, CTX), (CTX, T))
    SHORT = ((0, 512), (512, T))
    assert D == 1024 and J == 2 and H == 4 and DK == 64 and CTX == P and T == 640 and FE == 11 * P

    UW = T + 4
    names = ["aval", "agate", "gq", "gk", "gv", "gg", "lr", "dq", "dk", "dv", "dgate", "bd", "sb", "sc", "sx"]
    widths = {n: GW for n in names} | {"lr": 2 * LR, "bd": 3 * H}
    in_tiles, slot, col = [], {}, 0
    for n in names:
        slot[n] = len(in_tiles)
        for c in range(0, widths[n], P):
            in_tiles.append((n, len(in_tiles), col + c, min(P, widths[n] - c)))
        col += widths[n]
    assert col == N_IN
    PADDED = ("dq", "dk", "dv", "sx")
    PERMUTED = ("dq", "dk", "dv", "bd")
    U = len(in_tiles)
    FIRST = ("aval", "agate", "lr", "gq", "gk", "sb", "sc", "sx", "dq", "dk", "dv", "gv", "gg", "dgate", "bd")
    in_tiles.sort(key=lambda tile: FIRST.index(tile[0]))

    rows_a = [("b_ada", 6 * KD), ("ln1_g", KD), ("ln1_b", KD), ("ln2_g", KD), ("ln2_b", KD), ("conv_b", J),
              ("conv_ln_g", J), ("conv_ln_b", J), ("gla_norm_g", J), ("gdn_norm_g", J), ("gla_b_lr", 2 * J),
              ("sc_conv_w", 3 * J), ("gdn_conv_w", 9 * J)]
    rows_b = [("conv_w", CONV_K * J), ("c", KD), ("c_ctx", KD)]

    def offsets(rows):
        at, o = {}, 0
        for n, k in rows:
            at[n] = o
            o += k
        assert o <= P
        return at, o
    at_a, n_a = offsets(rows_a)
    at_b, n_b = offsets(rows_b)

    RING = 6
    RW = FT * P
    PER_EXPERT = 2 * FT + KD
    assert PER_EXPERT % RING == 0

    ctx = ExitStack()
    with ctx:
        def sb(name, shape, dt=F32):
            return ctx.enter_context(nc.sbuf_tensor(name, shape, dt))

        signals = {}

        def sem(name, l=None):
            if l is None or name not in signals:
                signals[name] = Signal(ctx.enter_context(nc.semaphore(name)))
            signals[name].base = signals[name].n
            return signals[name]

        x = sb("x", [P, KD, T])
        h = sb("h", [P, KD, T])
        ring = sb("ring", [P, RING, RW])
        u = sb("u", [P, U, UW])
        work = sb("work", [P, 4 * T + 4 * 688])
        tmp = work[:, 0:4 * T].rearrange("p (a t) -> p a t", a=4)
        wide = work[:, 4 * T:4 * T + 4 * 688].rearrange("p (a t) -> p a t", a=4)
        mix = sb("mix", [P, KD, T])
        h_rows = mix[:].rearrange("p k t -> p (k t)").rearrange("p (t f) -> p t f", t=TT)
        chunk_decay = sb("chunk_decay", [P, 2 * J * (T // CHUNK)])
        mod = sb("mod", [P, 6 * KD, 2])
        cond = sb("cond", [P, KD, 2])
        pa = sb("pa", [P, DEPTH, P])
        pb = sb("pb", [P, DEPTH, P])
        ident = sb("ident", [P, P])
        mean_d = sb("mean_d", [P, P])
        mean_g = sb("mean_g", [P, P])
        head_sum = sb("head_sum", [P, P])
        until = sb("until", [P, 2, P])
        chunk_until = sb("chunk_until", [P, 2, P])
        level = sb("level", [P, 7, 2, P], mybir.dt.bfloat16)
        level0t = sb("level0t", [P, 2, P])
        w_lr = sb("w_lr", [2 * LR, 2 * GW])
        pw = sb("pw", [P, J, GW])
        router = sb("router", [P, KD, NE])
        dtb = sb("dtb", [P, 2 * H])
        nega = sb("nega", [P, 2 * H])
        eps_col = sb("eps_col", [P, 2])
        resets = sb("resets", [P, 2, T])
        psum = ctx.enter_context(nc.psum_tensor("psum", [P, 4, 1024], F32))

        def bank(n):
            return psum[:, n // 2, (n % 2) * 512:(n % 2) * 512 + 512]

        ctx.enter_context(nc.allow_non_contiguous_dma(reason="small loads"))

        ring_loaded = [sem(f"ring_loaded{s}") for s in range(RING)]
        ring_used = sem("ring_used")

        def column_block(w, c, n=P):
            return w[:, c:c + n].rearrange("(k p) n -> p k n", p=P)

        def ring_view(s, k, n=P):
            return ring[:, s, 0:k * n].rearrange("p (k n) -> p k n", n=n)

        stream = []
        parts = {}
        for l in range(DEPTH):
            blocks = [(a["w_ada"][l], m * P, P, KD) for m in range(6 * KD)]
            parts["ada", l] = (sum(map(len, stream)), len(blocks))
            stream.append(blocks)
            blocks = [(a["w_in"][l], c, n, KD) for _, _, c, n in in_tiles]
            parts["in", l] = (sum(map(len, stream)), len(blocks))
            stream.append(blocks)
            blocks = [(a["w_out"][l], m * P, P, KD) for m in range(KD)]
            parts["out", l] = (sum(map(len, stream)), len(blocks))
            stream.append(blocks)
            count = (DENSE if l % 2 == 0 else NE) * PER_EXPERT
            parts["ffn", l] = (sum(map(len, stream)), count)
            stream.append([None] * count)
        flat = [b for part in stream for b in part]

        def expert_block(l, e, i):
            if l % 2 == 0:
                wg, wu, wd = a["ffn_w_gate"][l // 2], a["ffn_w_up"][l // 2], a["ffn_w_down"][l // 2]
                if i < 2 * FT:
                    w = (wg, wu)[i % 2]
                    cols = w[:, bass.ds(e * FE + (i // 2) * P, P)]
                    return cols.rearrange("(k p) n -> p k n", p=P), KD
                rows = wd[bass.ds(e * FE, FE), (i - 2 * FT) * P:(i - 2 * FT + 1) * P]
                return rows.rearrange("(k p) n -> p k n", p=P), FT
            wg, wu, wd = a["moe_w_gate"][l // 2], a["moe_w_up"][l // 2], a["moe_w_down"][l // 2]
            if i < 2 * FT:
                w = (wg, wu)[i % 2]
                c = (i // 2) * P
                return w[bass.ds(e, 1), :, c:c + P].rearrange("a (k p) n -> p (a k) n", p=P), KD
            c = (i - 2 * FT) * P
            return wd[bass.ds(e, 1), :, c:c + P].rearrange("a (k p) n -> p (a k) n", p=P), FT

        def load_block(eng, n):
            if n >= RING:
                eng.wait_ge(ring_used.sem, ring_used.at(n - RING + 1))
            s = n % RING
            if flat[n] is None:
                l = next(l for l in range(DEPTH) if parts["ffn", l][0] <= n < sum(parts["ffn", l]))
                i = n - parts["ffn", l][0]
                src, k = expert_block(l, i // PER_EXPERT, i % PER_EXPERT)
                dst = ring_view(s, k)
            else:
                w, c, m, k = flat[n]
                src, dst = column_block(w, c, m), ring_view(s, k, m)
            eng.dma_start(dst, src).then_inc(ring_loaded[s].sem, 16)

        def load_ahead(eng, part, turn=0, queues=1):
            base, count = parts[part]
            for n in range(base + RING, base + count + RING):
                if n < len(flat) and n % queues == turn:
                    load_block(eng, n)

        def block_landed(eng, n):
            eng.wait_ge(ring_loaded[n % RING].sem, ring_loaded[n % RING].at(16 * (n // RING + 1)))

        def start():
            small = sem("small_loaded")
            stage_in = sem("stage_loaded")
            x_in = sem("x_loaded")
            consts = sem("consts_built")
            turned = sem("start_turned")
            copied = sem("start_copied")
            act_copied = sem("start_act_copied")
            stage = wide[:, :, 0:P]
            x_rows = [u[:, 2 * t:2 * t + 2, :].rearrange("p s w -> p (s w)")[:, 0:D] for t in range(TT)]
            with nc.Block() as block:
                n_stage = 0

                @block.sync
                def _(sp):
                    for t in range(TT):
                        src = a["x_prompt"][0] if t == 0 else a["x_sample"][0, (t - 1) * P:t * P, :]
                        sp.dma_start(x_rows[t], src).then_inc(x_in.sem, x_in.up(16))
                    for n in range(RING):
                        load_block(sp, n)

                @block.gpsimd
                def _(pool):
                    def built(ins):
                        ins.then_inc(consts.sem, consts.up())
                        pool.wait_ge(consts.sem, consts.n)

                    def keep(v, pattern, base, mult):
                        built(nc.gpsimd.affine_select(out=v, in_=v, compare_op=ALU.is_ge, fill=0.0, base=base,
                                                      pattern=pattern, channel_multiplier=mult))
                    for v, value in ((ident, 0.0), (mean_d, 1.0 / D), (mean_g, 1.0 / GW), (head_sum, 1.0),
                                     (until, 1.0), (level, 1.0), (level0t, 1.0), (resets, 1.0)):
                        built(nc.gpsimd.memset(v[:], value))
                    built(nc.gpsimd.memset(w_lr[:], 0.0))
                    for t in range(0, T, CHUNK):
                        built(nc.gpsimd.memset(resets[:, 0, t:t + 1], 0.0))
                        built(nc.gpsimd.memset(resets[:, 1, t + CHUNK - 1:t + CHUNK], 0.0))
                    built(nc.gpsimd.memset(eps_col[:, 0:1], EPS))
                    built(nc.gpsimd.memset(eps_col[:, 1:2], 1e-6))
                    built(nc.gpsimd.affine_select(out=ident[:], in_=ident[:], compare_op=ALU.not_equal, fill=1.0,
                                                  base=0, pattern=[[-1, P]], channel_multiplier=1))

                    def same_block(v, size, dims):
                        n = P // size
                        v = v.rearrange("p (g c) -> p g c", c=size)
                        keep(v, [[-size, n], [0, size]], 0, 1)
                        keep(v, [[size, n], [0, size]], size - 1, -1)
                    same_block(head_sum[:], DK, 0)
                    for z, sign in ((0, 1), (1, -1)):
                        keep(until[:, z, :], [[sign, P]], 0, -sign)
                        built(nc.gpsimd.tensor_copy(chunk_until[:, z, :], until[:, z, :]))
                        same_block(chunk_until[:, z, :], CHUNK, 0)
                        for b in range(7):
                            v = level[:, b, z, :]
                            size = 2 << b
                            if size < P:
                                same_block(v, size, 0)
                            w = v.rearrange("p (g i c) -> p g i c", i=2, c=size // 2)
                            own, other = w[:, :, z, :], w[:, :, 1 - z, :]
                            built(nc.gpsimd.memset(own, 0.0))
                            n = P // size
                            if z == 0:
                                keep(other, [[size, n], [0, size // 2]], size // 2 - 1, -1)
                            else:
                                keep(other, [[-size, n], [0, size // 2]], -(size // 2), 1)
                        built(nc.gpsimd.tensor_copy(level0t[:, 1 - z, :], level[:, 0, z, :]))

                @block.scalar
                def _(act):
                    k = 0
                    for l in range(DEPTH):
                        for rows, at, half in ((rows_a, at_a, 0), (rows_b, at_b, 1)):
                            for n, count in rows:
                                if n == "c":
                                    src = a["c"].rearrange("b (k p) -> (b k) p", p=P)
                                elif n == "c_ctx":
                                    src = a["c_ctx"].rearrange("(k p) -> k p", p=P)
                                else:
                                    w = a[n][l]
                                    if len(w.shape) == 2:
                                        w = w.rearrange("a b -> (a b)")
                                    src = w.rearrange("(k p) -> k p", p=P)
                                act.dma_start(stage[at[n]:at[n] + count, 2 * l + half, :], src).then_inc(stage_in.sem, stage_in.up(16))
                                k += 1
                    assert k == DEPTH * (len(rows_a) + len(rows_b))

                @block.tensor
                def _(pe):
                    pe.wait_ge(consts.sem, consts.at(consts.n))
                    pe.wait_ge(stage_in.sem, stage_in.at(stage_in.n))
                    for l in range(DEPTH):
                        nc.tensor.transpose(psum[:, 0, (2 * l) * P:(2 * l) * P + n_a], stage[0:n_a, 2 * l, :],
                                            ident[0:n_a, 0:n_a])
                        nc.tensor.transpose(psum[:, 0, (2 * l + 1) * P:(2 * l + 1) * P + n_b],
                                                      stage[0:n_b, 2 * l + 1, :], ident[0:n_b, 0:n_b]).then_inc(turned.sem, turned.up())
                    for t in range(TT):
                        pe.wait_ge(x_in.sem, x_in.at(16 * TT))
                        if t >= 3:
                            pe.wait_ge(copied.sem, copied.at(DEPTH * 2 + t - 2))
                        for k in range(KD):
                            ins = nc.tensor.transpose(psum[:, 1 + t % 3, k * P:(k + 1) * P],
                                                      x_rows[t][:, k * P:(k + 1) * P], ident[:])
                        ins.then_inc(turned.sem, turned.up())

                @block.vector
                def _(dve):
                    dve.wait_ge(turned.sem, turned.at(DEPTH))
                    for l in range(DEPTH):
                        nc.vector.tensor_copy(pa[:, l, 0:n_a], psum[:, 0, 2 * l * P:2 * l * P + n_a]).then_inc(copied.sem, copied.up())
                        nc.vector.tensor_copy(pb[:, l, 0:n_b],
                                                        psum[:, 0, (2 * l + 1) * P:(2 * l + 1) * P + n_b]).then_inc(copied.sem, copied.up())
                    for t in range(TT):
                        dve.wait_ge(turned.sem, turned.at(DEPTH + t + 1))
                        nc.vector.tensor_copy(
                            x[:, :, t * P:(t + 1) * P], psum[:, 1 + t % 3, :].rearrange("p (k n) -> p k n", n=P)).then_inc(copied.sem, copied.up())
            with nc.Block() as block:
                @block.scalar
                def _(act):
                    for s, n in ((0, "c_ctx"), (1, "c")):
                        nc.scalar.activation(cond[:, :, s], pb[:, 0, at_b[n]:at_b[n] + KD], ACT.Silu)

        def modulation(l):
            landed = sem("small_weights_landed", l)
            products = sem("ada_products", l)
            added = sem("ada_added", l)
            base, count = parts["ada", l]
            with nc.Block() as block:
                @block.sync
                def _(sp):
                    load_ahead(sp, ("ada", l), 0, 2)

                @block.scalar
                def _(act):
                    load_ahead(act, ("ada", l), 1, 2)

                @block.gpsimd
                def _(pool):
                    for z in range(2):
                        pool.dma_start(w_lr[z * LR:(z + 1) * LR, z * GW:(z + 1) * GW], a["gla_w_lr"][l, z]).then_inc(landed.sem, landed.up(16))
                    pool.dma_start(pw[:], a["conv_pw"][l].rearrange("(k p) n -> p k n", p=P)).then_inc(landed.sem, landed.up(16))
                    pool.dma_start(dtb[:], a["gdn_dt_bias"][l].rearrange("a h -> (a h)").partition_broadcast(P)).then_inc(landed.sem, landed.up(16))
                    pool.dma_start(nega[:], a["gdn_a_log"][l].rearrange("a h -> (a h)").partition_broadcast(P)).then_inc(landed.sem, landed.up(16))
                    n = 5
                    if l % 2 == 1:
                        pool.dma_start(router[:], a["moe_router"][l // 2].rearrange("(k p) n -> p k n", p=P)).then_inc(landed.sem, landed.up(16))
                        n += 1
                    pool.wait_ge(landed.sem, landed.at(16 * n))

                @block.tensor
                def _(pe):
                    for m in range(count):
                        block_landed(pe, base + m)
                        w = ring_view((base + m) % RING, KD)
                        for k in range(KD):
                            ins = nc.tensor.matmul(psum[:, 0, 2 * m:2 * m + 2], w[:, k, :], cond[:, k, :],
                                                   start=(k == 0), stop=(k == KD - 1))
                        ins.then_inc(ring_used.sem, ring_used.up())

                @block.vector
                def _(dve):
                    dve.wait_ge(ring_used.sem, ring_used.at(base + count))
                    nc.vector.tensor_tensor(
                        mod[:], psum[:, 0, 0:2 * count].rearrange("p (m s) -> p m s", s=2),
                        pa[:, l, 0:count].unsqueeze(2).to_broadcast([P, count, 2]), ALU.add).then_inc(added.sem, added.up())
                    dve.wait_ge(added.sem, added.n)
                    for c in (1, 4):
                        v = mod[:, c * KD:(c + 1) * KD, :]
                        nc.vector.tensor_scalar(v, v, 1.0, None, ALU.add).then_inc(added.sem, added.up())

        def modulate(c):
            with nc.Block() as block:
                @block.vector
                def _(dve):
                    for k in range(0, KD, 2):
                        for s, (t0, t1) in enumerate(SEQS):
                            nc.vector.tensor_scalar(h[:, k, t0:t1], x[:, k, t0:t1], mod[:, (c + 1) * KD + k, s:s + 1],
                                                    mod[:, c * KD + k, s:s + 1], ALU.mult, ALU.add)

                @block.scalar
                def _(act):
                    for k in range(1, KD, 2):
                        for s, (t0, t1) in enumerate(SEQS):
                            nc.scalar.activation(h[:, k, t0:t1], x[:, k, t0:t1], ACT.Identity,
                                                 scale=mod[:, (c + 1) * KD + k, s:s + 1],
                                                 bias=mod[:, c * KD + k, s:s + 1])

        PADC = CONV_K // 2
        CW = T + PADC
        conv_in, conv = wide[:, 0:J, :], wide[:, J:2 * J, :]

        def gla_parts():
            q = [u[:, slot["gq"] + j, 0:T] for j in range(J)]
            k = [u[:, slot["gk"] + j, 0:T] for j in range(J)]
            qe = [[u[:, j, 0:T] for j in range(J)], q]
            ke = [[u[:, J + j, 0:T] for j in range(J)], k]
            kd = [[mix[:, J + z * J + j, :] for j in range(J)] for z in range(2)]
            return qe, ke, kd

        def project_in(l):
            base, count = parts["in", l]
            copied = sem("in_copied", l)
            low_rank = sem("in_low_rank", l)
            pads = sem("in_pads", l)
            gate = sem("in_conformer_gate", l)
            conv_step = sem("in_conformer_conv", l)
            decay_act = sem("in_decay_scalar", l)
            decay_vec = sem("in_decay_vector", l)
            short_step = sem("in_short_conv", l)
            taps = sem("in_gdn_conv", l)
            PAIRS = [(z, j) for z in range(2) for j in range(J)]
            units = []
            for i in range(count):
                units.append(("tile", i))
                if i >= 10 and i % 2 == 0 and (i - 10) // 2 < len(PAIRS):
                    units.append(("low", (i - 10) // 2))

            def unit(kind, i):
                return units.index((kind, i))

            def group_copied(n, j=0):
                i = next(i for i, tile in enumerate(in_tiles) if tile[1] == slot[n] + j)
                return copied.at(unit("tile", i) + 1)

            def copies(i, pair):
                n, s, _, m = in_tiles[i]
                src = psum[0:m, pair, :]
                pad = 1 if n in PADDED else 0
                if n in PERMUTED:
                    lat = u[0:m, s, CTX + 2 * pad:T + 2 * pad].rearrange("p (c r) -> p c r", r=ROWS)
                    return [(u[0:m, s, pad:CTX + pad], src[:, 0:CTX]),
                            (lat, src[:, CTX:T].rearrange("p (r c) -> p c r", c=GRID_W))]
                if pad:
                    return [(u[0:m, s, pad:CTX + pad], src[:, 0:CTX]),
                            (u[0:m, s, CTX + 2 * pad:T + 2 * pad], src[:, CTX:T])]
                return [(u[0:m, s, 0:T], src[:, 0:T])]

            sg = [u[:, slot["agate"] + j, 0:T] for j in range(J)]
            q = [u[:, slot["gq"] + j, 0:T] for j in range(J)]
            k_ = [u[:, slot["gk"] + j, 0:T] for j in range(J)]
            qe, ke, kd = gla_parts()
            dec = chunk_decay[:].rearrange("p (z j n) -> p z j n", z=2, j=J)
            taps_out = [u[:, slot["sb"] + i, 0:T + 1] for i in range(3 * J)]
            ADD, SCA, VEC = J * CONV_K, 7, 6
            with nc.Block() as block:
                @block.sync
                def _(sp):
                    load_ahead(sp, ("in", l))

                @block.tensor
                def _(pe):
                    for n, (kind, i) in enumerate(units):
                        if n >= 4:
                            pe.wait_ge(copied.sem, copied.at(n - 3))
                        if kind == "low":
                            z, j = PAIRS[i]
                            for c0, c1 in SHORT:
                                ins = nc.tensor.matmul(psum[:, n % 4, c0:c1], w_lr[:, z * GW + j * P:z * GW + (j + 1) * P],
                                                       u[0:2 * LR, slot["lr"], c0:c1], start=True, stop=True)
                            ins.then_inc(low_rank.sem, low_rank.up())
                            continue
                        m = in_tiles[i][3]
                        block_landed(pe, base + i)
                        w = ring_view((base + i) % RING, KD, m)
                        for k in range(KD):
                            for c0, c1 in SHORT:
                                ins = nc.tensor.matmul(psum[0:m, n % 4, c0:c1], w[:, k, :], h[:, k, c0:c1],
                                                       start=(k == 0), stop=(k == KD - 1))
                        ins.then_inc(ring_used.sem, ring_used.up())

                @block.gpsimd
                def _(pool):
                    for j in range(J):
                        for c0, c1 in ((0, PADC), (CTX + PADC, CTX + 2 * PADC), (T + 2 * PADC, T + 3 * PADC)):
                            nc.gpsimd.memset(conv_in[:, j, c0:c1], 0.0).then_inc(pads.sem, pads.up())
                    for n in PADDED:
                        for j in range(J):
                            for c in (0, CTX + 1, T + 2):
                                nc.gpsimd.memset(u[:, slot[n] + j, c:c + 1], 0.0).then_inc(pads.sem, pads.up())

                @block.scalar
                def _(act):
                    silu_next = 0
                    for n, (kind, i) in enumerate(units):
                        if kind == "low":
                            z, j = PAIRS[i]
                            o = at_a["gla_b_lr"] + z * J + j
                            act.wait_ge(low_rank.sem, low_rank.at(i + 1))
                            if i:
                                act.wait_ge(decay_vec.sem, decay_vec.at(VEC * i))
                            nc.scalar.activation(tmp[:, 0, :], psum[:, n % 4, 0:T], ACT.Identity, bias=pa[:, l, o:o + 1])\
                                .then_inc(copied.sem, copied.up())
                            act.wait_ge(copied.sem, copied.n)
                            nc.scalar.activation(tmp[:, 1, :], tmp[:, 0, :], ACT.Abs).then_inc(decay_act.sem, decay_act.up())
                            act.wait_ge(decay_act.sem, decay_act.n)
                            nc.scalar.activation(tmp[:, 1, :], tmp[:, 1, :], ACT.Exp, scale=-1.0)\
                                .then_inc(decay_act.sem, decay_act.up())
                            act.wait_ge(decay_act.sem, decay_act.n)
                            nc.scalar.activation(tmp[:, 1, :], tmp[:, 1, :], ACT.Ln, bias=1.0)\
                                .then_inc(decay_act.sem, decay_act.up())
                            act.wait_ge(decay_vec.sem, decay_vec.at(VEC * i + 3))
                            nc.scalar.activation(tmp[:, 0, :], tmp[:, 2, :], ACT.Exp, scale=1.0 / GLA_TAU)\
                                .then_inc(decay_act.sem, decay_act.up())
                            nc.scalar.activation(tmp[:, 3, :], tmp[:, 2, :], ACT.Exp, scale=-1.0 / GLA_TAU)\
                                .then_inc(decay_act.sem, decay_act.up())
                            last = tmp[:, 2, :].rearrange("p (n c) -> p n c", c=CHUNK)
                            last = last[:, :, CHUNK - 1] if z == 0 else last[:, :, 0]
                            nc.scalar.activation(dec[:, z, j, :], last, ACT.Exp, scale=1.0 / GLA_TAU)\
                                .then_inc(decay_act.sem, decay_act.up())
                            act.wait_ge(decay_vec.sem, decay_vec.at(VEC * i + 5))
                            nc.scalar.activation(kd[z][j], tmp[:, 1, :], ACT.Exp, scale=1.0 / GLA_TAU)\
                                .then_inc(decay_act.sem, decay_act.up())
                            continue
                        act.wait_ge(ring_used.sem, ring_used.at(base + i + 1))
                        for d, s in copies(i, n % 4):
                            ins = nc.scalar.activation(d, s, ACT.Copy)
                        ins.then_inc(copied.sem, copied.up())
                        if in_tiles[i][0] == "agate":
                            v = sg[in_tiles[i][1] - slot["agate"]]
                            act.wait_ge(copied.sem, copied.n)
                            nc.scalar.activation(v, v, ACT.Sigmoid).then_inc(gate.sem, gate.up())
                        if i >= 22:
                            act.wait_ge(taps.sem, taps.at(3 * (silu_next + 1)))
                            for s, (a0, a1) in enumerate(SEQS):
                                nc.scalar.activation(u[:, slot["dq"] + silu_next, a0:a1],
                                                     taps_out[silu_next][:, a0 + s:a1 + s], ACT.Silu)
                            silu_next += 1
                    assert silu_next == 3 * J
                    nc.scalar.activation(nega[:], nega[:], ACT.Exp)

                @block.vector
                def _(dve):
                    dve.wait_ge(pads.sem, pads.at(3 * J))
                    for j in range(J):
                        dve.wait_ge(gate.sem, gate.at(j + 1))
                        for s, (t0, t1) in enumerate(SEQS):
                            o = PADC * (s + 1)
                            nc.vector.tensor_tensor(conv_in[:, j, t0 + o:t1 + o], u[:, slot["aval"] + j, t0:t1],
                                                    sg[j][:, t0:t1], ALU.mult).then_inc(conv_step.sem, conv_step.up())
                    dve.wait_ge(conv_step.sem, conv_step.n)
                    for k in range(CONV_K):
                        for j in range(J):
                            w = pb[:, l, at_b["conv_w"] + k * J + j:at_b["conv_w"] + k * J + j + 1]
                            if k == 0:
                                b = pa[:, l, at_a["conv_b"] + j:at_a["conv_b"] + j + 1]
                                ins = nc.vector.tensor_scalar(conv[:, j, 0:CW], conv_in[:, j, 0:CW], w, b,
                                                              ALU.mult, ALU.add)
                            else:
                                dve.wait_ge(conv_step.sem, conv_step.n - 1)
                                ins = nc.vector.scalar_tensor_tensor(out=conv[:, j, 0:CW], in0=conv_in[:, j, k:k + CW],
                                                                     scalar=w, in1=conv[:, j, 0:CW],
                                                                     op0=ALU.mult, op1=ALU.add)
                            ins.then_inc(conv_step.sem, conv_step.up())
                    dve.wait_ge(copied.sem, group_copied("gk", J - 1))
                    for i, (z, j) in enumerate(PAIRS):
                        dve.wait_ge(decay_act.sem, decay_act.at(SCA * i + 1))
                        nc.vector.tensor_scalar(tmp[:, 0, :], tmp[:, 0, :], 0.0, None, ALU.min)\
                            .then_inc(decay_vec.sem, decay_vec.up())
                        dve.wait_ge(decay_vec.sem, decay_vec.n)
                        dve.wait_ge(decay_act.sem, decay_act.at(SCA * i + 3))
                        nc.vector.tensor_tensor(tmp[:, 0, :], tmp[:, 0, :], tmp[:, 1, :], ALU.subtract)\
                            .then_inc(decay_vec.sem, decay_vec.up())
                        dve.wait_ge(decay_vec.sem, decay_vec.n)
                        cum, la, r = tmp[:, 2, :], tmp[:, 0, :], resets[:, z, :]
                        if z == 1:
                            cum, la, r = cum[:, ::-1], la[:, ::-1], r[:, ::-1]
                        nc.vector.tensor_tensor_scan(cum, r, la, 0.0, ALU.mult, ALU.add)\
                            .then_inc(decay_vec.sem, decay_vec.up())
                        dve.wait_ge(decay_act.sem, decay_act.at(SCA * i + 5))
                        nc.vector.scalar_tensor_tensor(out=qe[z][j], in0=q[j], scalar=QSCALE, in1=tmp[:, 0, :],
                                                       op0=ALU.mult, op1=ALU.mult).then_inc(decay_vec.sem, decay_vec.up())
                        cums = tmp[:, 2, :].rearrange("p (n c) -> p n c", c=CHUNK)
                        last = cums[:, :, CHUNK - 1:CHUNK] if z == 0 else cums[:, :, 0:1]
                        dve.wait_ge(decay_vec.sem, decay_vec.n)
                        nc.vector.tensor_tensor(tmp[:, 1, :].rearrange("p (n c) -> p n c", c=CHUNK),
                                                last.to_broadcast([P, NCH, CHUNK]), cums, ALU.subtract)\
                            .then_inc(decay_vec.sem, decay_vec.up())
                        dve.wait_ge(decay_act.sem, decay_act.at(SCA * i + 7))
                        nc.vector.tensor_tensor(kd[z][j], kd[z][j], k_[j], ALU.mult)
                        nc.vector.tensor_tensor(ke[z][j], k_[j], tmp[:, 3, :], ALU.mult)\
                            .then_inc(decay_vec.sem, decay_vec.up())
                    dve.wait_ge(pads.sem, pads.n)
                    dve.wait_ge(copied.sem, group_copied("sx", J - 1))
                    for j in range(J):
                        sx, sc, sbt = (u[:, slot[n] + j, :] for n in ("sx", "sc", "sb"))
                        for s, (t0, t1) in enumerate(SEQS):
                            v = sx[:, t0 + 1 + s:t1 + 1 + s]
                            nc.vector.tensor_tensor(v, v, sc[:, t0:t1], ALU.mult).then_inc(short_step.sem, short_step.up())
                        dve.wait_ge(short_step.sem, short_step.n)
                        cv = mix[:, 0:2, :].rearrange("p a t -> p (a t)")[:, 0:T + 1]
                        o = at_a["sc_conv_w"] + j
                        conv3(dve, short_step, cv, sx, lambda k: pa[:, l, o + k * J:o + k * J + 1], T + 1)
                        dve.wait_ge(short_step.sem, short_step.n)
                        for s, (t0, t1) in enumerate(SEQS):
                            nc.vector.tensor_tensor(mix[:, 3 * J + j, t0:t1], cv[:, t0 + s:t1 + s], sbt[:, t0:t1],
                                                    ALU.mult).then_inc(short_step.sem, short_step.up())
                        dve.wait_ge(short_step.sem, short_step.n)
                    for i in range(3 * J):
                        dve.wait_ge(copied.sem, group_copied(("dq", "dk", "dv")[i // J], i % J))
                        o = at_a["gdn_conv_w"] + i
                        conv3(dve, taps, taps_out[i], u[:, slot["dq"] + i, :],
                              lambda k: pa[:, l, o + k * 3 * J:o + k * 3 * J + 1], T + 1)

        def conv3(dve, done, dst, src, w, width):
            nc.vector.tensor_scalar(dst, src[:, 0:width], w(0), None, ALU.mult).then_inc(done.sem, done.up())
            for k in (1, 2):
                dve.wait_ge(done.sem, done.n)
                nc.vector.scalar_tensor_tensor(out=dst, in0=src[:, k:k + width], scalar=w(k), in1=dst,
                                               op0=ALU.mult, op1=ALU.add).then_inc(done.sem, done.up())

        def conformer(l):
            ends = ((0, CTX), (CTX + PADC, CW))
            banks = ((0, 512), (512, CW))
            mean, var, out_tiles = (sem(f"conf_{n}", l) for n in ("mean", "variance", "outputs"))
            centred, squared, scaled, active = (sem(f"conf_{n}", l) for n in ("centred", "squared", "scaled", "active"))
            rstd = sem("conf_rstd", l)
            sq = tmp[:, :, :].rearrange("p a t -> p (a t)")
            sq = [sq[:, j * CW:(j + 1) * CW] for j in range(J)]
            std = tmp[:, :, :].rearrange("p a t -> p (a t)")[:, J * CW:(J + 1) * CW]
            with nc.Block() as block:
                @block.scalar
                def _(act):
                    for j in range(J):
                        act.wait_ge(centred.sem, centred.at(j + 1))
                        nc.scalar.activation(sq[j], conv[:, j, 0:CW], ACT.Square).then_inc(squared.sem, squared.up())
                    act.wait_ge(var.sem, var.at(1))
                    nc.scalar.activation(std, psum[:, 1, 0:CW], ACT.Ln, bias=eps_col[:, 0:1]).then_inc(rstd.sem, rstd.up())
                    act.wait_ge(rstd.sem, rstd.n)
                    nc.scalar.activation(std, std, ACT.Exp, scale=-0.5).then_inc(rstd.sem, rstd.up())
                    for j in range(J):
                        act.wait_ge(scaled.sem, scaled.at(j + 1))
                        nc.scalar.activation(conv[:, j, 0:CW], conv[:, j, 0:CW], ACT.Silu,
                                             scale=pa[:, l, at_a["conv_ln_g"] + j:at_a["conv_ln_g"] + j + 1],
                                             bias=pa[:, l, at_a["conv_ln_b"] + j:at_a["conv_ln_b"] + j + 1])\
                            .then_inc(active.sem, active.up())
                    act.wait_ge(out_tiles.sem, out_tiles.at(1))
                    for (t0, t1), (c0, c1) in zip(SEQS, ends):
                        nc.scalar.activation(mix[:, 0, t0:t1], psum[:, 2, c0:c1], ACT.Copy)

                @block.vector
                def _(dve):
                    dve.wait_ge(mean.sem, mean.at(1))
                    for j in range(J):
                        nc.vector.tensor_tensor(conv[:, j, 0:CW], conv[:, j, 0:CW], psum[:, 0, 0:CW], ALU.subtract)\
                            .then_inc(centred.sem, centred.up())
                    dve.wait_ge(rstd.sem, rstd.at(2))
                    dve.wait_ge(centred.sem, centred.at(J))
                    for j in range(J):
                        nc.vector.tensor_tensor(conv[:, j, 0:CW], conv[:, j, 0:CW], std, ALU.mult)\
                            .then_inc(scaled.sem, scaled.up())
                    dve.wait_ge(out_tiles.sem, out_tiles.at(2))
                    for (t0, t1), (c0, c1) in zip(SEQS, ends):
                        nc.vector.tensor_copy(mix[:, 1, t0:t1], psum[:, 3, c0:c1])

                @block.tensor
                def _(pe):
                    for j in range(J):
                        for c0, c1 in banks:
                            ins = nc.tensor.matmul(psum[:, 0, c0:c1], mean_g[:], conv[:, j, c0:c1],
                                                   start=(j == 0), stop=(j == J - 1))
                    ins.then_inc(mean.sem, mean.up())
                    pe.wait_ge(squared.sem, squared.at(J))
                    for j in range(J):
                        for c0, c1 in banks:
                            ins = nc.tensor.matmul(psum[:, 1, c0:c1], mean_g[:], sq[j][:, c0:c1],
                                                   start=(j == 0), stop=(j == J - 1))
                    ins.then_inc(var.sem, var.up())
                    pe.wait_ge(active.sem, active.at(J))
                    for m in range(J):
                        for k in range(J):
                            for c0, c1 in banks:
                                ins = nc.tensor.matmul(psum[:, 2 + m, c0:c1], pw[:, k, m * P:(m + 1) * P],
                                                       conv[:, k, c0:c1], start=(k == 0), stop=(k == J - 1))
                        ins.then_inc(out_tiles.sem, out_tiles.up())

        def gla(l):
            v = [u[:, slot["gv"] + j, 0:T] for j in range(J)]
            qe, ke, kd = gla_parts()
            free = slot["sb"]
            kd_tok = u[:, free:free + 4, :].rearrange("p s w -> p (s w)")[:, 0:TT * 2 * GW]\
                .rearrange("p (t z f) -> p t z f", t=TT, z=2)
            v_tok = u[:, free + 4:free + 6, :].rearrange("p s w -> p (s w)")[:, 0:TT * GW]\
                .rearrange("p (t f) -> p t f", t=TT)
            PAIRS = [(z, j) for z in range(2) for j in range(J)]
            dec = chunk_decay[:].rearrange("p (z j n) -> p z j n", z=2, j=J)

            copied_d, copied_e = sem("gla_turned_vector", l), sem("gla_turned_scalar", l)
            turned = sem("gla_turned", l)
            jobs = [(v[j], lambda j=j: v_tok[:, :, j * P:(j + 1) * P]) for j in range(J)] + \
                   [(kd[z][j], lambda z=z, j=j: kd_tok[:, :, z, j * P:(j + 1) * P]) for z, j in PAIRS]
            with nc.Block() as block:
                @block.tensor
                def _(pe):
                    for i, (src, _) in enumerate(jobs):
                        if i >= 4:
                            pe.wait_ge((copied_d, copied_e)[i % 2].sem, (copied_d, copied_e)[i % 2].at((i - 4) // 2 + 1))
                        for t in range(TT):
                            ins = nc.tensor.transpose(psum[:, i % 4, t * P:(t + 1) * P], src[:, t * P:(t + 1) * P],
                                                      ident[:])
                        ins.then_inc(turned.sem, turned.up())

                @block.vector
                def _(dve):
                    for i in range(0, len(jobs), 2):
                        dve.wait_ge(turned.sem, turned.at(i + 1))
                        nc.vector.tensor_copy(jobs[i][1](), psum[:, i % 4, 0:T].rearrange("p (t n) -> p t n", n=P)).then_inc(copied_d.sem, copied_d.up())

                @block.scalar
                def _(act):
                    for i in range(1, len(jobs), 2):
                        act.wait_ge(turned.sem, turned.at(i + 1))
                        nc.scalar.activation(jobs[i][1](), psum[:, i % 4, 0:T].rearrange("p (t n) -> p t n", n=P),
                                                         ACT.Copy).then_inc(copied_e.sem, copied_e.up())

            updates, states = sem("gla_updates", l), sem("gla_states", l)
            state_in, state_out = sem("gla_state_in", l), sem("gla_state_out", l)
            S = tmp[:].rearrange("p a t -> p (a t)").rearrange("p (z j n e) -> p z j n e", z=2, j=J, e=DK)
            final = wide[:, 0, 0:2 * J * DK].rearrange("p (z j e) -> p z j e", z=2, e=DK)
            CC = CTX // CHUNK

            def update(i, n):
                c = (n % 2) * 512 + (n // 2) * DK
                return psum[:, i, c:c + DK]
            orders = {0: (list(range(CC)), list(range(CC, NCH))), 1: (list(range(CC))[::-1], list(range(CC, NCH))[::-1])}
            with nc.Block() as block:
                @block.sync
                def _(sp):
                    for z, j in PAIRS:
                        sp.dma_start(S[:, z, j, orders[z][1][0], :],
                                     a["state_gla"][0, l, z, 2 * j:2 * j + 2].rearrange("h d e -> (h d) e")).then_inc(state_in.sem, state_in.up(16))
                    sp.wait_ge(states.sem, states.at(4 + 4 * NCH - 4))
                    for z, j in PAIRS:
                        sp.dma_start(out["gla"][0, l, z, 2 * j:2 * j + 2].rearrange("h d e -> (h d) e"),
                                     final[:, z, j, :]).then_inc(state_out.sem, state_out.up(16))
                    sp.wait_ge(state_out.sem, state_out.at(64))

                @block.tensor
                def _(pe):
                    for i, (z, j) in enumerate(PAIRS):
                        for n in range(NCH):
                            r0 = (n % 2) * CHUNK
                            for hp in range(2):
                                c = j * P + hp * DK
                                ins = nc.tensor.matmul(update(i, n)[hp * DK:(hp + 1) * DK, :],
                                                       kd_tok[r0:r0 + CHUNK, n // 2, z, c:c + DK],
                                                       v_tok[r0:r0 + CHUNK, n // 2, c:c + DK], start=True, stop=True)
                        ins.then_inc(updates.sem, updates.up())

                @block.vector
                def _(dve):
                    for z, j in PAIRS:
                        nc.vector.memset(S[:, z, j, orders[z][0][0], :], 0.0).then_inc(states.sem, states.up())
                    dve.wait_ge(states.sem, states.n)
                    dve.wait_ge(state_in.sem, state_in.at(64))
                    dve.wait_ge(updates.sem, updates.at(4))
                    for step in range(NCH - CC):
                        for seq in range(2):
                            for i, (z, j) in enumerate(PAIRS):
                                order = orders[z][seq]
                                if step >= len(order) or (seq == 1 and step == len(order) - 1):
                                    continue
                                n = order[step]
                                to = S[:, z, j, order[step + 1], :] if step + 1 < len(order) else final[:, z, j, :]
                                ins = nc.vector.scalar_tensor_tensor(
                                    out=to, in0=S[:, z, j, n, :], scalar=dec[:, z, j, n:n + 1],
                                    in1=update(i, n), op0=ALU.mult, op1=ALU.add)
                                ins.then_inc(states.sem, states.up())
                        dve.wait_ge(states.sem, states.n)

            scores, masked, outs, kept = (sem(f"gla_{n}", l) for n in ("scores", "masked", "outs", "kept"))
            att = u[:, free:free + 4, :].rearrange("p s w -> p (s w)")
            att = att[:, 0:4 * 512].rearrange("p (b h c) -> p b h c", b=4, h=H)
            o = [v[j] for j in range(J)]
            with nc.Block() as block:
                @block.tensor
                def _(pe):
                    def attend(t):
                        for z in range(2):
                            i = 2 * t + z
                            if i >= 3:
                                pe.wait_ge(masked.sem, masked.at(i - 2))
                            for hd in range(H):
                                r0 = (hd % 2) * DK
                                c = (hd % 2) * 512 + (hd // 2) * P
                                ins = nc.tensor.matmul(psum[:, i % 3, c:c + P],
                                                       ke[z][hd // 2][r0:r0 + DK, t * P:(t + 1) * P],
                                                       qe[z][hd // 2][r0:r0 + DK, t * P:(t + 1) * P],
                                                       start=True, stop=True)
                            ins.then_inc(scores.sem, scores.up())
                    attend(0)
                    for t in range(TT):
                        if t + 1 < TT:
                            attend(t + 1)
                        pe.wait_ge(masked.sem, masked.at(2 * t + 2))
                        if t >= 2:
                            pe.wait_ge(kept.sem, kept.at(t - 1))
                        for hd in range(H):
                            r0, j = (hd % 2) * DK, hd // 2
                            o_ps = bank(6 + t % 2)[r0:r0 + DK, j * P:(j + 1) * P]
                            for z in range(2):
                                nc.tensor.matmul(o_ps, v_tok[:, t, hd * DK:(hd + 1) * DK], att[:, (2 * t + z) % 4, hd, :],
                                                 start=(z == 0), stop=False, skip_group_check=True)
                            for z in range(2):
                                for c in range(2):
                                    n = 2 * t + c
                                    ins = nc.tensor.matmul(o_ps[:, c * CHUNK:(c + 1) * CHUNK],
                                                           S[r0:r0 + DK, z, j, n, :],
                                                           qe[z][j][r0:r0 + DK, n * CHUNK:(n + 1) * CHUNK],
                                                           start=False, stop=(z == 1), skip_group_check=True)
                        ins.then_inc(outs.sem, outs.up())

                @block.vector
                def _(dve):
                    for t in range(TT):
                        for z in range(2):
                            i = 2 * t + z
                            dve.wait_ge(scores.sem, scores.at(i + 1))
                            if i >= 4:
                                dve.wait_ge(outs.sem, outs.at(i // 2 - 1))
                            nc.vector.tensor_tensor(
                                att[:, i % 4, :, :].rearrange("p (j i) c -> p i j c", i=2),
                                psum[:, i % 3, :].rearrange("p (i r) -> p i r", i=2)[:, :, 0:J * P]
                                .rearrange("p i (j c) -> p i j c", j=J),
                                chunk_until[:, z, :].unsqueeze(1).unsqueeze(1).to_broadcast([P, 2, J, P]), ALU.mult).then_inc(masked.sem, masked.up())

                @block.scalar
                def _(act):
                    for t in range(TT):
                        act.wait_ge(outs.sem, outs.at(t + 1))
                        dst = u[:, slot["gv"]:slot["gv"] + J, t * P:(t + 1) * P]
                        nc.scalar.activation(dst, bank(6 + t % 2)[:, 0:J * P].rearrange("p (j c) -> p j c", j=J),
                                                     ACT.Copy).then_inc(kept.sem, kept.up())
            gated_norm(l, "gla", slot["gv"], slot["gg"], J, at_a["gla_norm_g"], permuted=False)

        def gated_norm(l, name, o_slot, gate_slot, first, norm, permuted):
            scalar_done, tensor_done, vector_done = (sem(f"{name}_norm_{n}", l) for n in ("scalar", "products", "vector"))
            with nc.Block() as block:
                @block.scalar
                def _(act):
                    for j in range(J):
                        nc.scalar.activation(tmp[:, j, :], u[:, o_slot + j, 0:T], ACT.Square).then_inc(scalar_done.sem, scalar_done.up())
                    for j in range(J):
                        nc.scalar.activation(u[:, gate_slot + j, 0:T], u[:, gate_slot + j, 0:T], ACT.Silu).then_inc(scalar_done.sem, scalar_done.up())
                    for j in range(J):
                        act.wait_ge(tensor_done.sem, tensor_done.at(j + 1))
                        nc.scalar.activation(tmp[:, J + j, :], psum[:, j, 0:T], ACT.Ln, bias=eps_col[:, 0:1],
                                                  scale=1.0 / DK).then_inc(scalar_done.sem, scalar_done.up())
                    act.wait_ge(scalar_done.sem, scalar_done.n)
                    for j in range(J):
                        nc.scalar.activation(tmp[:, J + j, :], tmp[:, J + j, :], ACT.Exp, scale=-0.5).then_inc(scalar_done.sem, scalar_done.up())

                @block.tensor
                def _(pe):
                    for j in range(J):
                        pe.wait_ge(scalar_done.sem, scalar_done.at(j + 1))
                        for c0, c1 in SHORT:
                            ins = nc.tensor.matmul(psum[:, j, c0:c1], head_sum[:], tmp[:, j, c0:c1], start=True, stop=True)
                        ins.then_inc(tensor_done.sem, tensor_done.up())

                @block.vector
                def _(dve):
                    for j in range(J):
                        dve.wait_ge(scalar_done.sem, scalar_done.at(3 * J + j + 1))
                        o = u[:, o_slot + j, :]
                        nc.vector.tensor_tensor(o[:, 0:T], o[:, 0:T], tmp[:, J + j, :], ALU.mult).then_inc(vector_done.sem, vector_done.up())
                        dve.wait_ge(vector_done.sem, vector_done.n)
                        for t0, t1 in SEQS:
                            src, gt, dst = o[:, t0:t1], u[:, gate_slot + j, t0:t1], mix[:, first + j, t0:t1]
                            if permuted and t0:
                                src = src.rearrange("p (c r) -> p r c", r=ROWS)
                                gt, dst = (w.rearrange("p (r c) -> p r c", r=ROWS) for w in (gt, dst))
                            nc.vector.scalar_tensor_tensor(out=dst, in0=src, scalar=pa[:, l, norm + j:norm + j + 1],
                                                                in1=gt, op0=ALU.mult, op1=ALU.mult).then_inc(vector_done.sem, vector_done.up())

        def gdn(l):
            feat = [u[:, slot["dq"] + i, 0:T] for i in range(3 * J)]

            def area(first, n, size):
                return u[:, first:first + n, :].rearrange("p s w -> p (s w)")[:, 0:size]
            k_tok = area(6, 2, TT * GW).rearrange("p (t f) -> p t f", t=TT)
            v_tok = area(8, 2, TT * GW).rearrange("p (t f) -> p t f", t=TT)
            o_acc = [u[:, 10 + j, 0:T] for j in range(J)]
            col = u[:, 12, :]
            beta = col[:, 0:TT * H].rearrange("p (t h) -> p t h", t=TT)
            dd = col[:, 20:20 + TT * 2 * H].rearrange("p (t z) -> p t z", t=TT)
            la = col[:, 60:60 + TT * 2 * H].rearrange("p (t z) -> p t z", t=TT)
            g = col[:, 100:100 + TT * 2 * H].rearrange("p (t z) -> p t z", t=TT)
            eg = col[:, 140:140 + TT * 2 * H].rearrange("p (t z) -> p t z", t=TT)
            t0c = col[:, 180:180 + TT * 2 * H].rearrange("p (t z) -> p t z", t=TT)
            vector_done2, scalar_done2, tensor_done2 = (sem(f"gdn_norm_{n}", l) for n in ("vector2", "scalar2", "products2"))
            with nc.Block() as block:
                @block.scalar
                def _(act):
                    for i in range(2 * J):
                        nc.scalar.activation(tmp[:, i, :], feat[i], ACT.Square).then_inc(scalar_done2.sem, scalar_done2.up())
                    act.wait_ge(vector_done2.sem, vector_done2.at(2))
                    nc.scalar.activation(beta, beta, ACT.Sigmoid).then_inc(scalar_done2.sem, scalar_done2.up())
                    for i in range(2 * J):
                        act.wait_ge(tensor_done2.sem, tensor_done2.at(2 + i))
                        nc.scalar.activation(tmp[:, i, :], psum[:, i, 0:T], ACT.Ln, bias=eps_col[:, 1:2]).then_inc(scalar_done2.sem, scalar_done2.up())
                    act.wait_ge(scalar_done2.sem, scalar_done2.n)
                    for i in range(2 * J):
                        nc.scalar.activation(tmp[:, i, :], tmp[:, i, :], ACT.Exp, scale=-0.5).then_inc(scalar_done2.sem, scalar_done2.up())
                    act.wait_ge(vector_done2.sem, vector_done2.at(1))
                    nc.scalar.activation(t0c, dd, ACT.Abs).then_inc(scalar_done2.sem, scalar_done2.up())
                    act.wait_ge(scalar_done2.sem, scalar_done2.n)
                    nc.scalar.activation(t0c, t0c, ACT.Exp, scale=-1.0).then_inc(scalar_done2.sem, scalar_done2.up())
                    act.wait_ge(scalar_done2.sem, scalar_done2.n)
                    nc.scalar.activation(t0c, t0c, ACT.Ln, bias=1.0).then_inc(scalar_done2.sem, scalar_done2.up())

                @block.tensor
                def _(pe):
                    bdt = u[0:3 * H, slot["bd"], :]
                    for t in range(TT):
                        ins = nc.tensor.transpose(psum[:, 3, 768 + 16 * t:768 + 16 * t + 3 * H],
                                                  bdt[:, t * P:(t + 1) * P], ident[0:3 * H, 0:3 * H])
                    ins.then_inc(tensor_done2.sem, tensor_done2.up())
                    for i in range(2 * J):
                        pe.wait_ge(scalar_done2.sem, scalar_done2.at(i + 1))
                        for c0, c1 in SHORT:
                            if i == 3 and c0:
                                pe.wait_ge(vector_done2.sem, vector_done2.at(2))
                            ins = nc.tensor.matmul(psum[:, i, c0:c1], head_sum[:], tmp[:, i, c0:c1], start=True, stop=True)
                        ins.then_inc(tensor_done2.sem, tensor_done2.up())

                @block.vector
                def _(dve):
                    dve.wait_ge(tensor_done2.sem, tensor_done2.at(1))
                    nc.vector.tensor_tensor(
                        dd, psum[:, 3, 768:768 + TT * 16].rearrange("p (t c) -> p t c", c=16)[:, :, H:3 * H],
                        dtb[:].unsqueeze(1).to_broadcast([P, TT, 2 * H]), ALU.add).then_inc(vector_done2.sem, vector_done2.up())
                    nc.vector.tensor_copy(
                        beta, psum[:, 3, 768:768 + TT * 16].rearrange("p (t c) -> p t c", c=16)[:, :, 0:H]).then_inc(vector_done2.sem, vector_done2.up())
                    for i in range(2 * J):
                        dve.wait_ge(scalar_done2.sem, scalar_done2.at(10 + i))
                        if i < J:
                            nc.vector.scalar_tensor_tensor(out=feat[i], in0=feat[i], scalar=QSCALE,
                                                                 in1=tmp[:, i, :], op0=ALU.mult, op1=ALU.mult).then_inc(vector_done2.sem, vector_done2.up())
                        else:
                            nc.vector.tensor_tensor(feat[i], feat[i], tmp[:, i, :], ALU.mult).then_inc(vector_done2.sem, vector_done2.up())
                    dve.wait_ge(scalar_done2.sem, scalar_done2.at(16))
                    nc.vector.scalar_tensor_tensor(out=la, in0=dd, scalar=0.0, in1=t0c, op0=ALU.max, op1=ALU.add).then_inc(vector_done2.sem, vector_done2.up())
                    dve.wait_ge(vector_done2.sem, vector_done2.n)
                    nc.vector.scalar_tensor_tensor(out=la, in0=la, scalar=-1.0,
                                                         in1=nega[:].unsqueeze(1).to_broadcast([P, TT, 2 * H]),
                                                         op0=ALU.mult, op1=ALU.mult).then_inc(vector_done2.sem, vector_done2.up())
            scalar_done3, tensor_done3, vector_done3 = (sem(f"gdn_turn_{n}", l) for n in ("scalar3", "products3", "vector3"))
            with nc.Block() as block:
                @block.tensor
                def _(pe):
                    for i in range(4):
                        for t in range(TT):
                            ins = nc.tensor.transpose(psum[:, i, t * P:(t + 1) * P], feat[J + i][:, t * P:(t + 1) * P],
                                                      ident[:])
                        ins.then_inc(tensor_done3.sem, tensor_done3.up())
                    pe.wait_ge(vector_done3.sem, vector_done3.at(1))
                    for z in range(2):
                        ins = nc.tensor.matmul(psum[:, 0, z * TT * H:(z + 1) * TT * H], until[:, z, :],
                                               la[:, :, z * H:(z + 1) * H], start=True, stop=True)
                    ins.then_inc(tensor_done3.sem, tensor_done3.up())

                @block.vector
                def _(dve):
                    for i in (0, 2):
                        dve.wait_ge(tensor_done3.sem, tensor_done3.at(i + 1))
                        dst = (k_tok, v_tok)[i // 2][:, :, 0:P]
                        nc.vector.tensor_copy(dst, psum[:, i, 0:T].rearrange("p (t n) -> p t n", n=P)).then_inc(vector_done3.sem, vector_done3.up())
                    dve.wait_ge(tensor_done3.sem, tensor_done3.at(5))
                    nc.vector.tensor_copy(g.rearrange("p t (z h) -> p z t h", z=2),
                                                psum[:, 0, 0:2 * TT * H].rearrange("p (z t h) -> p z t h", z=2, t=TT)).then_inc(vector_done3.sem, vector_done3.up())

                @block.scalar
                def _(act):
                    for i in (1, 3):
                        act.wait_ge(tensor_done3.sem, tensor_done3.at(i + 1))
                        dst = (k_tok, v_tok)[i // 2][:, :, P:2 * P]
                        nc.scalar.activation(dst, psum[:, i, 0:T].rearrange("p (t n) -> p t n", n=P), ACT.Copy).then_inc(scalar_done3.sem, scalar_done3.up())
                    act.wait_ge(vector_done3.sem, vector_done3.at(3))
                    nc.scalar.activation(eg, g, ACT.Exp).then_inc(scalar_done3.sem, scalar_done3.up())
            gdn_chunks(l, feat, k_tok, v_tok, o_acc, beta, la, g, eg)
            gated_norm(l, "gdn", 10, slot["dgate"], 2 * J, at_a["gdn_norm_g"], permuted=True)

        def gdn_chunks(l, feat, k_tok, v_tok, o_acc, beta, la, g, eg):
            qf, kf = feat[0:J], feat[J:2 * J]
            rounds = [(0, 0)] + [(1 + i, TT - 1 - i) for i in range(TT - 1)]
            seen = set()
            first_visit = []
            for r in rounds:
                pair = []
                for t in r:
                    pair.append(t not in seen)
                    seen.add(t)
                first_visit.append(pair)
            flat_a = u[:, 0:6, :].rearrange("p s w -> p (s w)")
            flat_b = u[:, slot["sb"]:slot["sb"] + 6, :].rearrange("p s w -> p (s w)")
            flat_t = tmp[:].rearrange("p a t -> p (a t)")
            flat_w = wide[:].rearrange("p a t -> p (a t)")

            def bufs(f, n):
                return [f[:, i * 512:(i + 1) * 512].rearrange("p (h c) -> p h c", h=H) for i in range(n)]
            ba, bb, bt, bw = bufs(flat_a, 7), bufs(flat_b, 7), bufs(flat_t, 5), bufs(flat_w, 5)
            side_bufs = []
            for s, own, more in ((0, ba, bt), (1, bb, bw)):
                side_bufs.append(dict(D=own[0], LT=own[1], QK=own[2], Ti=own[3], TiT=own[4], X=own[5], M=own[6],
                                      EG=more[0], VB=more[1][:, :, 0:DK], KB=more[1][:, :, DK:2 * DK],
                                      KD=more[2][:, :, 0:DK], VN=more[2][:, :, DK:2 * DK],
                                      QG=more[3].rearrange("p h c -> p (h c)")[:, 0:J * P].rearrange("p (j c) -> p j c", j=J),
                                      WT=more[3].rearrange("p h c -> p (h c)")[:, J * P:2 * J * P].rearrange("p (j c) -> p j c", j=J),
                                      S=more[4].rearrange("p h c -> p (h c)")[:, 0:J * DK].rearrange("p (j e) -> p j e", j=J),
                                      EL=more[4].rearrange("p h c -> p (h c)")[:, 200:200 + H],
                                      EK=more[4].rearrange("p h c -> p (h c)")[:, 208:208 + H]))
            LV = 6
            names_ = ["decay_rows", "kk_qk", "turned_l", "x", "tx", "wt", "vn", "out", "upd"]
            tensor_done = {n: sem(f"gdnc_pe_{n}", l) for n in names_}
            vector_done = sem("gdnc_vector", l)
            scalar_done = sem("gdnc_scalar", l)
            pool_done = sem("gdnc_pool", l)
            st_in, st_out = sem("gdn_state_in", l), sem("gdn_state_out", l)

            DV = {n: i for i, n in enumerate(
                ["state", "dm", "dmin", "ek", "qg0", "qg1", "qkm", "ltb", "lt", "vb", "kd", "kb0", "kb", "ti0", "tit0"] +
                [f"{n}{b}" for b in range(LV) for n in ("t", "tt")] + ["vn", "oacc", "s0", "s1", "s2", "s3"])}
            AC = {n: i for i, n in enumerate(["exp", "eg", "el", "ekx"] + [f"x{b}" for b in range(LV)] + ["wt"])}
            PO = {n: i for i, n in enumerate(["strict"] + [f"m{b}" for b in range(LV)])}

            def dn(r, n, s):
                return (r * len(DV) + DV[n]) * 2 + s + 1

            def an(r, n, s):
                return (r * len(AC) + AC[n]) * 2 + s + 1

            def pn(r, n, s):
                return (r * len(PO) + PO[n]) * 2 + s + 1

            def en(r, s, per=1, i=0):
                return (r * per + i) * 2 + s + 1

            R = len(rounds)
            with nc.Block() as block:
                @block.sync
                def _(sp):
                    for s in range(2):
                        sp.wait_ge(vector_done.sem, vector_done.at(dn(0, "s3", s)))
                        for j in range(J):
                            sp.dma_start(out["gdn"][0, l, s, 2 * j:2 * j + 2].rearrange("h d e -> (h d) e"),
                                         side_bufs[s]["S"][:, j, :]).then_inc(st_out.sem, st_out.up(16))
                    for n in ("out",):
                        sp.wait_ge(tensor_done[n].sem, tensor_done[n].at(en(0, 1)))
                    sp.wait_ge(st_out.sem, st_out.at(64))
                    for s in range(2):
                        for j in range(J):
                            sp.dma_start(side_bufs[s]["S"][:, j, :],
                                         a["state_gdn"][0, l, s, 2 * j:2 * j + 2].rearrange("h d e -> (h d) e")).then_inc(st_in.sem, st_in.up(16))

                @block.tensor
                def _(pe):
                    for r, tiles in enumerate(rounds):
                        for s, t in enumerate(tiles):
                            B = side_bufs[s]
                            b0, b1, b2, b3 = (bank(4 * s + i) for i in range(4))
                            if r:
                                pe.wait_ge(vector_done.sem, vector_done.at(dn(r - 1, "s3", s)))
                            for hd in range(H):
                                nc.tensor.matmul(b0[:, hd * P:(hd + 1) * P],
                                                 la[:, t, s * H + hd:s * H + hd + 1].to_broadcast([P, P]),
                                                 until[:, s, :], start=True, stop=True)
                            for hd in range(H):
                                ins = nc.tensor.matmul(b3[:, hd * P:(hd + 1) * P],
                                                       beta[:, t, hd:hd + 1].to_broadcast([P, P]), ident[:],
                                                       start=True, stop=True)
                            ins.then_inc(tensor_done["decay_rows"].sem, tensor_done["decay_rows"].up())
                        for hp, (s, t) in ((i, side) for i in range(2) for side in enumerate(tiles)):
                            b0, b1, b2, b3 = (bank(4 * s + i) for i in range(4))
                            if hp == 1:
                                pe.wait_ge(tensor_done["kk_qk"].sem, tensor_done["kk_qk"].at((r * 2) * 2 + s + 1))
                            for hd in range(hp, H, 2):
                                r0, j = (hd % 2) * DK, hd // 2
                                ks = kf[j][r0:r0 + DK, t * P:(t + 1) * P]
                                nc.tensor.matmul(b1[:, hd * P:(hd + 1) * P], ks, ks, start=True, stop=True)
                                ins = nc.tensor.matmul(b2[:, hd * P:(hd + 1) * P], ks,
                                                       qf[j][r0:r0 + DK, t * P:(t + 1) * P], start=True, stop=True)
                            ins.then_inc(tensor_done["kk_qk"].sem, tensor_done["kk_qk"].up())
                        for s, t in enumerate(tiles):
                            B = side_bufs[s]
                            pe.wait_ge(vector_done.sem, vector_done.at(dn(r, "lt", s)))
                            for hd in range(H):
                                ins = nc.tensor.transpose(bank(4 * s + 3)[:, hd * P:(hd + 1) * P], B["LT"][:, hd, :], ident[:])
                            ins.then_inc(tensor_done["turned_l"].sem, tensor_done["turned_l"].up())
                        for b in range(LV):
                            for s, t in enumerate(tiles):
                                B = side_bufs[s]
                                b0 = bank(4 * s)
                                pe.wait_ge(pool_done.sem, pool_done.at(pn(r, f"m{b}", s)))
                                pe.wait_ge(vector_done.sem, vector_done.at(dn(r, "ti0" if b == 0 else f"tt{b - 1}", s)))
                                if b == 0:
                                    pe.wait_ge(scalar_done.sem, scalar_done.at(an(r, "ekx", s)))
                                else:
                                    pe.wait_ge(scalar_done.sem, scalar_done.at(an(r, f"x{b - 1}", s)))
                                for hd in range(H):
                                    ins = nc.tensor.matmul(b0[:, hd * P:(hd + 1) * P], B["M"][:, hd, :], B["Ti"][:, hd, :],
                                                           start=True, stop=True)
                                ins.then_inc(tensor_done["x"].sem, tensor_done["x"].up())
                            for s, t in enumerate(tiles):
                                B = side_bufs[s]
                                b1, b2 = bank(4 * s + 1), bank(4 * s + 2)
                                pe.wait_ge(scalar_done.sem, scalar_done.at(an(r, f"x{b}", s)))
                                pe.wait_ge(vector_done.sem, vector_done.at(dn(r, "tit0" if b == 0 else f"tt{b - 1}", s)))
                                for hd in range(H):
                                    if b < LV - 1:
                                        nc.tensor.matmul(b1[:, hd * P:(hd + 1) * P], B["TiT"][:, hd, :], B["X"][:, hd, :],
                                                         start=True, stop=True)
                                    ins = nc.tensor.matmul(b2[:, hd * P:(hd + 1) * P], B["X"][:, hd, :], B["TiT"][:, hd, :],
                                                           start=True, stop=True)
                                ins.then_inc(tensor_done["tx"].sem, tensor_done["tx"].up())
                        for s, t in enumerate(tiles):
                            B = side_bufs[s]
                            b3 = bank(4 * s + 3)
                            pe.wait_ge(vector_done.sem, vector_done.at(dn(r, f"tt{LV - 1}", s)))
                            for hd in range(H):
                                r0, j = (hd % 2) * DK, hd // 2
                                ins = nc.tensor.matmul(b3[r0:r0 + DK, j * P:(j + 1) * P], B["KB"][:, hd, :], B["TiT"][:, hd, :],
                                                       start=True, stop=True)
                            ins.then_inc(tensor_done["wt"].sem, tensor_done["wt"].up())
                        for s, t in enumerate(tiles):
                            B = side_bufs[s]
                            pe.wait_ge(scalar_done.sem, scalar_done.at(an(r, "wt", s)))
                            for hd in range(H):
                                r0, j = (hd % 2) * DK, hd // 2
                                vn = bank(4 * s + hd % 2)[:, j * DK:(j + 1) * DK]
                                nc.tensor.matmul(vn, B["TiT"][:, hd, :], B["VB"][:, hd, :], start=True, stop=False)
                                ins = nc.tensor.matmul(vn, B["WT"][r0:r0 + DK, j, :], B["S"][r0:r0 + DK, j, :],
                                                       start=False, stop=True)
                            ins.then_inc(tensor_done["vn"].sem, tensor_done["vn"].up())
                        for s, t in enumerate(tiles):
                            B = side_bufs[s]
                            b2, b3 = bank(4 * s + 2), bank(4 * s + 3)
                            pe.wait_ge(vector_done.sem, vector_done.at(dn(r, "vn", s)))
                            for hd in range(H):
                                r0, j = (hd % 2) * DK, hd // 2
                                o = b3[r0:r0 + DK, j * P:(j + 1) * P]
                                nc.tensor.matmul(o, B["VN"][:, hd, :], B["QK"][:, hd, :], start=True, stop=False)
                                ins = nc.tensor.matmul(o, B["S"][r0:r0 + DK, j, :], B["QG"][r0:r0 + DK, j, :],
                                                       start=False, stop=True)
                            ins.then_inc(tensor_done["out"].sem, tensor_done["out"].up())
                            for hd in range(H):
                                r0, j = (hd % 2) * DK, hd // 2
                                ins = nc.tensor.matmul(b2[r0:r0 + DK, j * DK:(j + 1) * DK], B["KD"][:, hd, :],
                                                       B["VN"][:, hd, :], start=True, stop=True)
                            ins.then_inc(tensor_done["upd"].sem, tensor_done["upd"].up())

                @block.scalar
                def _(act):
                    for r, tiles in enumerate(rounds):
                        def both(step):
                            for s, t in enumerate(tiles):
                                step(s, t, side_bufs[s])

                        def exp(s, t, B):
                            act.wait_ge(vector_done.sem, vector_done.at(dn(r, "dmin", s)))
                            nc.scalar.activation(B["D"], B["D"], ACT.Exp).then_inc(scalar_done.sem, scalar_done.up())

                        def egr(s, t, B):
                            act.wait_ge(vector_done.sem, vector_done.at(dn(r, "ek", s)))
                            if r:
                                act.wait_ge(vector_done.sem, vector_done.at(dn(r - 1, "qg1", s)))
                            nc.scalar.activation(B["EG"], bank(4 * s).rearrange("p (h c) -> p h c", h=H), ACT.Exp).then_inc(scalar_done.sem, scalar_done.up())

                        def el(s, t, B):
                            last = bank(4 * s).rearrange("p (h c) -> p h c", h=H)[:, :, (P - 1) if s == 0 else 0]
                            if r:
                                act.wait_ge(vector_done.sem, vector_done.at(dn(r - 1, "s3", s)))
                            nc.scalar.activation(B["EL"], last, ACT.Exp).then_inc(scalar_done.sem, scalar_done.up())

                        def ekx(s, t, B):
                            act.wait_ge(vector_done.sem, vector_done.at(dn(r, "ek", s)))
                            nc.scalar.activation(B["EK"], B["EK"], ACT.Exp).then_inc(scalar_done.sem, scalar_done.up())
                        for f in (exp, egr, el, ekx):
                            both(f)
                        for b in range(LV):
                            def xcopy(s, t, B):
                                act.wait_ge(tensor_done["x"].sem, tensor_done["x"].at(en(r, s, LV, b)))
                                if b:
                                    act.wait_ge(tensor_done["tx"].sem, tensor_done["tx"].at(en(r, s, LV, b - 1)))
                                nc.scalar.activation(B["X"], bank(4 * s).rearrange("p (h c) -> p h c", h=H), ACT.Copy).then_inc(scalar_done.sem, scalar_done.up())
                            both(xcopy)

                        def wt(s, t, B):
                            act.wait_ge(tensor_done["wt"].sem, tensor_done["wt"].at(en(r, s)))
                            nc.scalar.mul(B["WT"], bank(4 * s + 3)[:, 0:J * P].rearrange("p (j c) -> p j c", j=J), -1.0).then_inc(scalar_done.sem, scalar_done.up())
                        both(wt)

                @block.gpsimd
                def _(pool):
                    for r, tiles in enumerate(rounds):
                        for s, t in enumerate(tiles):
                            B = side_bufs[s]
                            pool.wait_ge(scalar_done.sem, scalar_done.at(an(r, "exp", s)))
                            nc.gpsimd.tensor_tensor(B["D"], B["D"], until[:, s:s + 1, :].to_broadcast([P, H, P]), ALU.mult).then_inc(pool_done.sem, pool_done.up())
                        for b in range(LV):
                            for s, t in enumerate(tiles):
                                B = side_bufs[s]
                                if b == 0:
                                    pool.wait_ge(vector_done.sem, vector_done.at(dn(r, "lt", s)))
                                else:
                                    pool.wait_ge(tensor_done["x"].sem, tensor_done["x"].at(en(r, s, LV, b - 1)))
                                nc.gpsimd.tensor_tensor(B["M"], B["LT"],
                                                              level[:, b + 1, s:s + 1, :].to_broadcast([P, H, P]), ALU.mult).then_inc(pool_done.sem, pool_done.up())

                @block.vector
                def _(dve):
                    def v3(n):
                        return bank(n).rearrange("p (h c) -> p h c", h=H)

                    for r, tiles in enumerate(rounds):
                        def both(step):
                            for s, t in enumerate(tiles):
                                step(s, t, side_bufs[s])

                        def state(s, t, B):
                            if r == 0:
                                ins = nc.vector.memset(B["S"], 0.0)
                            else:
                                if r == 1:
                                    dve.wait_ge(st_in.sem, st_in.at(64))
                                ins = nc.vector.memset(B["EK"], 0.0)
                            ins.then_inc(vector_done.sem, vector_done.up())

                        def dm(s, t, B):
                            dve.wait_ge(tensor_done["decay_rows"].sem, tensor_done["decay_rows"].at(en(r, s)))
                            if r:
                                dve.wait_ge(pool_done.sem, pool_done.at(pn(r - 1, f"m{LV - 1}", s)))
                            gz = g[:, t, s * H:(s + 1) * H].unsqueeze(2).to_broadcast([P, H, P])
                            nc.vector.tensor_tensor(B["D"], v3(4 * s), gz, ALU.subtract).then_inc(vector_done.sem, vector_done.up())

                        def dmin(s, t, B):
                            dve.wait_ge(vector_done.sem, vector_done.at(dn(r, "dm", s)))
                            nc.vector.tensor_scalar(B["D"], B["D"], 0.0, None, ALU.min).then_inc(vector_done.sem, vector_done.up())

                        def ek(s, t, B):
                            last = v3(4 * s)[:, :, (P - 1) if s == 0 else 0]
                            dve.wait_ge(vector_done.sem, vector_done.at(dn(r, "state", s)))
                            nc.vector.tensor_tensor(B["EK"], last, g[:, t, s * H:(s + 1) * H], ALU.subtract).then_inc(vector_done.sem, vector_done.up())

                        def qg(s, t, B, hp):
                            dve.wait_ge(scalar_done.sem, scalar_done.at(an(r, "eg", s)))
                            r0 = hp * DK
                            egv = B["EG"].rearrange("p (j i) c -> p j i c", i=2)[r0:r0 + DK, :, hp, :]
                            qv = u[r0:r0 + DK, slot["dq"]:slot["dq"] + J, t * P:(t + 1) * P]
                            nc.vector.tensor_tensor(B["QG"][r0:r0 + DK, :, :], qv, egv, ALU.mult).then_inc(vector_done.sem, vector_done.up())

                        def qkm(s, t, B):
                            dve.wait_ge(tensor_done["kk_qk"].sem, tensor_done["kk_qk"].at(en(r, s, 2, 1)))
                            dve.wait_ge(pool_done.sem, pool_done.at(pn(r, "strict", s)))
                            nc.vector.tensor_tensor(B["QK"], v3(4 * s + 2), B["D"], ALU.mult).then_inc(vector_done.sem, vector_done.up())

                        def ltb(s, t, B):
                            nc.vector.tensor_tensor(B["LT"], v3(4 * s + 1), B["D"], ALU.mult).then_inc(vector_done.sem, vector_done.up())

                        def lt(s, t, B):
                            dve.wait_ge(vector_done.sem, vector_done.at(dn(r, "ltb", s)))
                            nc.vector.tensor_tensor(B["LT"], v3(4 * s + 3), B["LT"], ALU.mult).then_inc(vector_done.sem, vector_done.up())

                        def vb(s, t, B):
                            bt = beta[:, t, :].unsqueeze(2).to_broadcast([P, H, DK])
                            nc.vector.tensor_tensor(B["VB"], v_tok[:, t, :].rearrange("p (h e) -> p h e", h=H), bt, ALU.mult).then_inc(vector_done.sem, vector_done.up())

                        def kdec(s, t, B):
                            dve.wait_ge(scalar_done.sem, scalar_done.at(an(r, "ekx", s)))
                            bt = B["EK"].unsqueeze(2).to_broadcast([P, H, DK])
                            nc.vector.tensor_tensor(B["KD"], k_tok[:, t, :].rearrange("p (h e) -> p h e", h=H), bt, ALU.mult).then_inc(vector_done.sem, vector_done.up())

                        def kb0(s, t, B):
                            bt = beta[:, t, :].unsqueeze(2).to_broadcast([P, H, DK])
                            nc.vector.tensor_tensor(B["KB"], k_tok[:, t, :].rearrange("p (h e) -> p h e", h=H), bt, ALU.mult).then_inc(vector_done.sem, vector_done.up())

                        def kb(s, t, B):
                            dve.wait_ge(vector_done.sem, vector_done.at(dn(r, "kb0", s)))
                            bt = eg[:, t, s * H:(s + 1) * H].unsqueeze(2).to_broadcast([P, H, DK])
                            nc.vector.tensor_tensor(B["KB"], B["KB"], bt, ALU.mult).then_inc(vector_done.sem, vector_done.up())

                        def ti0(s, t, B):
                            dve.wait_ge(tensor_done["turned_l"].sem, tensor_done["turned_l"].at(en(r, s)))
                            m = level0t[:, s:s + 1, :].to_broadcast([P, H, P])
                            nc.vector.tensor_tensor(B["Ti"], v3(4 * s + 3), m, ALU.mult).then_inc(vector_inner.sem, 1)
                            vector_inner.n += 1
                            dve.wait_ge(vector_inner.sem, vector_inner.n)
                            nc.vector.scalar_tensor_tensor(out=B["Ti"], in0=B["Ti"], scalar=-1.0,
                                                                 in1=ident[:].unsqueeze(1).to_broadcast([P, H, P]),
                                                                 op0=ALU.mult, op1=ALU.add).then_inc(vector_done.sem, vector_done.up())

                        def tit0(s, t, B):
                            m = level[:, 0, s:s + 1, :].to_broadcast([P, H, P])
                            nc.vector.tensor_tensor(B["TiT"], B["LT"], m, ALU.mult).then_inc(vector_inner.sem, 1)
                            vector_inner.n += 1
                            dve.wait_ge(vector_inner.sem, vector_inner.n)
                            nc.vector.scalar_tensor_tensor(out=B["TiT"], in0=B["TiT"], scalar=-1.0,
                                                                 in1=ident[:].unsqueeze(1).to_broadcast([P, H, P]),
                                                                 op0=ALU.mult, op1=ALU.add).then_inc(vector_done.sem, vector_done.up())
                        for f in (state, dm, dmin, ek):
                            both(f)
                        both(lambda s, t, B: qg(s, t, B, 0))
                        both(lambda s, t, B: qg(s, t, B, 1))
                        for f in (qkm, ltb, lt, vb, kdec, kb0, kb, ti0, tit0):
                            both(f)
                        for b in range(LV):
                            def ti(s, t, B):
                                dve.wait_ge(tensor_done["tx"].sem, tensor_done["tx"].at(en(r, s, LV, b)))
                                if b < LV - 1:
                                    ins = nc.vector.tensor_tensor(B["Ti"], B["Ti"], v3(4 * s + 1), ALU.subtract)
                                else:
                                    ins = nc.vector.memset(B["Ti"][:, 0, 0:1], 0.0)
                                ins.then_inc(vector_done.sem, vector_done.up())

                            def tit(s, t, B):
                                nc.vector.tensor_tensor(B["TiT"], B["TiT"], v3(4 * s + 2), ALU.subtract).then_inc(vector_done.sem, vector_done.up())
                            both(ti)
                            both(tit)

                        def vn(s, t, B):
                            dve.wait_ge(tensor_done["vn"].sem, tensor_done["vn"].at(en(r, s)))
                            nc.vector.tensor_copy(B["VN"].rearrange("p (j i) e -> p i j e", i=2),
                                                        psum[:, 2 * s, :].rearrange("p (i r) -> p i r", i=2)[:, :, 0:J * DK]
                                                        .rearrange("p i (j e) -> p i j e", j=J)).then_inc(vector_done.sem, vector_done.up())

                        def oacc(s, t, B):
                            dve.wait_ge(tensor_done["out"].sem, tensor_done["out"].at(en(r, s)))
                            o = u[:, 10:10 + J, t * P:(t + 1) * P]
                            src = bank(4 * s + 3)[:, 0:J * P].rearrange("p (j c) -> p j c", j=J)
                            if first_visit[r][s]:
                                ins = nc.vector.tensor_copy(o, src)
                            else:
                                dve.wait_ge(vector_done.sem, vector_done.n)
                                ins = nc.vector.tensor_tensor(o, o, src, ALU.add)
                            ins.then_inc(vector_done.sem, vector_done.up())

                        def upd(s, t, B, hd):
                            r0, j = (hd % 2) * DK, hd // 2
                            dve.wait_ge(tensor_done["upd"].sem, tensor_done["upd"].at(en(r, s)))
                            dve.wait_ge(scalar_done.sem, scalar_done.at(an(r, "el", s)))
                            Sv = B["S"][r0:r0 + DK, j, :]
                            nc.vector.scalar_tensor_tensor(out=Sv, in0=Sv, scalar=B["EL"][r0:r0 + DK, hd:hd + 1],
                                                                 in1=bank(4 * s + 2)[r0:r0 + DK, j * DK:(j + 1) * DK],
                                                                 op0=ALU.mult, op1=ALU.add).then_inc(vector_done.sem, vector_done.up())
                        both(vn)
                        both(oacc)
                        for hd in range(H):
                            both(lambda s, t, B: upd(s, t, B, hd))
            return

        vector_inner = sem("vector_inner")

        def close(l, name, c, ln_g, ln_b):
            vector_done, scalar_done, tensor_done = (sem(f"{name}_{n}", l) for n in ("vector", "scalar", "products"))
            sq = [u[:, k, 0:T] for k in range(KD)]
            rs = tmp[:, 0, :]
            with nc.Block() as block:
                @block.tensor
                def _(pe):
                    for k in range(KD):
                        for c0, c1 in SHORT:
                            ins = nc.tensor.matmul(psum[:, 0, c0:c1], mean_d[:], x[:, k, c0:c1],
                                                   start=(k == 0), stop=(k == KD - 1))
                    ins.then_inc(tensor_done.sem, tensor_done.up())
                    for k in range(KD):
                        pe.wait_ge(scalar_done.sem, scalar_done.at(k + 1))
                        for c0, c1 in SHORT:
                            ins = nc.tensor.matmul(psum[:, 1, c0:c1], mean_d[:], sq[k][:, c0:c1],
                                                   start=(k == 0), stop=(k == KD - 1))
                    ins.then_inc(tensor_done.sem, tensor_done.up())

                @block.vector
                def _(dve):
                    dve.wait_ge(tensor_done.sem, tensor_done.at(1))
                    for k in range(KD):
                        nc.vector.tensor_tensor(x[:, k, :], x[:, k, :], psum[:, 0, 0:T], ALU.subtract).then_inc(vector_done.sem, vector_done.up())
                    dve.wait_ge(scalar_done.sem, scalar_done.at(KD + 2))
                    dve.wait_ge(vector_done.sem, vector_done.n)
                    for k in range(KD):
                        nc.vector.tensor_tensor(x[:, k, :], x[:, k, :], rs, ALU.mult).then_inc(vector_done.sem, vector_done.up())

                @block.scalar
                def _(act):
                    for k in range(KD):
                        act.wait_ge(vector_done.sem, vector_done.at(k + 1))
                        nc.scalar.activation(sq[k], x[:, k, :], ACT.Square).then_inc(scalar_done.sem, scalar_done.up())
                    act.wait_ge(tensor_done.sem, tensor_done.at(2))
                    nc.scalar.activation(rs, psum[:, 1, 0:T], ACT.Ln, bias=eps_col[:, 0:1]).then_inc(scalar_done.sem, scalar_done.up())
                    act.wait_ge(scalar_done.sem, scalar_done.n)
                    nc.scalar.activation(rs, rs, ACT.Exp, scale=-0.5).then_inc(scalar_done.sem, scalar_done.up())
                    for k in range(KD):
                        act.wait_ge(vector_done.sem, vector_done.at(KD + k + 1))
                        nc.scalar.activation(x[:, k, :], x[:, k, :], ACT.Identity,
                                                  scale=pa[:, l, ln_g + k:ln_g + k + 1],
                                                  bias=pa[:, l, ln_b + k:ln_b + k + 1]).then_inc(scalar_done.sem, scalar_done.up())

        def project_out(l):
            base, count = parts["out", l]
            vector_done, scalar_done = sem("out_added", l), sem("out_scaled", l)
            with nc.Block() as block:
                @block.sync
                def _(sp):
                    load_ahead(sp, ("out", l))

                @block.scalar
                def _(act):
                    for k in range(KD):
                        nc.scalar.mul(x[:, k, :], x[:, k, :], ALPHA).then_inc(scalar_done.sem, scalar_done.up())

                @block.tensor
                def _(pe):
                    for m in range(KD):
                        block_landed(pe, base + m)
                        if m >= 4:
                            pe.wait_ge(vector_done.sem, vector_done.at(2 * (m - 3)))
                        w = ring_view((base + m) % RING, KD)
                        for k in range(KD):
                            for c0, c1 in SHORT:
                                ins = nc.tensor.matmul(psum[:, m % 4, c0:c1], w[:, k, :], mix[:, k, c0:c1],
                                                       start=(k == 0), stop=(k == KD - 1))
                        ins.then_inc(ring_used.sem, ring_used.up())

                @block.vector
                def _(dve):
                    for m in range(KD):
                        dve.wait_ge(ring_used.sem, ring_used.at(base + m + 1))
                        dve.wait_ge(scalar_done.sem, scalar_done.at(m + 1))
                        for s, (t0, t1) in enumerate(SEQS):
                            nc.vector.scalar_tensor_tensor(out=x[:, m, t0:t1], in0=psum[:, m % 4, t0:t1],
                                                                scalar=mod[:, 2 * KD + m, s:s + 1], in1=x[:, m, t0:t1],
                                                                op0=ALU.mult, op1=ALU.add).then_inc(vector_done.sem, vector_done.up())

        hidden = [u[:, f, 0:T] for f in range(FT)]
        sums = [u[:, FT + m, 0:T] for m in range(KD)]
        weight_rows = u[:, FT:FT + NE, 0:T]
        place_rows = u[:, FT + NE:FT + 2 * NE, 0:T]
        counting = u[:, FT + 2 * NE, 0:T]
        onehot = work[:, 2 * T:2 * T + TT * T].rearrange("p (t n) -> p t n", t=TT)
        rest = work[:, 2 * T + TT * T:]
        places = rest[:, 0:TT * NE].rearrange("p (e t) -> p e t", t=TT)
        slot_number = rest[:, 40:40 + TT]
        blocks_used = rest[:, 48:48 + NE].bitcast(I32)
        y_rows = u[:].rearrange("p s w -> p (s w)")[:, 0:TT * D].rearrange("p (b f) -> p b f", b=TT)
        assert TT * D <= FT * UW and 2 * T + TT * T + 60 <= 4 * T + 4 * 688 and FT + 2 * NE + 1 <= U

        def route(l):
            ones = until[:, 0, P - 1:P]
            area = wide[:, 0, :]
            logits = area[:, 0:TT * NE].rearrange("p (t n) -> p t n", t=TT)
            top = area[:, 40:80].rearrange("p (t n) -> p t n", t=TT)
            index = area[:, 80:120].rearrange("p (t n) -> p t n", t=TT)
            idx = area[:, 120:160].bitcast(U32).rearrange("p (t n) -> p t n", t=TT)
            share = area[:, 160:170].rearrange("p (i t) -> p i t", i=2)
            comb = area[:, 200:240].rearrange("p (t n) -> p t n", t=TT)
            part = area[:, 240:280].rearrange("p (t n) -> p t n", t=TT)
            numbers = area[:, 280:320].rearrange("p (t n) -> p t n", t=TT)
            chosen = area[:, 320:360].rearrange("p (t n) -> p t n", t=TT)
            total = area[:, 360:360 + NE]
            blocks = area[:, 368:368 + NE]
            more = area[:, 376:376 + NE]
            numbers_built = sem("route_numbers", l)
            ranks = sem("route_ranks", l)
            ranks_read = sem("route_ranks_read", l)
            logits_ready = sem("route_logits", l)
            spread = sem("route_spread", l)
            spread_read = sem("route_spread_read", l)
            turned = sem("route_turned", l)
            turned_read = sem("route_turned_read", l)
            lead = sem("route_lead", l)
            lead_exp = sem("route_lead_exp", l)
            inner = sem("route_inner", l)
            chosen_ready = sem("route_chosen", l)
            with nc.Block() as block:
                @block.gpsimd
                def _(pool):
                    for n in range(NE):
                        nc.gpsimd.memset(numbers[:, :, n], float(n)).then_inc(numbers_built.sem, numbers_built.up())

                @block.tensor
                def _(pe):
                    for t in range(TT):
                        for k in range(KD):
                            ins = nc.tensor.matmul(psum[:, 0, t * NE:(t + 1) * NE], h[:, k, t * P:(t + 1) * P],
                                                   router[:, k, :], start=(k == 0), stop=(k == KD - 1))
                    ins.then_inc(logits_ready.sem, logits_ready.up())
                    for t in range(TT):
                        if t >= 3:
                            pe.wait_ge(turned_read.sem, turned_read.at(t - 2))
                        for k in range(KD):
                            ins = nc.tensor.transpose(psum[:, 1 + t % 3, k * P:(k + 1) * P], h[:, k, t * P:(t + 1) * P],
                                                      ident[:])
                        ins.then_inc(turned.sem, turned.up())
                    pe.wait_ge(chosen_ready.sem, chosen_ready.at(1))
                    for t in range(TT):
                        for s in range(t + 1):
                            nc.tensor.matmul(psum[:, 0, t * NE:(t + 1) * NE],
                                             until[:, 0, :] if s == t else ones.to_broadcast([P, P]),
                                             chosen[:, s, :], start=(s == 0), stop=(s == t))
                    for s in range(TT):
                        nc.tensor.matmul(psum[:, 0, TT * NE:(TT + 1) * NE], ones.to_broadcast([P, P]),
                                         chosen[:, s, :], start=(s == 0), stop=(s == TT - 1))
                    nc.tensor.matmul(psum[:, 0, 512:512 + P], ones.to_broadcast([P, P]), until[:, 0, :],
                                     start=True, stop=True)
                    nc.tensor.matmul(psum[:, 0, 512 + P:512 + P + 2], until[:, 0, :], ones.to_broadcast([P, 2]),
                                     start=True, stop=True).then_inc(ranks.sem, ranks.up())
                    pe.wait_ge(ranks_read.sem, ranks_read.at(1))
                    pe.wait_ge(turned_read.sem, turned_read.at(TT))
                    for i in range(2 * NE):
                        if i >= 4:
                            pe.wait_ge(spread_read.sem, spread_read.at(i - 3))
                        for t in range(TT):
                            col = comb[:, t, i // 2:i // 2 + 1] if i % 2 == 0 else places[:, i // 2, t:t + 1]
                            ins = nc.tensor.matmul(psum[:, i % 4, t * P:(t + 1) * P], col.to_broadcast([P, P]),
                                                   ident[:], start=True, stop=True)
                        ins.then_inc(spread.sem, spread.up())

                @block.vector
                def _(dve):
                    def step(ins):
                        ins.then_inc(inner.sem, inner.up())
                        dve.wait_ge(inner.sem, inner.n)
                    dve.wait_ge(logits_ready.sem, logits_ready.at(1))
                    step(nc.vector.tensor_copy(logits, psum[:, 0, 0:TT * NE].rearrange("p (t n) -> p t n", t=TT)))
                    for t in range(TT):
                        step(nc.vector.max(top[:, t, :], logits[:, t, :]))
                        step(nc.vector.max_index(idx[:, t, :], top[:, t, :], logits[:, t, :]))
                    step(nc.vector.tensor_copy(index, idx))
                    dve.wait_ge(numbers_built.sem, numbers_built.at(NE))
                    for dst, i in ((comb, 0), (part, 1)):
                        step(nc.vector.tensor_tensor(dst, numbers, index[:, :, i:i + 1].to_broadcast([P, TT, NE]),
                                                     ALU.is_equal))
                    nc.vector.tensor_tensor(chosen, comb, part, ALU.add).then_inc(chosen_ready.sem, chosen_ready.up())
                    nc.vector.tensor_tensor(share[:, 1, :], top[:, :, 1], top[:, :, 0], ALU.subtract)\
                        .then_inc(lead.sem, lead.up())
                    dve.wait_ge(lead_exp.sem, lead_exp.at(1))
                    step(nc.vector.tensor_scalar(share[:, 0, :], share[:, 1, :], 1.0, None, ALU.add))
                    step(nc.vector.reciprocal(share[:, 0, :], share[:, 0, :]))
                    step(nc.vector.tensor_tensor(share[:, 1, :], share[:, 1, :], share[:, 0, :], ALU.mult))
                    dve.wait_ge(chosen_ready.sem, chosen_ready.at(1))
                    for dst, i in ((comb, 0), (part, 1)):
                        step(nc.vector.tensor_tensor(dst, dst, share[:, i, :].unsqueeze(2).to_broadcast([P, TT, NE]),
                                                     ALU.mult))
                    step(nc.vector.tensor_tensor(comb, comb, part, ALU.add))
                    dve.wait_ge(ranks.sem, ranks.at(1))
                    step(nc.vector.tensor_tensor(places.rearrange("p e t -> p t e"),
                                                 psum[:, 0, 0:TT * NE].rearrange("p (t n) -> p t n", t=TT),
                                                 chosen, ALU.mult))
                    step(nc.vector.tensor_copy(total, psum[:, 0, TT * NE:(TT + 1) * NE]))
                    for t in range(TT):
                        step(nc.vector.tensor_scalar(counting[:, t * P:(t + 1) * P], psum[:, 0, 512:512 + P],
                                                     float(t * P), None, ALU.add))
                        step(nc.vector.tensor_scalar(slot_number[:, t:t + 1], psum[:, 0, 512 + P:512 + P + 1],
                                                     float(t * P), None, ALU.add))
                    step(nc.vector.tensor_scalar(blocks, total, float(P), 1.0, ALU.is_gt, ALU.add))
                    for b in range(2, TT):
                        step(nc.vector.tensor_scalar(more, total, float(b * P), None, ALU.is_gt))
                        step(nc.vector.tensor_tensor(blocks, blocks, more, ALU.add))
                    nc.vector.tensor_copy(blocks_used, blocks).then_inc(ranks_read.sem, ranks_read.up())

                @block.scalar
                def _(act):
                    for t in range(TT):
                        act.wait_ge(turned.sem, turned.at(t + 1))
                        nc.scalar.activation(h_rows[:, t, :], psum[:, 1 + t % 3, :], ACT.Copy)\
                            .then_inc(turned_read.sem, turned_read.up())
                    act.wait_ge(lead.sem, lead.at(1))
                    nc.scalar.activation(share[:, 1, :], share[:, 1, :], ACT.Exp).then_inc(lead_exp.sem, lead_exp.up())
                    for i in range(2 * NE):
                        act.wait_ge(spread.sem, spread.at(i + 1))
                        dst = (weight_rows, place_rows)[i % 2][:, i // 2, :]
                        nc.scalar.activation(dst, psum[:, i % 4, 0:T], ACT.Copy)\
                            .then_inc(spread_read.sem, spread_read.up())

        def feed_forward(l):
            base, count = parts["ffn", l]
            experts = count // PER_EXPERT
            moe = l % 2 == 1
            slot_free = sem("ffn_slot_free", l)
            gates, hid, added, scaled = (sem(f"ffn_{n}_{l}") for n in ("gates", "hidden", "added", "scaled"))
            with nc.Block() as block:
                @block.sync
                def _(sp):
                    def turn(e, last):
                        for i in range(RING, PER_EXPERT + RING):
                            n = base + i
                            if i >= PER_EXPERT and last:
                                if base + count + i - PER_EXPERT < len(flat):
                                    load_block(sp, base + count + i - PER_EXPERT)
                                continue
                            src, k = expert_block(l, e + (1 if i >= PER_EXPERT else 0), i % PER_EXPERT)
                            sp.wait_ge(ring_used.sem, e * PER_EXPERT + (n - RING + 1))
                            sp.sem_inc(slot_free.sem, 1)
                            sp.dma_start(ring_view(n % RING, k), src).then_inc(ring_loaded[n % RING].sem, 16)
                    with sp.Fori(0, experts - 1) as e:
                        turn(e, False)
                    turn(experts - 1, True)

                @block.tensor
                def _(pe):
                    with pe.Fori(0, experts) as e:
                        for i in range(2 * FT):
                            n = base + i
                            pe.wait_ge(ring_loaded[n % RING].sem, (e * (PER_EXPERT // RING) + (n // RING + 1)) * 16)
                            if i >= 4:
                                pe.wait_ge(hid.sem, e * FT + ((i - 4) // 2 + 1))
                            w = ring_view(n % RING, KD)
                            for k in range(KD):
                                for c0, c1 in SHORT:
                                    ins = nc.tensor.matmul(psum[:, i % 4, c0:c1], w[:, k, :], h[:, k, c0:c1],
                                                           start=(k == 0), stop=(k == KD - 1))
                            ins.then_inc(ring_used.sem, 1)
                        for m in range(KD):
                            n = base + 2 * FT + m
                            pe.wait_ge(ring_loaded[n % RING].sem, (e * (PER_EXPERT // RING) + (n // RING + 1)) * 16)
                            if m == 0:
                                pe.wait_ge(hid.sem, e * FT + FT)
                            if m >= 4:
                                pe.wait_ge(scaled.sem, e * KD + m - 3)
                            w = ring_view(n % RING, FT)
                            for k in range(FT):
                                for c0, c1 in SHORT:
                                    ins = nc.tensor.matmul(psum[:, m % 4, c0:c1], w[:, k, :], hidden[k][:, c0:c1],
                                                           start=(k == 0), stop=(k == FT - 1))
                            ins.then_inc(ring_used.sem, 1)
                        pe.wait_ge(scaled.sem, e * KD + KD)

                @block.scalar
                def _(act):
                    with act.Fori(0, experts) as e:
                        for f in range(FT):
                            act.wait_ge(ring_used.sem, e * PER_EXPERT + (base + 2 * f + 1))
                            if f >= 2:
                                act.wait_ge(hid.sem, e * FT + (f - 1))
                            nc.scalar.activation(tmp[:, f % 2, :], psum[:, (2 * f) % 4, 0:T], ACT.Silu).then_inc(gates.sem, 1)

                @block.vector
                def _(dve):
                    nc.vector.memset(u[:, FT:FT + KD, :], 0.0).then_inc(vector_inner.sem, 1)
                    vector_inner.n += 1
                    dve.wait_ge(vector_inner.sem, vector_inner.n)
                    with dve.Fori(0, experts) as e:
                        for f in range(FT):
                            dve.wait_ge(gates.sem, e * FT + f + 1)
                            dve.wait_ge(ring_used.sem, e * PER_EXPERT + (base + 2 * f + 2))
                            nc.vector.tensor_tensor(hidden[f], tmp[:, f % 2, :], psum[:, (2 * f + 1) % 4, 0:T],
                                                    ALU.mult).then_inc(hid.sem, 1)
                        for m in range(KD):
                            dve.wait_ge(ring_used.sem, e * PER_EXPERT + (base + 2 * FT + m + 1))
                            if moe:
                                if m >= 2:
                                    dve.wait_ge(added.sem, e * KD + (m - 1))
                                nc.vector.tensor_tensor(tmp[:, 2 + m % 2, :], psum[:, m % 4, 0:T],
                                                        weight_rows[:, bass.ds(e, 1), :].rearrange("p a t -> p (a t)"),
                                                        ALU.mult).then_inc(scaled.sem, 1)
                            else:
                                nc.vector.tensor_tensor(sums[m], sums[m], psum[:, m % 4, 0:T], ALU.add)\
                                    .then_inc(scaled.sem, 1)
                        if moe:
                            dve.wait_ge(added.sem, e * KD + KD)
                        else:
                            dve.wait_ge(scaled.sem, e * KD + KD)

                if moe:
                    @block.gpsimd
                    def _(pool):
                        pool.wait_ge(vector_inner.sem, vector_inner.n)
                        with pool.Fori(0, experts) as e:
                            for m in range(KD):
                                pool.wait_ge(scaled.sem, e * KD + m + 1)
                                nc.gpsimd.tensor_tensor(sums[m], sums[m], tmp[:, 2 + m % 2, :], ALU.add)\
                                    .then_inc(added.sem, 1)
                            pool.wait_ge(added.sem, e * KD + KD)

        def mixture(l):
            base, count = parts["ffn", l]
            slot_taken = [sem(f"moe_slot_taken_by_{q}", l) for q in ("sync", "scalar")]
            gathered = sem("moe_gathered", l)
            tokens_in = [sem(f"moe_tokens_in_by_{e}", l) for e in ("scalar", "vector")]
            pick_ready = sem("moe_pick_ready", l)
            place_ready = sem("moe_place_ready", l)
            gates = sem("moe_gates", l)
            hid = sem("moe_hidden", l)
            outputs_in = [sem(f"moe_outputs_in_by_{e}", l) for e in ("scalar", "vector")]
            turned = sem("moe_outputs_turned", l)
            rows_in = [sem(f"moe_rows_in_by_{e}", l) for e in ("scalar", "vector")]
            spread = sem("moe_spread", l)
            added = sem("moe_added", l)
            x_scaled = sem("moe_x_scaled", l)
            HALF = KD // 2

            def pieces(width):
                return [(c0, min(c1, width)) for c0, c1 in SHORT if c0 < width]

            with nc.Block() as block:
                def load(eng, e, i, last):
                    n = base + i
                    if i + RING < PER_EXPERT or not last:
                        src, k = expert_block(l, e + (i + RING) // PER_EXPERT, (i + RING) % PER_EXPERT)
                        eng.dma_start(ring_view(n % RING, k), src).then_inc(ring_loaded[n % RING].sem, 16)

                @block.sync
                def _(sp):
                    def turn(e, last):
                        for i in range(0, PER_EXPERT, 2):
                            sp.wait_ge(ring_used.sem, e * PER_EXPERT + (base + i + 1))
                            sp.sem_inc(slot_taken[0].sem, 1)
                            load(sp, e, i, last)
                    with sp.Fori(0, NE - 1) as e:
                        turn(e, False)
                    turn(NE - 1, True)

                @block.tensor
                def _(pe):
                    def turn(e, width):
                        blocks = width // P
                        pe.wait_ge(pick_ready.sem, e + 1)
                        for m in range(KD):
                            if m >= 4:
                                pe.wait_ge(tokens_in[m % 2].sem, e * HALF + ((m - 4) // 2 + 1))
                            for t in range(TT):
                                for c0, c1 in pieces(width):
                                    ins = nc.tensor.matmul(psum[:, m % 4, c0:c1], h_rows[:, t, m * P:(m + 1) * P],
                                                           onehot[:, t, c0:c1], start=(t == 0), stop=(t == TT - 1))
                            ins.then_inc(gathered.sem, 1)
                        pe.wait_ge(tokens_in[0].sem, e * HALF + HALF)
                        pe.wait_ge(tokens_in[1].sem, e * HALF + HALF)
                        for i in range(2 * FT):
                            n = base + i
                            pe.wait_ge(ring_loaded[n % RING].sem, (e * (PER_EXPERT // RING) + (n // RING + 1)) * 16)
                            if i >= 4:
                                pe.wait_ge(hid.sem, e * FT + ((i - 4) // 2 + 1))
                            w = ring_view(n % RING, KD)
                            for k in range(KD):
                                for c0, c1 in pieces(width):
                                    ins = nc.tensor.matmul(psum[:, i % 4, c0:c1], w[:, k, :], h[:, k, c0:c1],
                                                           start=(k == 0), stop=(k == KD - 1))
                            ins.then_inc(ring_used.sem, 1)
                        for m in range(KD):
                            n = base + 2 * FT + m
                            pe.wait_ge(ring_loaded[n % RING].sem, (e * (PER_EXPERT // RING) + (n // RING + 1)) * 16)
                            if m == 0:
                                pe.wait_ge(hid.sem, e * FT + FT)
                            if m >= 4:
                                pe.wait_ge(outputs_in[m % 2].sem, e * HALF + ((m - 4) // 2 + 1))
                            w = ring_view(n % RING, FT)
                            for k in range(FT):
                                for c0, c1 in pieces(width):
                                    ins = nc.tensor.matmul(psum[:, m % 4, c0:c1], w[:, k, :], hidden[k][:, c0:c1],
                                                           start=(k == 0), stop=(k == FT - 1))
                            ins.then_inc(ring_used.sem, 1)
                        pe.wait_ge(outputs_in[0].sem, e * HALF + HALF)
                        pe.wait_ge(outputs_in[1].sem, e * HALF + HALF)
                        for m in range(KD):
                            if m >= 4:
                                pe.wait_ge(rows_in[m % 2].sem, e * HALF + ((m - 4) // 2 + 1))
                            for b in range(blocks):
                                ins = nc.tensor.transpose(psum[:, m % 4, b * P:(b + 1) * P], h[:, m, b * P:(b + 1) * P],
                                                          ident[:])
                            ins.then_inc(turned.sem, 1)
                        pe.wait_ge(rows_in[0].sem, e * HALF + HALF)
                        pe.wait_ge(rows_in[1].sem, e * HALF + HALF)
                        pe.wait_ge(place_ready.sem, e * TT + TT)
                        for m in range(KD):
                            if m >= 4:
                                pe.wait_ge(added.sem, e * KD + (m - 3))
                            for b in range(blocks):
                                for c0, c1 in SHORT:
                                    ins = nc.tensor.matmul(psum[:, m % 4, c0:c1], y_rows[:, b, m * P:(m + 1) * P],
                                                           onehot[:, b, c0:c1], start=(b == 0), stop=(b == blocks - 1))
                            ins.then_inc(spread.sem, 1)
                        pe.wait_ge(added.sem, e * KD + KD)

                    with pe.Fori(0, NE) as e:
                        used = pe.value_load(blocks_used[0:1, bass.ds(e, 1)], min_val=1, max_val=TT)
                        for b in range(1, TT + 1):
                            with pe.If(used == b):
                                turn(e, b * P)

                @block.scalar
                def _(act):
                    for k in range(KD):
                        nc.scalar.mul(x[:, k, :], x[:, k, :], ALPHA).then_inc(x_scaled.sem, x_scaled.up())

                    def turn(e, last):
                        for m in range(0, KD, 2):
                            act.wait_ge(gathered.sem, e * KD + (m + 1))
                            nc.scalar.activation(h[:, m, :], psum[:, m % 4, 0:T], ACT.Copy).then_inc(tokens_in[0].sem, 1)
                        for f in range(FT):
                            act.wait_ge(ring_used.sem, e * PER_EXPERT + (base + 2 * f + 1))
                            if f >= 2:
                                act.wait_ge(hid.sem, e * FT + (f - 1))
                            nc.scalar.activation(tmp[:, f % 2, :], psum[:, (2 * f) % 4, 0:T], ACT.Silu)\
                                .then_inc(gates.sem, 1)
                            if f >= 1:
                                load(act, e, 2 * f - 1, last)
                        for m in range(0, KD, 2):
                            act.wait_ge(ring_used.sem, e * PER_EXPERT + (base + 2 * FT + m + 1))
                            nc.scalar.activation(h[:, m, :], psum[:, m % 4, 0:T], ACT.Copy).then_inc(outputs_in[0].sem, 1)
                            load(act, e, 2 * FT + m - 1, last)
                        act.wait_ge(ring_used.sem, e * PER_EXPERT + (base + PER_EXPERT))
                        act.sem_inc(slot_taken[1].sem, 1)
                        load(act, e, PER_EXPERT - 1, last)
                        for m in range(0, KD, 2):
                            act.wait_ge(turned.sem, e * KD + (m + 1))
                            nc.scalar.activation(y_rows[:, :, m * P:(m + 1) * P],
                                                 psum[:, m % 4, 0:T].rearrange("p (b f) -> p b f", b=TT),
                                                 ACT.Copy).then_inc(rows_in[0].sem, 1)

                    with act.Fori(0, NE - 1) as e:
                        turn(e, False)
                    turn(NE - 1, True)

                @block.vector
                def _(dve):
                    dve.wait_ge(x_scaled.sem, x_scaled.at(KD))
                    with dve.Fori(0, NE) as e:
                        nc.vector.tensor_tensor(onehot, counting.unsqueeze(1).to_broadcast([P, TT, T]),
                                                places[:, bass.ds(e, 1), :].rearrange("p a t -> p (a t)")
                                                .unsqueeze(2).to_broadcast([P, TT, T]),
                                                ALU.is_equal).then_inc(pick_ready.sem, 1)
                        for m in range(1, KD, 2):
                            dve.wait_ge(gathered.sem, e * KD + (m + 1))
                            nc.vector.tensor_copy(h[:, m, :], psum[:, m % 4, 0:T]).then_inc(tokens_in[1].sem, 1)
                        for b in range(TT):
                            nc.vector.scalar_tensor_tensor(
                                out=onehot[:, b, :], in0=place_rows[:, bass.ds(e, 1), :].rearrange("p a t -> p (a t)"),
                                scalar=slot_number[:, b:b + 1],
                                in1=weight_rows[:, bass.ds(e, 1), :].rearrange("p a t -> p (a t)"),
                                op0=ALU.is_equal, op1=ALU.mult).then_inc(place_ready.sem, 1)
                        for f in range(FT):
                            dve.wait_ge(gates.sem, e * FT + f + 1)
                            dve.wait_ge(ring_used.sem, e * PER_EXPERT + (base + 2 * f + 2))
                            nc.vector.tensor_tensor(hidden[f], tmp[:, f % 2, :], psum[:, (2 * f + 1) % 4, 0:T],
                                                    ALU.mult).then_inc(hid.sem, 1)
                        for m in range(1, KD, 2):
                            dve.wait_ge(ring_used.sem, e * PER_EXPERT + (base + 2 * FT + m + 1))
                            nc.vector.tensor_copy(h[:, m, :], psum[:, m % 4, 0:T]).then_inc(outputs_in[1].sem, 1)
                        for m in range(1, KD, 2):
                            dve.wait_ge(turned.sem, e * KD + (m + 1))
                            nc.vector.tensor_copy(y_rows[:, :, m * P:(m + 1) * P],
                                                  psum[:, m % 4, 0:T].rearrange("p (b f) -> p b f", b=TT))\
                                .then_inc(rows_in[1].sem, 1)
                        for m in range(KD):
                            dve.wait_ge(spread.sem, e * KD + (m + 1))
                            for s, (t0, t1) in enumerate(SEQS):
                                ins = nc.vector.scalar_tensor_tensor(
                                    out=x[:, m, t0:t1], in0=psum[:, m % 4, t0:t1], scalar=mod[:, 5 * KD + m, s:s + 1],
                                    in1=x[:, m, t0:t1], op0=ALU.mult, op1=ALU.add)
                            ins.then_inc(added.sem, 1)
                        dve.wait_ge(added.sem, e * KD + KD)

        def residual(l):
            vector_done, scalar_done = sem("res_vector", l), sem("res_scalar", l)
            with nc.Block() as block:
                @block.scalar
                def _(act):
                    for k in range(KD):
                        nc.scalar.mul(x[:, k, :], x[:, k, :], ALPHA).then_inc(scalar_done.sem, scalar_done.up())

                @block.vector
                def _(dve):
                    for m in range(KD):
                        dve.wait_ge(scalar_done.sem, scalar_done.at(m + 1))
                        for s, (t0, t1) in enumerate(SEQS):
                            nc.vector.scalar_tensor_tensor(out=x[:, m, t0:t1], in0=sums[m][:, t0:t1],
                                                                scalar=mod[:, 5 * KD + m, s:s + 1], in1=x[:, m, t0:t1],
                                                                op0=ALU.mult, op1=ALU.add).then_inc(vector_done.sem, vector_done.up())

        def finish():
            turned, copied, stored = sem("end_turned"), sem("end_copied"), sem("end_stored")
            rows = [u[:, 2 * t:2 * t + 2, :].rearrange("p s w -> p (s w)")[:, 0:D] for t in range(TT)]
            with nc.Block() as block:
                @block.tensor
                def _(pe):
                    for t in range(TT):
                        if t >= 4:
                            pe.wait_ge(copied.sem, copied.at(t - 3))
                        for k in range(KD):
                            ins = nc.tensor.transpose(psum[:, t % 4, k * P:(k + 1) * P], x[:, k, t * P:(t + 1) * P], ident[:])
                        ins.then_inc(turned.sem, turned.up())

                @block.vector
                def _(dve):
                    for t in range(TT):
                        dve.wait_ge(turned.sem, turned.at(t + 1))
                        nc.vector.tensor_copy(rows[t], psum[:, t % 4, :]).then_inc(copied.sem, copied.up())

                @block.sync
                def _(sp):
                    for t in range(TT):
                        sp.wait_ge(copied.sem, copied.at(t + 1))
                        dst = out["yp"][0] if t == 0 else out["ys"][0, (t - 1) * P:t * P, :]
                        sp.dma_start(dst, rows[t]).then_inc(stored.sem, stored.up(16))
                    sp.wait_ge(stored.sem, stored.at(16 * TT))

        start()
        for l in range(DEPTH):
            modulation(l)
            modulate(0)
            project_in(l)
            conformer(l)
            gla(l)
            gdn(l)
            project_out(l)
            close(l, "ln1", 0, at_a["ln1_g"], at_a["ln1_b"])
            modulate(3)
            if l % 2 == 1:
                route(l)
                mixture(l)
            else:
                feed_forward(l)
                residual(l)
            ring_used.n = sum(parts["ffn", l])
            close(l, "ln2", 0, at_a["ln2_g"], at_a["ln2_b"])
        finish()


_INS = ["x_prompt", "x_sample", "c", "state_gla", "state_gdn", "c_ctx", "w_ada", "b_ada", "w_in", "w_out", "conv_w",
        "conv_b", "conv_ln_g", "conv_ln_b", "conv_pw", "gla_w_lr", "gla_b_lr", "gla_norm_g", "gdn_conv_w",
        "gdn_a_log", "gdn_dt_bias", "gdn_norm_g", "sc_conv_w", "ln1_g", "ln1_b", "ln2_g", "ln2_b", "ffn_w_gate",
        "ffn_w_up", "ffn_w_down", "moe_router", "moe_w_gate", "moe_w_up", "moe_w_down"]


def kernel(**inputs):
    import numpy as _np
    import concourse.bacc as _bacc
    from concourse import mybir as _mybir
    from concourse.bass_utils import run_bass_kernel_spmd as _run

    nc = _bacc.Bacc("TRN2", target_bir_lowering=False, num_devices=1)
    arrays, args = {}, {}
    for name in _INS:
        v = _np.ascontiguousarray(inputs[name])
        arrays[f"in_{name}_dram"] = v
        args[name] = nc.dram_tensor(f"in_{name}_dram", v.shape, _mybir.dt.from_np(v.dtype), kind="ExternalInput").ap()
    sp, ss = inputs["x_prompt"].shape, inputs["x_sample"].shape
    outs = {"yp": sp, "ys": ss, "gla": inputs["state_gla"].shape, "gdn": inputs["state_gdn"].shape}
    handles = {n: nc.dram_tensor(f"out_{n}_dram", tuple(s), F32, kind="ExternalOutput").ap() for n, s in outs.items()}
    trunk_kernel(nc, args, handles)
    r = _run(nc, [arrays], core_ids=[0])
    return tuple(r.results[0][f"out_{n}_dram"] for n in ("yp", "ys", "gla", "gdn"))
```

```python
from contextlib import ExitStack

import concourse.bass as bass
from concourse import mybir

F32 = mybir.dt.float32
BF16 = mybir.dt.bfloat16
F32R = mybir.dt.float32r
I32 = mybir.dt.int32
U32 = mybir.dt.uint32
ALU = mybir.AluOpType
ACT = mybir.ActivationFunctionType
AX = mybir.AxisListType

P = 128


class Signal:

    def __init__(self, sem):
        self.sem = sem
        self.n = 0
        self.base = 0

    def up(self, k=1):
        self.n += k
        return k

    def at(self, value):
        return self.base + value


def trunk_kernel(nc, a, out):
    DEPTH, D, N_IN = a["w_in"].shape
    CTX = a["x_prompt"].shape[1]
    LAT = a["x_sample"].shape[1]
    T = CTX + LAT
    TT = T // P
    KD = D // P
    GRID_W = 64
    ROWS = LAT // GRID_W
    CONV_K, GW = a["conv_w"].shape[1:]
    J = GW // P
    H = a["state_gla"].shape[3]
    DK = a["state_gla"].shape[4]
    LR = a["gla_w_lr"].shape[2]
    GLA_TAU = 16.0
    CHUNK = 64
    NCH = T // CHUNK
    NE = a["moe_w_gate"].shape[1]
    FE = a["moe_w_gate"].shape[3]
    FT = FE // P
    DENSE = a["ffn_w_gate"].shape[2] // FE
    ALPHA = (2 * DEPTH) ** 0.25
    EPS = 1e-5
    QSCALE = DK ** -0.5
    SEQS = ((0, CTX), (CTX, T))
    SHORT = ((0, 512), (512, T))
    assert D == 1024 and J == 2 and H == 4 and DK == 64 and CTX == P and T == 640 and FE == 11 * P

    UW = T + 4
    names = ["aval", "agate", "gq", "gk", "gv", "gg", "lr", "dq", "dk", "dv", "dgate", "bd", "sb", "sc", "sx"]
    widths = {n: GW for n in names} | {"lr": 2 * LR, "bd": 3 * H}
    in_tiles, slot, col = [], {}, 0
    for n in names:
        slot[n] = len(in_tiles)
        for c in range(0, widths[n], P):
            in_tiles.append((n, len(in_tiles), col + c, min(P, widths[n] - c)))
        col += widths[n]
    assert col == N_IN
    PADDED = ("dq", "dk", "dv", "sx")
    PERMUTED = ("dq", "dk", "dv")
    U = len(in_tiles)
    FIRST = ("aval", "agate", "lr", "gq", "gk", "sb", "sc", "sx", "dq", "dk", "dv", "gv", "gg", "dgate", "bd")
    in_tiles.sort(key=lambda tile: FIRST.index(tile[0]))
    narrow_at = {tile[0]: tile[2] for tile in in_tiles if tile[0] in ("lr", "bd")}
    in_tiles = [tile for tile in in_tiles if tile[0] not in narrow_at]
    NARROW = {"lr": (0, 2 * LR), "bd": (2 * LR, 2 * LR + 3 * H)}
    assert 2 * LR == 32

    rows_a = [("b_ada", 6 * KD), ("ln1_g", KD), ("ln1_b", KD), ("ln2_g", KD), ("ln2_b", KD), ("conv_b", J),
              ("conv_ln_g", J), ("conv_ln_b", J), ("gla_norm_g", J), ("gdn_norm_g", J), ("gla_b_lr", 2 * J),
              ("sc_conv_w", 3 * J), ("gdn_conv_w", 9 * J)]
    rows_b = [("conv_w", CONV_K * J), ("c", KD), ("c_ctx", KD)]

    def offsets(rows):
        at, o = {}, 0
        for n, k in rows:
            at[n] = o
            o += k
        assert o <= P
        return at, o
    at_a, n_a = offsets(rows_a)
    at_b, n_b = offsets(rows_b)

    RING = 6
    RW = FT * P
    PER_EXPERT = 2 * FT + KD
    assert PER_EXPERT % RING == 0

    ctx = ExitStack()
    with ctx:
        def sb(name, shape, dt=F32):
            return ctx.enter_context(nc.sbuf_tensor(name, shape, dt))

        signals = {}

        def sem(name, l=None):
            if l is None or name not in signals:
                signals[name] = Signal(ctx.enter_context(nc.semaphore(name)))
            signals[name].base = signals[name].n
            return signals[name]

        x = sb("x", [P, KD, T])
        ring = sb("ring", [P, RING, RW])
        chunk_decay = sb("chunk_decay", [P, 2 * J * (T // CHUNK)])
        x_sum = sb("x_sum", [P, T])
        mod = sb("mod", [P, 6 * KD, 2])
        cond = sb("cond", [P, KD, 2])
        pa = sb("pa", [P, DEPTH, P])
        pb = sb("pb", [P, DEPTH, P])
        ident = sb("ident", [P, P])
        mean_d = sb("mean_d", [P, P])
        mean_g = sb("mean_g", [P, P])
        head_sum = sb("head_sum", [P, P])
        until = sb("until", [P, 2, P])
        chunk_until = sb("chunk_until", [P, 2, P], BF16)
        level = sb("level", [P, 7, 2, P], BF16)
        level0t = sb("level0t", [P, 2, P], BF16)
        w_lr = sb("w_lr", [2 * LR, 2 * GW])
        pw = sb("pw", [P, J, GW])
        w_narrow = sb("w_narrow", [P, KD, 2 * LR + 3 * H])
        router = sb("router", [P, KD, NE])
        dtb = sb("dtb", [P, 2 * H])
        nega = sb("nega", [P, 2 * H])
        eps_col = sb("eps_col", [P, 2])
        resets = sb("resets", [P, 2, T])
        psum = ctx.enter_context(nc.psum_tensor("psum", [P, 4, 1024], F32))

        def bank(n):
            return psum[:, n // 2, (n % 2) * 512:(n % 2) * 512 + 512]

        ctx.enter_context(nc.allow_non_contiguous_dma(reason="small loads"))

        PADC = CONV_K // 2
        CW = T + PADC
        WW = 688
        STEP = P // 4
        FEW = 2 * P
        assert TT * D <= FT * UW and 2 * T + TT * T + 64 <= 4 * T + 4 * WW and FT + 2 * NE + 1 <= U and TT * FEW <= 2 * T
        lower, upper = ctx.enter_context(ExitStack()), ctx.enter_context(ExitStack())
        h = mix = h_rows = u = work = tmp = wide = x_rows = conv_in = conv = hidden = None
        weight_rows = place_rows = counting = onehot = onehot_few = places = slot_number = steps_used = y_rows = None

        def place_lower(tag):
            nonlocal h, mix, h_rows, x_rows
            h = lower.enter_context(nc.sbuf_tensor(f"h_{tag}", [P, KD, T], F32))
            mix = lower.enter_context(nc.sbuf_tensor(f"mix_{tag}", [P, KD, T], F32))
            x_rows = [h[:].rearrange("p k t -> p (k t)")[:, t * D:(t + 1) * D] for t in range(TT)]
            h_rows = mix[:].rearrange("p k t -> p (k t)").rearrange("p (t f) -> p t f", t=TT)

        def place_upper(tag):
            nonlocal u, work, tmp, wide, conv_in, conv, hidden
            nonlocal weight_rows, place_rows, counting, onehot, onehot_few, places, slot_number, steps_used, y_rows
            u = upper.enter_context(nc.sbuf_tensor(f"u_{tag}", [P, U, UW], F32))
            work = upper.enter_context(nc.sbuf_tensor(f"work_{tag}", [P, 4 * T + 4 * WW], F32))
            tmp = work[:, 0:4 * T].rearrange("p (a t) -> p a t", a=4)
            wide = work[:, 4 * T:4 * T + 4 * WW].rearrange("p (a t) -> p a t", a=4)
            conv_in, conv = wide[:, 0:J, :], wide[:, J:2 * J, :]
            hidden = [u[:, f, 0:T] for f in range(FT)]
            weight_rows = u[:, FT:FT + NE, 0:T]
            place_rows = u[:, FT + NE:FT + 2 * NE, 0:T]
            counting = u[:, FT + 2 * NE, 0:T]
            onehot = work[:, 2 * T:2 * T + TT * T].rearrange("p (t n) -> p t n", t=TT)
            rest = work[:, 2 * T + TT * T:4 * T + 4 * WW]
            onehot_few = work[:, 0:TT * FEW].rearrange("p (t n) -> p t n", t=TT)
            places = rest[:, 0:TT * (NE + 1)].rearrange("p (e t) -> p e t", t=TT)
            slot_number = rest[:, 48:48 + TT]
            steps_used = rest[:, 56:56 + NE].bitcast(I32)
            y_rows = u[:].rearrange("p s w -> p (s w)")[:, 0:TT * D].rearrange("p (b f) -> p b f", b=TT)

        place_lower("first")
        place_upper("first")

        ring_loaded = [sem(f"ring_loaded{s}") for s in range(RING)]
        ring_used = sem("ring_used")

        def column_block(w, c, n=P):
            return w[:, c:c + n].rearrange("(k p) n -> p k n", p=P)

        def ring_view(s, k, n=P):
            return ring[:, s, 0:k * n].rearrange("p (k n) -> p k n", n=n)

        stream = []
        parts = {}
        for l in range(DEPTH):
            blocks = [(a["w_ada"][l], m * P, P, KD) for m in range(6 * KD)]
            parts["ada", l] = (sum(map(len, stream)), len(blocks))
            stream.append(blocks)
            blocks = [(a["w_in"][l], c, n, KD) for _, _, c, n in in_tiles]
            parts["in", l] = (sum(map(len, stream)), len(blocks))
            stream.append(blocks)
            blocks = [(a["w_out"][l], m * P, P, KD) for m in range(KD)]
            parts["out", l] = (sum(map(len, stream)), len(blocks))
            stream.append(blocks)
            count = (DENSE if l % 2 == 0 else NE) * PER_EXPERT
            parts["ffn", l] = (sum(map(len, stream)), count)
            stream.append([None] * count)
        flat = [b for part in stream for b in part]

        def expert_block(l, e, i):
            if l % 2 == 0:
                wg, wu, wd = a["ffn_w_gate"][l // 2], a["ffn_w_up"][l // 2], a["ffn_w_down"][l // 2]
                if i < 2 * FT:
                    w = (wg, wu)[i % 2]
                    cols = w[:, bass.ds(e * FE + (i // 2) * P, P)]
                    return cols.rearrange("(k p) n -> p k n", p=P), KD
                rows = wd[bass.ds(e * FE, FE), (i - 2 * FT) * P:(i - 2 * FT + 1) * P]
                return rows.rearrange("(k p) n -> p k n", p=P), FT
            wg, wu, wd = a["moe_w_gate"][l // 2], a["moe_w_up"][l // 2], a["moe_w_down"][l // 2]
            if i < 2 * FT:
                w = (wg, wu)[i % 2]
                c = (i // 2) * P
                return w[bass.ds(e, 1), :, c:c + P].rearrange("a (k p) n -> p (a k) n", p=P), KD
            c = (i - 2 * FT) * P
            return wd[bass.ds(e, 1), :, c:c + P].rearrange("a (k p) n -> p (a k) n", p=P), FT

        def load_block(eng, n):
            if n >= RING:
                eng.wait_ge(ring_used.sem, ring_used.at(n - RING + 1))
            s = n % RING
            if flat[n] is None:
                l = next(l for l in range(DEPTH) if parts["ffn", l][0] <= n < sum(parts["ffn", l]))
                i = n - parts["ffn", l][0]
                src, k = expert_block(l, i // PER_EXPERT, i % PER_EXPERT)
                dst = ring_view(s, k)
            else:
                w, c, m, k = flat[n]
                src, dst = column_block(w, c, m), ring_view(s, k, m)
            eng.dma_start(dst, src).then_inc(ring_loaded[s].sem, 16)

        def load_ahead(eng, part, turn=0, queues=1):
            base, count = parts[part]
            for n in range(base + RING, base + count + RING):
                if n < len(flat) and n % queues == turn:
                    load_block(eng, n)

        def block_landed(eng, n):
            eng.wait_ge(ring_loaded[n % RING].sem, ring_loaded[n % RING].at(16 * (n // RING + 1)))

        x_in = sem("x_loaded")

        def constants(pool):
            consts = sem("masks_built")
            def built(ins):
                ins.then_inc(consts.sem, consts.up())
                pool.wait_ge(consts.sem, consts.n)

            def keep(v, pattern, base, mult):
                built(nc.gpsimd.affine_select(out=v, in_=v, compare_op=ALU.is_ge, fill=0.0, base=base,
                                              pattern=pattern, channel_multiplier=mult))
            for v, value in ((mean_d, 1.0 / D), (mean_g, 1.0 / GW), (head_sum, 1.0),
                             (until, 1.0), (level, 1.0), (level0t, 1.0), (resets, 1.0)):
                built(nc.gpsimd.memset(v[:], value))
            for t in range(0, T, CHUNK):
                built(nc.gpsimd.memset(resets[:, 0, t:t + 1], 0.0))
                built(nc.gpsimd.memset(resets[:, 1, t + CHUNK - 1:t + CHUNK], 0.0))
            def same_block(v, size, dims):
                n = P // size
                v = v.rearrange("p (g c) -> p g c", c=size)
                keep(v, [[-size, n], [0, size]], 0, 1)
                keep(v, [[size, n], [0, size]], size - 1, -1)
            same_block(head_sum[:], DK, 0)
            for z, sign in ((0, 1), (1, -1)):
                keep(until[:, z, :], [[sign, P]], 0, -sign)
                built(nc.gpsimd.tensor_copy(chunk_until[:, z, :], until[:, z, :]))
                same_block(chunk_until[:, z, :], CHUNK, 0)
                for b in range(7):
                    v = level[:, b, z, :]
                    size = 2 << b
                    if size < P:
                        same_block(v, size, 0)
                    w = v.rearrange("p (g i c) -> p g i c", i=2, c=size // 2)
                    own, other = w[:, :, z, :], w[:, :, 1 - z, :]
                    built(nc.gpsimd.memset(own, 0.0))
                    n = P // size
                    if z == 0:
                        keep(other, [[size, n], [0, size // 2]], size // 2 - 1, -1)
                    else:
                        keep(other, [[-size, n], [0, size // 2]], -(size // 2), 1)
                built(nc.gpsimd.tensor_copy(level0t[:, 1 - z, :], level[:, 0, z, :]))

        def start():
            stage_in, stage_in_odd = sem("stage_loaded"), sem("stage_of_odd_layers_loaded")
            consts = sem("consts_built")
            turned = sem("start_turned")
            copied = sem("start_copied")
            stage = wide[:, :, 0:P]

            def parameter_rows(l):
                for rows, at, half in ((rows_a, at_a, 0), (rows_b, at_b, 1)):
                    for n, count in rows:
                        if n == "c":
                            src = a["c"].rearrange("b (k p) -> (b k) p", p=P)
                        elif n == "c_ctx":
                            src = a["c_ctx"].rearrange("(k p) -> k p", p=P)
                        else:
                            w = a[n][l]
                            if len(w.shape) == 2:
                                w = w.rearrange("a b -> (a b)")
                            src = w.rearrange("(k p) -> k p", p=P)
                        yield stage[at[n]:at[n] + count, 2 * l + half, :], src

            with nc.Block() as block:
                @block.sync
                def _(sp):
                    sp.dma_start(x_rows[0], a["x_prompt"][0]).then_inc(x_in.sem, x_in.up(16))
                    sp.dma_start(h[:].rearrange("p k t -> p (k t)")[:, D:TT * D].rearrange("p (t f) -> p t f", f=D),
                                 a["x_sample"][0].rearrange("(t p) f -> p t f", p=P)).then_inc(x_in.sem, x_in.up(16))
                    for n in range(RING):
                        load_block(sp, n)

                @block.gpsimd
                def _(pool):
                    for l in range(1, DEPTH, 2):
                        for dst, src in parameter_rows(l):
                            pool.dma_start(dst, src).then_inc(stage_in_odd.sem, stage_in_odd.up(16))
                    nc.gpsimd.memset(ident[:], 0.0).then_inc(consts.sem, consts.up())
                    pool.wait_ge(consts.sem, consts.n)
                    nc.gpsimd.affine_select(out=ident[:], in_=ident[:], compare_op=ALU.not_equal, fill=1.0,
                                            base=0, pattern=[[-1, P]], channel_multiplier=1)\
                        .then_inc(consts.sem, consts.up())
                    nc.gpsimd.memset(w_lr[:], 0.0)
                    nc.gpsimd.memset(eps_col[:, 0:1], EPS)
                    nc.gpsimd.memset(eps_col[:, 1:2], 1e-6)

                @block.scalar
                def _(act):
                    for l in range(0, DEPTH, 2):
                        for dst, src in parameter_rows(l):
                            act.dma_start(dst, src).then_inc(stage_in.sem, stage_in.up(16))

                @block.tensor
                def _(pe):
                    pe.wait_ge(consts.sem, consts.at(consts.n))
                    pe.wait_ge(stage_in.sem, stage_in.at(stage_in.n))
                    pe.wait_ge(stage_in_odd.sem, stage_in_odd.at(stage_in_odd.n))
                    for l in range(DEPTH):
                        nc.tensor.transpose(psum[:, 0, (2 * l) * P:(2 * l) * P + n_a], stage[0:n_a, 2 * l, :],
                                            ident[0:n_a, 0:n_a])
                        nc.tensor.transpose(psum[:, 0, (2 * l + 1) * P:(2 * l + 1) * P + n_b],
                                                      stage[0:n_b, 2 * l + 1, :], ident[0:n_b, 0:n_b])\
                                                          .then_inc(turned.sem, turned.up())

                @block.vector
                def _(dve):
                    dve.wait_ge(turned.sem, turned.at(DEPTH))
                    for l in range(DEPTH):
                        nc.vector.tensor_copy(pa[:, l, 0:n_a], psum[:, 0, 2 * l * P:2 * l * P + n_a])\
                            .then_inc(copied.sem, copied.up())
                        nc.vector.tensor_copy(pb[:, l, 0:n_b],
                                                        psum[:, 0, (2 * l + 1) * P:(2 * l + 1) * P + n_b])\
                                                            .then_inc(copied.sem, copied.up())
            with nc.Block() as block:
                @block.scalar
                def _(act):
                    for s, n in ((0, "c_ctx"), (1, "c")):
                        nc.scalar.activation(cond[:, :, s], pb[:, 0, at_b[n]:at_b[n] + KD], ACT.Silu)

        def modulation(l):
            landed = sem("small_weights_landed", l)
            kept = sem("ada_group_kept", l)
            cut = sem("ada_cut", l)
            turned = sem("ada_turned", l)
            added = sem("ada_added", l)
            x_turned, x_kept = sem("x_turned", l), sem("x_kept", l)
            base, count = parts["ada", l]
            PER = 512 // P
            GROUPS = count // PER
            ada_rows = u[:].rearrange("p s w -> p (s w)")[0:2, 0:count * P]
            cut_rows = wide[:].rearrange("p a t -> p (a t)")[:, 0:P]
            with nc.Block() as block:
                @block.sync
                def _(sp):
                    load_ahead(sp, ("ada", l))
                    sp.wait_ge(kept.sem, kept.at(GROUPS))
                    for s in range(2):
                        sp.dma_start(cut_rows[s * count:(s + 1) * count, :],
                                     ada_rows[s:s + 1, :].rearrange("p (m n) -> p m n", n=P))\
                                         .then_inc(cut.sem, cut.up(16))
                    sp.wait_ge(cut.sem, cut.at(32))

                @block.gpsimd
                def _(pool):
                    for z in range(2):
                        pool.dma_start(w_lr[z * LR:(z + 1) * LR, z * GW:(z + 1) * GW], a["gla_w_lr"][l, z])\
                            .then_inc(landed.sem, landed.up(16))
                    for n, (c0, c1) in NARROW.items():
                        at = narrow_at[n]
                        pool.dma_start(w_narrow[:, :, c0:c1],
                                       a["w_in"][l][:, at:at + c1 - c0].rearrange("(k p) n -> p k n", p=P))\
                            .then_inc(landed.sem, landed.up(16))
                    pool.dma_start(pw[:], a["conv_pw"][l].rearrange("(k p) n -> p k n", p=P))\
                        .then_inc(landed.sem, landed.up(16))
                    pool.dma_start(dtb[:], a["gdn_dt_bias"][l].rearrange("a h -> (a h)").partition_broadcast(P))\
                        .then_inc(landed.sem, landed.up(16))
                    pool.dma_start(nega[:], a["gdn_a_log"][l].rearrange("a h -> (a h)").partition_broadcast(P))\
                        .then_inc(landed.sem, landed.up(16))
                    if l % 2 == 1:
                        pool.dma_start(router[:], a["moe_router"][l // 2].rearrange("(k p) n -> p k n", p=P))\
                            .then_inc(landed.sem, landed.up(16))
                    if l == 0:
                        constants(pool)
                    pool.wait_ge(landed.sem, landed.n)

                @block.tensor
                def _(pe):
                    if l == 0:
                        pe.wait_ge(x_in.sem, x_in.at(x_in.n))
                        for t in range(TT):
                            if t >= 2:
                                pe.wait_ge(x_kept.sem, x_kept.at(t - 1))
                            for k in range(KD):
                                ins = nc.tensor.transpose(psum[:, 2 + t % 2, k * P:(k + 1) * P],
                                                          x_rows[t][:, k * P:(k + 1) * P], ident[:])
                            ins.then_inc(x_turned.sem, x_turned.up())
                    for g in range(GROUPS):
                        if g >= 4:
                            pe.wait_ge(kept.sem, kept.at(g - 3))
                        for m in range(g * PER, (g + 1) * PER):
                            block_landed(pe, base + m)
                            w = ring_view((base + m) % RING, KD)
                            c = (m % PER) * P
                            for k in range(KD):
                                ins = nc.tensor.matmul(bank(g % 4)[0:2, c:c + P], cond[:, k, :], w[:, k, :],
                                                       start=(k == 0), stop=(k == KD - 1))
                            ins.then_inc(ring_used.sem, ring_used.up())
                    pe.wait_ge(kept.sem, kept.at(GROUPS))
                    pe.wait_ge(cut.sem, cut.at(32))
                    nc.tensor.transpose(psum[:, 0, 0:2 * count], cut_rows[0:2 * count, :], ident[0:2 * count, 0:2 * count])\
                        .then_inc(turned.sem, turned.up())

                @block.vector
                def _(dve):
                    if l == 0:
                        for t in range(TT):
                            dve.wait_ge(x_turned.sem, x_turned.at(t + 1))
                            nc.vector.tensor_copy(x[:, :, t * P:(t + 1) * P],
                                                  psum[:, 2 + t % 2, :].rearrange("p (k n) -> p k n", n=P))\
                                .then_inc(x_kept.sem, x_kept.up())
                    for g in range(GROUPS):
                        dve.wait_ge(ring_used.sem, ring_used.at(base + (g + 1) * PER))
                        nc.vector.tensor_copy(ada_rows[:, g * 512:(g + 1) * 512], bank(g % 4)[0:2, :])\
                            .then_inc(kept.sem, kept.up())
                    dve.wait_ge(turned.sem, turned.at(1))
                    nc.vector.tensor_tensor(
                        mod[:].rearrange("p m s -> p s m"), psum[:, 0, 0:2 * count].rearrange("p (s m) -> p s m", s=2),
                        pa[:, l, 0:count].unsqueeze(1).to_broadcast([P, 2, count]), ALU.add)\
                            .then_inc(added.sem, added.up())
                    dve.wait_ge(added.sem, added.n)
                    for c in (1, 4):
                        v = mod[:, c * KD:(c + 1) * KD, :]
                        nc.vector.tensor_scalar(v, v, 1.0, None, ALU.add)

        def modulate(c):
            with nc.Block() as block:
                @block.vector
                def _(dve):
                    for k in range(0, KD, 2):
                        for s, (t0, t1) in enumerate(SEQS):
                            nc.vector.tensor_scalar(h[:, k, t0:t1], x[:, k, t0:t1], mod[:, (c + 1) * KD + k, s:s + 1],
                                                    mod[:, c * KD + k, s:s + 1], ALU.mult, ALU.add)

                @block.scalar
                def _(act):
                    for k in range(1, KD, 2):
                        for s, (t0, t1) in enumerate(SEQS):
                            nc.scalar.activation(h[:, k, t0:t1], x[:, k, t0:t1], ACT.Identity,
                                                 scale=mod[:, (c + 1) * KD + k, s:s + 1],
                                                 bias=mod[:, c * KD + k, s:s + 1])

        def gla_parts():
            q = [u[:, slot["gq"] + j, 0:T] for j in range(J)]
            k = [u[:, slot["gk"] + j, 0:T] for j in range(J)]
            qe = [[u[:, j, 0:T] for j in range(J)], q]
            ke = [[u[:, J + j, 0:T] for j in range(J)], k]
            kd = [[mix[:, J + z * J + j, :] for j in range(J)] for z in range(2)]
            return qe, ke, kd

        def project_in(l):
            base, count = parts["in", l]
            copied = sem("in_copied", l)
            low_rank = sem("in_low_rank", l)
            narrow = sem("in_narrow", l)
            pads = sem("in_pads", l)
            gate = sem("in_conformer_gate", l)
            conv_step = sem("in_conformer_conv", l)
            decay_act = sem("in_decay_scalar", l)
            decay_vec = sem("in_decay_vector", l)
            short_step = sem("in_short_conv", l)
            taps = sem("in_gdn_conv", l)
            PAIRS = [(z, j) for z in range(2) for j in range(J)]
            units = []
            for i in range(count):
                units.append(("tile", i))
                if i == 3:
                    units.append(("narrow", 0))
                if i >= 9 and i % 2 == 1 and (i - 9) // 2 < len(PAIRS):
                    units.append(("low", (i - 9) // 2))

            def unit(kind, i):
                return units.index((kind, i))

            def group_copied(n, j=0):
                i = next(i for i, tile in enumerate(in_tiles) if tile[1] == slot[n] + j)
                return copied.at(unit("tile", i) + 1)

            def copies(i, pair):
                n, s, _, m = in_tiles[i]
                src = psum[0:m, pair, :]
                pad = 1 if n in PADDED else 0
                if n in PERMUTED:
                    lat = u[0:m, s, CTX + 2 * pad:T + 2 * pad].rearrange("p (c r) -> p c r", r=ROWS)
                    return [(u[0:m, s, pad:CTX + pad], src[:, 0:CTX]),
                            (lat, src[:, CTX:T].rearrange("p (r c) -> p c r", c=GRID_W))]
                if pad:
                    return [(u[0:m, s, pad:CTX + pad], src[:, 0:CTX]),
                            (u[0:m, s, CTX + 2 * pad:T + 2 * pad], src[:, CTX:T])]
                return [(u[0:m, s, 0:T], src[:, 0:T])]

            sg = [u[:, slot["agate"] + j, 0:T] for j in range(J)]
            q = [u[:, slot["gq"] + j, 0:T] for j in range(J)]
            k_ = [u[:, slot["gk"] + j, 0:T] for j in range(J)]
            qe, ke, kd = gla_parts()
            dec = chunk_decay[:].rearrange("p (z j n) -> p z j n", z=2, j=J)
            taps_out = [u[:, slot["sb"] + i, 0:T + 1] for i in range(3 * J)]
            SCA, VEC = 7, 6
            with nc.Block() as block:
                @block.sync
                def _(sp):
                    load_ahead(sp, ("in", l))

                @block.tensor
                def _(pe):
                    for n, (kind, i) in enumerate(units):
                        if n >= 4:
                            pe.wait_ge(copied.sem, copied.at(n - 3))
                        if kind == "low":
                            z, j = PAIRS[i]
                            for c0, c1 in SHORT:
                                ins = nc.tensor.matmul(psum[:, n % 4, c0:c1], w_lr[:, z * GW + j * P:z * GW + (j + 1) * P],
                                                       u[0:2 * LR, slot["lr"], c0:c1], start=True, stop=True)
                            ins.then_inc(low_rank.sem, low_rank.up())
                            continue
                        if kind == "narrow":
                            m = w_narrow.shape[2]
                            for k in range(KD):
                                for c0, c1 in SHORT:
                                    ins = nc.tensor.matmul(psum[0:m, n % 4, c0:c1], w_narrow[:, k, :], h[:, k, c0:c1],
                                                           start=(k == 0), stop=(k == KD - 1))
                            ins.then_inc(narrow.sem, narrow.up())
                            continue
                        m = in_tiles[i][3]
                        block_landed(pe, base + i)
                        w = ring_view((base + i) % RING, KD, m)
                        for k in range(KD):
                            for c0, c1 in SHORT:
                                ins = nc.tensor.matmul(psum[0:m, n % 4, c0:c1], w[:, k, :], h[:, k, c0:c1],
                                                       start=(k == 0), stop=(k == KD - 1))
                        ins.then_inc(ring_used.sem, ring_used.up())

                @block.gpsimd
                def _(pool):
                    for j in range(J):
                        for c0, c1 in ((0, PADC), (CTX + PADC, CTX + 2 * PADC), (T + 2 * PADC, T + 3 * PADC)):
                            nc.gpsimd.memset(conv_in[:, j, c0:c1], 0.0).then_inc(pads.sem, pads.up())
                    for n in PADDED:
                        for j in range(J):
                            for c in (0, CTX + 1, T + 2):
                                nc.gpsimd.memset(u[:, slot[n] + j, c:c + 1], 0.0).then_inc(pads.sem, pads.up())

                @block.scalar
                def _(act):
                    silu_next = 0
                    for n, (kind, i) in enumerate(units):
                        if kind == "low":
                            z, j = PAIRS[i]
                            o = at_a["gla_b_lr"] + z * J + j
                            act.wait_ge(low_rank.sem, low_rank.at(i + 1))
                            if i:
                                act.wait_ge(decay_vec.sem, decay_vec.at(VEC * i))
                            nc.scalar.activation(tmp[:, 0, :], psum[:, n % 4, 0:T], ACT.Identity, bias=pa[:, l, o:o + 1])\
                                .then_inc(copied.sem, copied.up())
                            act.wait_ge(copied.sem, copied.n)
                            nc.scalar.activation(tmp[:, 1, :], tmp[:, 0, :], ACT.Abs)\
                                .then_inc(decay_act.sem, decay_act.up())
                            act.wait_ge(decay_act.sem, decay_act.n)
                            nc.scalar.activation(tmp[:, 1, :], tmp[:, 1, :], ACT.Exp, scale=-1.0)\
                                .then_inc(decay_act.sem, decay_act.up())
                            act.wait_ge(decay_act.sem, decay_act.n)
                            nc.scalar.activation(tmp[:, 1, :], tmp[:, 1, :], ACT.Ln, bias=1.0)\
                                .then_inc(decay_act.sem, decay_act.up())
                            act.wait_ge(decay_vec.sem, decay_vec.at(VEC * i + 3))
                            nc.scalar.activation(tmp[:, 0, :], tmp[:, 2, :], ACT.Exp, scale=1.0 / GLA_TAU)\
                                .then_inc(decay_act.sem, decay_act.up())
                            nc.scalar.activation(tmp[:, 3, :], tmp[:, 2, :], ACT.Exp, scale=-1.0 / GLA_TAU)\
                                .then_inc(decay_act.sem, decay_act.up())
                            last = tmp[:, 2, :].rearrange("p (n c) -> p n c", c=CHUNK)
                            last = last[:, :, CHUNK - 1] if z == 0 else last[:, :, 0]
                            nc.scalar.activation(dec[:, z, j, :], last, ACT.Exp, scale=1.0 / GLA_TAU)\
                                .then_inc(decay_act.sem, decay_act.up())
                            act.wait_ge(decay_vec.sem, decay_vec.at(VEC * i + 5))
                            nc.scalar.activation(kd[z][j], tmp[:, 1, :], ACT.Exp, scale=1.0 / GLA_TAU)\
                                .then_inc(decay_act.sem, decay_act.up())
                            continue
                        if kind == "narrow":
                            act.wait_ge(narrow.sem, narrow.at(1))
                            (r0, r1), (b0, b1) = NARROW["lr"], NARROW["bd"]
                            nc.scalar.activation(u[r0:r1, slot["lr"], 0:T], psum[r0:r1, n % 4, 0:T], ACT.Copy)
                            src, to = psum[b0:b1, n % 4, :], u[b0:b1, slot["bd"], :]
                            nc.scalar.activation(to[:, 0:CTX], src[:, 0:CTX], ACT.Copy)
                            nc.scalar.activation(to[:, CTX:T].rearrange("p (c r) -> p c r", r=ROWS),
                                                 src[:, CTX:T].rearrange("p (r c) -> p c r", c=GRID_W), ACT.Copy)\
                                .then_inc(copied.sem, copied.up())
                            continue
                        act.wait_ge(ring_used.sem, ring_used.at(base + i + 1))
                        for d, s in copies(i, n % 4):
                            ins = nc.scalar.activation(d, s, ACT.Copy)
                        ins.then_inc(copied.sem, copied.up())
                        if in_tiles[i][0] == "agate":
                            v = sg[in_tiles[i][1] - slot["agate"]]
                            act.wait_ge(copied.sem, copied.n)
                            nc.scalar.activation(v, v, ACT.Sigmoid).then_inc(gate.sem, gate.up())
                        if i >= count - 3 * J:
                            act.wait_ge(taps.sem, taps.at(3 * (silu_next + 1)))
                            for s, (a0, a1) in enumerate(SEQS):
                                nc.scalar.activation(u[:, slot["dq"] + silu_next, a0:a1],
                                                     taps_out[silu_next][:, a0 + s:a1 + s], ACT.Silu)
                            silu_next += 1
                    assert silu_next == 3 * J
                    nc.scalar.activation(nega[:], nega[:], ACT.Exp)

                @block.vector
                def _(dve):
                    dve.wait_ge(pads.sem, pads.at(3 * J))
                    for j in range(J):
                        dve.wait_ge(gate.sem, gate.at(j + 1))
                        for s, (t0, t1) in enumerate(SEQS):
                            o = PADC * (s + 1)
                            nc.vector.tensor_tensor(conv_in[:, j, t0 + o:t1 + o], u[:, slot["aval"] + j, t0:t1],
                                                    sg[j][:, t0:t1], ALU.mult).then_inc(conv_step.sem, conv_step.up())
                    dve.wait_ge(conv_step.sem, conv_step.n)
                    for k in range(CONV_K):
                        for j in range(J):
                            w = pb[:, l, at_b["conv_w"] + k * J + j:at_b["conv_w"] + k * J + j + 1]
                            if k == 0:
                                b = pa[:, l, at_a["conv_b"] + j:at_a["conv_b"] + j + 1]
                                ins = nc.vector.tensor_scalar(conv[:, j, 0:CW], conv_in[:, j, 0:CW], w, b,
                                                              ALU.mult, ALU.add)
                            else:
                                dve.wait_ge(conv_step.sem, conv_step.n - 1)
                                ins = nc.vector.scalar_tensor_tensor(out=conv[:, j, 0:CW], in0=conv_in[:, j, k:k + CW],
                                                                     scalar=w, in1=conv[:, j, 0:CW],
                                                                     op0=ALU.mult, op1=ALU.add)
                            ins.then_inc(conv_step.sem, conv_step.up())
                    dve.wait_ge(copied.sem, group_copied("gk", J - 1))
                    for i, (z, j) in enumerate(PAIRS):
                        dve.wait_ge(decay_act.sem, decay_act.at(SCA * i + 1))
                        nc.vector.tensor_scalar(tmp[:, 0, :], tmp[:, 0, :], 0.0, None, ALU.min)\
                            .then_inc(decay_vec.sem, decay_vec.up())
                        dve.wait_ge(decay_vec.sem, decay_vec.n)
                        dve.wait_ge(decay_act.sem, decay_act.at(SCA * i + 3))
                        nc.vector.tensor_tensor(tmp[:, 0, :], tmp[:, 0, :], tmp[:, 1, :], ALU.subtract)\
                            .then_inc(decay_vec.sem, decay_vec.up())
                        dve.wait_ge(decay_vec.sem, decay_vec.n)
                        cum, la, r = tmp[:, 2, :], tmp[:, 0, :], resets[:, z, :]
                        if z == 1:
                            cum, la, r = cum[:, ::-1], la[:, ::-1], r[:, ::-1]
                        nc.vector.tensor_tensor_scan(cum, r, la, 0.0, ALU.mult, ALU.add)\
                            .then_inc(decay_vec.sem, decay_vec.up())
                        dve.wait_ge(decay_act.sem, decay_act.at(SCA * i + 5))
                        nc.vector.scalar_tensor_tensor(out=qe[z][j], in0=q[j], scalar=QSCALE, in1=tmp[:, 0, :],
                                                       op0=ALU.mult, op1=ALU.mult)\
                                                           .then_inc(decay_vec.sem, decay_vec.up())
                        cums = tmp[:, 2, :].rearrange("p (n c) -> p n c", c=CHUNK)
                        last = cums[:, :, CHUNK - 1:CHUNK] if z == 0 else cums[:, :, 0:1]
                        dve.wait_ge(decay_vec.sem, decay_vec.n)
                        nc.vector.tensor_tensor(tmp[:, 1, :].rearrange("p (n c) -> p n c", c=CHUNK),
                                                last.to_broadcast([P, NCH, CHUNK]), cums, ALU.subtract)\
                            .then_inc(decay_vec.sem, decay_vec.up())
                        dve.wait_ge(decay_act.sem, decay_act.at(SCA * i + 7))
                        nc.vector.tensor_tensor(kd[z][j], kd[z][j], k_[j], ALU.mult)
                        nc.vector.tensor_tensor(ke[z][j], k_[j], tmp[:, 3, :], ALU.mult)\
                            .then_inc(decay_vec.sem, decay_vec.up())
                    dve.wait_ge(pads.sem, pads.n)
                    dve.wait_ge(copied.sem, group_copied("sx", J - 1))
                    for j in range(J):
                        sx, sc, sbt = (u[:, slot[n] + j, :] for n in ("sx", "sc", "sb"))
                        for s, (t0, t1) in enumerate(SEQS):
                            v = sx[:, t0 + 1 + s:t1 + 1 + s]
                            nc.vector.tensor_tensor(v, v, sc[:, t0:t1], ALU.mult)\
                                .then_inc(short_step.sem, short_step.up())
                        dve.wait_ge(short_step.sem, short_step.n)
                        cv = mix[:, 0:2, :].rearrange("p a t -> p (a t)")[:, 0:T + 1]
                        o = at_a["sc_conv_w"] + j
                        conv3(dve, short_step, cv, sx, lambda k: pa[:, l, o + k * J:o + k * J + 1], T + 1)
                        dve.wait_ge(short_step.sem, short_step.n)
                        for s, (t0, t1) in enumerate(SEQS):
                            nc.vector.tensor_tensor(mix[:, 3 * J + j, t0:t1], cv[:, t0 + s:t1 + s], sbt[:, t0:t1],
                                                    ALU.mult).then_inc(short_step.sem, short_step.up())
                        dve.wait_ge(short_step.sem, short_step.n)
                    for i in range(3 * J):
                        dve.wait_ge(copied.sem, group_copied(("dq", "dk", "dv")[i // J], i % J))
                        o = at_a["gdn_conv_w"] + i
                        conv3(dve, taps, taps_out[i], u[:, slot["dq"] + i, :],
                              lambda k: pa[:, l, o + k * 3 * J:o + k * 3 * J + 1], T + 1)

        def conv3(dve, done, dst, src, w, width):
            nc.vector.tensor_scalar(dst, src[:, 0:width], w(0), None, ALU.mult).then_inc(done.sem, done.up())
            for k in (1, 2):
                dve.wait_ge(done.sem, done.n)
                nc.vector.scalar_tensor_tensor(out=dst, in0=src[:, k:k + width], scalar=w(k), in1=dst,
                                               op0=ALU.mult, op1=ALU.add).then_inc(done.sem, done.up())

        def gla(l):
            v = [u[:, slot["gv"] + j, 0:T] for j in range(J)]
            qe, ke, kd = gla_parts()
            free = slot["sb"]
            kd_tok = u[:, free:free + 4, :].rearrange("p s w -> p (s w)")[:, 0:TT * 2 * GW]\
                .rearrange("p (t z f) -> p t z f", t=TT, z=2)
            v_tok = u[:, free + 4:free + 6, :].rearrange("p s w -> p (s w)")[:, 0:TT * GW]\
                .rearrange("p (t f) -> p t f", t=TT)
            PAIRS = [(z, j) for z in range(2) for j in range(J)]
            dec = chunk_decay[:].rearrange("p (z j n) -> p z j n", z=2, j=J)

            copied = [sem(f"gla_turned_copied_by_{e}", l) for e in ("vector", "scalar")]
            turned = sem("gla_turned", l)
            mean, var, out_tiles = (sem(f"conf_{n}", l) for n in ("mean", "variance", "outputs"))
            centred, squared, scaled, active = (sem(f"conf_{n}", l) for n in ("centred", "squared", "scaled", "active"))
            rstd = sem("conf_rstd", l)
            ends = ((0, CTX), (CTX + PADC, CW))
            banks = ((0, 512), (512, CW))
            sq = [tmp[:, :, :].rearrange("p a t -> p (a t)")[:, j * CW:(j + 1) * CW] for j in range(J)]
            std = tmp[:, :, :].rearrange("p a t -> p (a t)")[:, J * CW:(J + 1) * CW]
            jobs = [(v[j], v_tok[:, :, j * P:(j + 1) * P]) for j in range(J)] + \
                   [(kd[z][j], kd_tok[:, :, z, j * P:(j + 1) * P]) for z, j in PAIRS]
            with nc.Block() as block:
                @block.tensor
                def _(pe):
                    def turn(i):
                        if i >= 2:
                            pe.wait_ge(copied[i % 2].sem, copied[i % 2].at(i // 2))
                        for t in range(TT):
                            ins = nc.tensor.transpose(psum[:, 2 + i % 2, t * P:(t + 1) * P],
                                                      jobs[i][0][:, t * P:(t + 1) * P], ident[:])
                        ins.then_inc(turned.sem, turned.up())
                    for j in range(J):
                        for c0, c1 in banks:
                            ins = nc.tensor.matmul(psum[:, 0, c0:c1], mean_g[:], conv[:, j, c0:c1],
                                                   start=(j == 0), stop=(j == J - 1))
                    ins.then_inc(mean.sem, mean.up())
                    for i in (0, 1):
                        turn(i)
                    pe.wait_ge(squared.sem, squared.at(J))
                    for j in range(J):
                        for c0, c1 in banks:
                            ins = nc.tensor.matmul(psum[:, 1, c0:c1], mean_g[:], sq[j][:, c0:c1],
                                                   start=(j == 0), stop=(j == J - 1))
                    ins.then_inc(var.sem, var.up())
                    for i in range(2, len(jobs)):
                        turn(i)
                    pe.wait_ge(active.sem, active.at(J))
                    for m in range(J):
                        for k in range(J):
                            for c0, c1 in banks:
                                ins = nc.tensor.matmul(psum[:, m, c0:c1], pw[:, k, m * P:(m + 1) * P],
                                                       conv[:, k, c0:c1], start=(k == 0), stop=(k == J - 1))
                        ins.then_inc(out_tiles.sem, out_tiles.up())

                @block.vector
                def _(dve):
                    def copy(i):
                        dve.wait_ge(turned.sem, turned.at(i + 1))
                        nc.vector.tensor_copy(jobs[i][1], psum[:, 2 + i % 2, 0:T].rearrange("p (t n) -> p t n", n=P))\
                            .then_inc(copied[0].sem, copied[0].up())
                    dve.wait_ge(mean.sem, mean.at(1))
                    for j in range(J):
                        nc.vector.tensor_tensor(conv[:, j, 0:CW], conv[:, j, 0:CW], psum[:, 0, 0:CW], ALU.subtract)\
                            .then_inc(centred.sem, centred.up())
                    copy(0)
                    copy(2)
                    dve.wait_ge(rstd.sem, rstd.at(2))
                    dve.wait_ge(centred.sem, centred.at(J))
                    for j in range(J):
                        nc.vector.tensor_tensor(conv[:, j, 0:CW], conv[:, j, 0:CW], std, ALU.mult)\
                            .then_inc(scaled.sem, scaled.up())
                    copy(4)
                    dve.wait_ge(out_tiles.sem, out_tiles.at(2))
                    for (t0, t1), (c0, c1) in zip(SEQS, ends):
                        nc.vector.tensor_copy(mix[:, 1, t0:t1], psum[:, 1, c0:c1])

                @block.scalar
                def _(act):
                    def copy(i):
                        act.wait_ge(turned.sem, turned.at(i + 1))
                        nc.scalar.activation(jobs[i][1], psum[:, 2 + i % 2, 0:T].rearrange("p (t n) -> p t n", n=P),
                                             ACT.Copy).then_inc(copied[1].sem, copied[1].up())
                    for j in range(J):
                        act.wait_ge(centred.sem, centred.at(j + 1))
                        nc.scalar.activation(sq[j], conv[:, j, 0:CW], ACT.Square).then_inc(squared.sem, squared.up())
                    copy(1)
                    act.wait_ge(var.sem, var.at(1))
                    nc.scalar.activation(std, psum[:, 1, 0:CW], ACT.Ln, bias=eps_col[:, 0:1])\
                        .then_inc(rstd.sem, rstd.up())
                    act.wait_ge(rstd.sem, rstd.n)
                    nc.scalar.activation(std, std, ACT.Exp, scale=-0.5).then_inc(rstd.sem, rstd.up())
                    copy(3)
                    for j in range(J):
                        act.wait_ge(scaled.sem, scaled.at(j + 1))
                        nc.scalar.activation(conv[:, j, 0:CW], conv[:, j, 0:CW], ACT.Silu,
                                             scale=pa[:, l, at_a["conv_ln_g"] + j:at_a["conv_ln_g"] + j + 1],
                                             bias=pa[:, l, at_a["conv_ln_b"] + j:at_a["conv_ln_b"] + j + 1])\
                            .then_inc(active.sem, active.up())
                    copy(5)
                    act.wait_ge(out_tiles.sem, out_tiles.at(1))
                    for (t0, t1), (c0, c1) in zip(SEQS, ends):
                        nc.scalar.activation(mix[:, 0, t0:t1], psum[:, 0, c0:c1], ACT.Copy)

            updates, states = sem("gla_updates", l), sem("gla_states", l)
            state_in, state_out = sem("gla_state_in", l), sem("gla_state_out", l)
            S = tmp[:].rearrange("p a t -> p (a t)").rearrange("p (z j n e) -> p z j n e", z=2, j=J, e=DK)
            final = wide[:, 0, 0:2 * J * DK].rearrange("p (z j e) -> p z j e", z=2, e=DK)
            CC = CTX // CHUNK

            def update(i, n):
                c = (n % 2) * 512 + (n // 2) * DK
                return psum[:, i, c:c + DK]
            orders = {0: (list(range(CC)), list(range(CC, NCH))), 1: (list(range(CC))[::-1], list(range(CC, NCH))[::-1])}
            with nc.Block() as block:
                @block.sync
                def _(sp):
                    for z, j in PAIRS:
                        sp.dma_start(S[:, z, j, orders[z][1][0], :],
                                     a["state_gla"][0, l, z, 2 * j:2 * j + 2].rearrange("h d e -> (h d) e"))\
                                         .then_inc(state_in.sem, state_in.up(16))
                    sp.wait_ge(states.sem, states.at(4 + 4 * NCH - 4))
                    for z, j in PAIRS:
                        sp.dma_start(out["gla"][0, l, z, 2 * j:2 * j + 2].rearrange("h d e -> (h d) e"),
                                     final[:, z, j, :]).then_inc(state_out.sem, state_out.up(16))
                    sp.wait_ge(state_out.sem, state_out.at(64))

                @block.tensor
                def _(pe):
                    for i, (z, j) in enumerate(PAIRS):
                        for n in range(NCH):
                            r0 = (n % 2) * CHUNK
                            for hp in range(2):
                                c = j * P + hp * DK
                                ins = nc.tensor.matmul(update(i, n)[hp * DK:(hp + 1) * DK, :],
                                                       kd_tok[r0:r0 + CHUNK, n // 2, z, c:c + DK],
                                                       v_tok[r0:r0 + CHUNK, n // 2, c:c + DK], start=True, stop=True)
                        ins.then_inc(updates.sem, updates.up())

                @block.vector
                def _(dve):
                    for z, j in PAIRS:
                        nc.vector.memset(S[:, z, j, orders[z][0][0], :], 0.0).then_inc(states.sem, states.up())
                    dve.wait_ge(states.sem, states.n)
                    dve.wait_ge(state_in.sem, state_in.at(64))
                    dve.wait_ge(updates.sem, updates.at(4))
                    for step in range(NCH - CC):
                        for seq in range(2):
                            for i, (z, j) in enumerate(PAIRS):
                                order = orders[z][seq]
                                if step >= len(order) or (seq == 1 and step == len(order) - 1):
                                    continue
                                n = order[step]
                                to = S[:, z, j, order[step + 1], :] if step + 1 < len(order) else final[:, z, j, :]
                                ins = nc.vector.scalar_tensor_tensor(
                                    out=to, in0=S[:, z, j, n, :], scalar=dec[:, z, j, n:n + 1],
                                    in1=update(i, n), op0=ALU.mult, op1=ALU.add)
                                ins.then_inc(states.sem, states.up())
                        dve.wait_ge(states.sem, states.n)

            scores, masked, outs, kept = (sem(f"gla_{n}", l) for n in ("scores", "masked", "outs", "kept"))
            att = u[:, free:free + 4, :].rearrange("p s w -> p (s w)")
            att = att[:, 0:4 * 512].rearrange("p (b h c) -> p b h c", b=4, h=H)
            o = [v[j] for j in range(J)]
            with nc.Block() as block:
                @block.tensor
                def _(pe):
                    def attend(t):
                        for z in range(2):
                            i = 2 * t + z
                            if i >= 3:
                                pe.wait_ge(masked.sem, masked.at(i - 2))
                            for hd in range(H):
                                r0 = (hd % 2) * DK
                                c = (hd % 2) * 512 + (hd // 2) * P
                                ins = nc.tensor.matmul(psum[:, i % 3, c:c + P],
                                                       ke[z][hd // 2][r0:r0 + DK, t * P:(t + 1) * P],
                                                       qe[z][hd // 2][r0:r0 + DK, t * P:(t + 1) * P],
                                                       start=True, stop=True)
                            ins.then_inc(scores.sem, scores.up())
                    attend(0)
                    for t in range(TT):
                        if t + 1 < TT:
                            attend(t + 1)
                        pe.wait_ge(masked.sem, masked.at(2 * t + 2))
                        if t >= 2:
                            pe.wait_ge(kept.sem, kept.at(t - 1))
                        for hd in range(H):
                            r0, j = (hd % 2) * DK, hd // 2
                            o_ps = bank(6 + t % 2)[r0:r0 + DK, j * P:(j + 1) * P]
                            for z in range(2):
                                nc.tensor.matmul(o_ps, v_tok[:, t, hd * DK:(hd + 1) * DK], att[:, (2 * t + z) % 4, hd, :],
                                                 start=(z == 0), stop=False, skip_group_check=True)
                            for z in range(2):
                                for c in range(2):
                                    n = 2 * t + c
                                    ins = nc.tensor.matmul(o_ps[:, c * CHUNK:(c + 1) * CHUNK],
                                                           S[r0:r0 + DK, z, j, n, :],
                                                           qe[z][j][r0:r0 + DK, n * CHUNK:(n + 1) * CHUNK],
                                                           start=False, stop=(z == 1), skip_group_check=True)
                        ins.then_inc(outs.sem, outs.up())

                @block.vector
                def _(dve):
                    for t in range(TT):
                        for z in range(2):
                            i = 2 * t + z
                            dve.wait_ge(scores.sem, scores.at(i + 1))
                            if i >= 4:
                                dve.wait_ge(outs.sem, outs.at(i // 2 - 1))
                            nc.vector.tensor_tensor(
                                att[:, i % 4, :, :].rearrange("p (j i) c -> p i j c", i=2),
                                psum[:, i % 3, :].rearrange("p (i r) -> p i r", i=2)[:, :, 0:J * P]
                                .rearrange("p i (j c) -> p i j c", j=J),
                                chunk_until[:, z, :].unsqueeze(1).unsqueeze(1).to_broadcast([P, 2, J, P]), ALU.mult)\
                                    .then_inc(masked.sem, masked.up())

                @block.scalar
                def _(act):
                    for t in range(TT):
                        act.wait_ge(outs.sem, outs.at(t + 1))
                        dst = u[:, slot["gv"]:slot["gv"] + J, t * P:(t + 1) * P]
                        nc.scalar.activation(dst, bank(6 + t % 2)[:, 0:J * P].rearrange("p (j c) -> p j c", j=J),
                                                     ACT.Copy).then_inc(kept.sem, kept.up())
            gated_norm(l, "gla", slot["gv"], slot["gg"], J, at_a["gla_norm_g"], permuted=False)

        def gated_norm(l, name, o_slot, gate_slot, first, norm, permuted):
            scalar_done, tensor_done, vector_done = (sem(f"{name}_norm_{n}", l) for n in ("scalar", "products", "vector"))
            with nc.Block() as block:
                @block.scalar
                def _(act):
                    for j in range(J):
                        nc.scalar.activation(tmp[:, j, :], u[:, o_slot + j, 0:T], ACT.Square)\
                            .then_inc(scalar_done.sem, scalar_done.up())
                    for j in range(J):
                        nc.scalar.activation(u[:, gate_slot + j, 0:T], u[:, gate_slot + j, 0:T], ACT.Silu)\
                            .then_inc(scalar_done.sem, scalar_done.up())
                    for j in range(J):
                        act.wait_ge(tensor_done.sem, tensor_done.at(j + 1))
                        nc.scalar.activation(tmp[:, J + j, :], psum[:, j, 0:T], ACT.Ln, bias=eps_col[:, 0:1],
                                                  scale=1.0 / DK).then_inc(scalar_done.sem, scalar_done.up())
                    act.wait_ge(scalar_done.sem, scalar_done.n)
                    for j in range(J):
                        nc.scalar.activation(tmp[:, J + j, :], tmp[:, J + j, :], ACT.Exp, scale=-0.5)\
                            .then_inc(scalar_done.sem, scalar_done.up())

                @block.tensor
                def _(pe):
                    for j in range(J):
                        pe.wait_ge(scalar_done.sem, scalar_done.at(j + 1))
                        for c0, c1 in SHORT:
                            ins = nc.tensor.matmul(psum[:, j, c0:c1], head_sum[:], tmp[:, j, c0:c1], start=True, stop=True)
                        ins.then_inc(tensor_done.sem, tensor_done.up())

                @block.vector
                def _(dve):
                    for j in range(J):
                        dve.wait_ge(scalar_done.sem, scalar_done.at(3 * J + j + 1))
                        o = u[:, o_slot + j, :]
                        nc.vector.tensor_tensor(o[:, 0:T], o[:, 0:T], tmp[:, J + j, :], ALU.mult)\
                            .then_inc(vector_done.sem, vector_done.up())
                        dve.wait_ge(vector_done.sem, vector_done.n)
                        for t0, t1 in SEQS:
                            src, gt, dst = o[:, t0:t1], u[:, gate_slot + j, t0:t1], mix[:, first + j, t0:t1]
                            if permuted and t0:
                                src = src.rearrange("p (c r) -> p r c", r=ROWS)
                                gt, dst = (w.rearrange("p (r c) -> p r c", r=ROWS) for w in (gt, dst))
                            nc.vector.scalar_tensor_tensor(out=dst, in0=src, scalar=pa[:, l, norm + j:norm + j + 1],
                                                                in1=gt, op0=ALU.mult, op1=ALU.mult)\
                                                                    .then_inc(vector_done.sem, vector_done.up())

        def gdn(l):
            feat = [u[:, slot["dq"] + i, 0:T] for i in range(3 * J)]

            def area(first, n, size):
                return u[:, first:first + n, :].rearrange("p s w -> p (s w)")[:, 0:size]
            k_tok = area(6, 2, TT * GW).rearrange("p (t f) -> p t f", t=TT)
            v_tok = area(8, 2, TT * GW).rearrange("p (t f) -> p t f", t=TT)
            o_acc = [u[:, 10 + j, 0:T] for j in range(J)]
            col = u[:, 12, :]
            beta = col[:, 0:TT * H].rearrange("p (t h) -> p t h", t=TT)
            dd = col[:, 20:20 + TT * 2 * H].rearrange("p (t z) -> p t z", t=TT)
            la = col[:, 60:60 + TT * 2 * H].rearrange("p (t z) -> p t z", t=TT)
            g = col[:, 100:100 + TT * 2 * H].rearrange("p (t z) -> p t z", t=TT)
            eg = col[:, 140:140 + TT * 2 * H].rearrange("p (t z) -> p t z", t=TT)
            t0c = col[:, 180:180 + TT * 2 * H].rearrange("p (t z) -> p t z", t=TT)
            norm_vector_step, norm_scalar_step, norm_tensor_step = (sem(f"gdn_norm_{n}", l) for n in ("vector2", "scalar2", "products2"))
            with nc.Block() as block:
                @block.scalar
                def _(act):
                    for i in range(2 * J):
                        nc.scalar.activation(tmp[:, i, :], feat[i], ACT.Square)\
                            .then_inc(norm_scalar_step.sem, norm_scalar_step.up())
                    act.wait_ge(norm_vector_step.sem, norm_vector_step.at(2))
                    nc.scalar.activation(beta, beta, ACT.Sigmoid).then_inc(norm_scalar_step.sem, norm_scalar_step.up())
                    for i in range(2 * J):
                        act.wait_ge(norm_tensor_step.sem, norm_tensor_step.at(2 + i))
                        nc.scalar.activation(tmp[:, i, :], psum[:, i, 0:T], ACT.Ln, bias=eps_col[:, 1:2])\
                            .then_inc(norm_scalar_step.sem, norm_scalar_step.up())
                    act.wait_ge(norm_scalar_step.sem, norm_scalar_step.n)
                    for i in range(2 * J):
                        nc.scalar.activation(tmp[:, i, :], tmp[:, i, :], ACT.Exp, scale=-0.5)\
                            .then_inc(norm_scalar_step.sem, norm_scalar_step.up())
                    act.wait_ge(norm_vector_step.sem, norm_vector_step.at(1))
                    nc.scalar.activation(t0c, dd, ACT.Abs).then_inc(norm_scalar_step.sem, norm_scalar_step.up())
                    act.wait_ge(norm_scalar_step.sem, norm_scalar_step.n)
                    nc.scalar.activation(t0c, t0c, ACT.Exp, scale=-1.0).then_inc(norm_scalar_step.sem, norm_scalar_step.up())
                    act.wait_ge(norm_scalar_step.sem, norm_scalar_step.n)
                    nc.scalar.activation(t0c, t0c, ACT.Ln, bias=1.0).then_inc(norm_scalar_step.sem, norm_scalar_step.up())

                @block.tensor
                def _(pe):
                    rows = slice(*NARROW["bd"])
                    bdt = u[rows, slot["bd"], :]
                    for t in range(TT):
                        ins = nc.tensor.transpose(psum[:, 3, 768 + 16 * t:768 + 16 * t + 3 * H],
                                                  bdt[:, t * P:(t + 1) * P], ident[rows, rows])
                    ins.then_inc(norm_tensor_step.sem, norm_tensor_step.up())
                    for i in range(2 * J):
                        pe.wait_ge(norm_scalar_step.sem, norm_scalar_step.at(i + 1))
                        for c0, c1 in SHORT:
                            if i == 3 and c0:
                                pe.wait_ge(norm_vector_step.sem, norm_vector_step.at(2))
                            ins = nc.tensor.matmul(psum[:, i, c0:c1], head_sum[:], tmp[:, i, c0:c1], start=True, stop=True)
                        ins.then_inc(norm_tensor_step.sem, norm_tensor_step.up())

                @block.vector
                def _(dve):
                    dve.wait_ge(norm_tensor_step.sem, norm_tensor_step.at(1))
                    nc.vector.tensor_tensor(
                        dd, psum[:, 3, 768:768 + TT * 16].rearrange("p (t c) -> p t c", c=16)[:, :, H:3 * H],
                        dtb[:].unsqueeze(1).to_broadcast([P, TT, 2 * H]), ALU.add)\
                            .then_inc(norm_vector_step.sem, norm_vector_step.up())
                    nc.vector.tensor_copy(
                        beta, psum[:, 3, 768:768 + TT * 16].rearrange("p (t c) -> p t c", c=16)[:, :, 0:H])\
                            .then_inc(norm_vector_step.sem, norm_vector_step.up())
                    for i in range(2 * J):
                        dve.wait_ge(norm_scalar_step.sem, norm_scalar_step.at(10 + i))
                        if i < J:
                            nc.vector.scalar_tensor_tensor(out=feat[i], in0=feat[i], scalar=QSCALE,
                                                                 in1=tmp[:, i, :], op0=ALU.mult, op1=ALU.mult)\
                                                                     .then_inc(norm_vector_step.sem, norm_vector_step.up())
                        else:
                            nc.vector.tensor_tensor(feat[i], feat[i], tmp[:, i, :], ALU.mult)\
                                .then_inc(norm_vector_step.sem, norm_vector_step.up())
                    dve.wait_ge(norm_scalar_step.sem, norm_scalar_step.at(16))
                    nc.vector.scalar_tensor_tensor(out=la, in0=dd, scalar=0.0, in1=t0c, op0=ALU.max, op1=ALU.add)\
                        .then_inc(norm_vector_step.sem, norm_vector_step.up())
                    dve.wait_ge(norm_vector_step.sem, norm_vector_step.n)
                    nc.vector.scalar_tensor_tensor(out=la, in0=la, scalar=-1.0,
                                                         in1=nega[:].unsqueeze(1).to_broadcast([P, TT, 2 * H]),
                                                         op0=ALU.mult, op1=ALU.mult)\
                                                             .then_inc(norm_vector_step.sem, norm_vector_step.up())
            turn_scalar_step, turn_tensor_step, turn_vector_step = (sem(f"gdn_turn_{n}", l) for n in ("scalar3", "products3", "vector3"))
            with nc.Block() as block:
                @block.tensor
                def _(pe):
                    for i in range(4):
                        for t in range(TT):
                            ins = nc.tensor.transpose(psum[:, i, t * P:(t + 1) * P], feat[J + i][:, t * P:(t + 1) * P],
                                                      ident[:])
                        ins.then_inc(turn_tensor_step.sem, turn_tensor_step.up())
                    pe.wait_ge(turn_vector_step.sem, turn_vector_step.at(1))
                    for z in range(2):
                        ins = nc.tensor.matmul(psum[:, 0, z * TT * H:(z + 1) * TT * H], until[:, z, :],
                                               la[:, :, z * H:(z + 1) * H], start=True, stop=True)
                    ins.then_inc(turn_tensor_step.sem, turn_tensor_step.up())

                @block.vector
                def _(dve):
                    for i in (0, 2):
                        dve.wait_ge(turn_tensor_step.sem, turn_tensor_step.at(i + 1))
                        dst = (k_tok, v_tok)[i // 2][:, :, 0:P]
                        nc.vector.tensor_copy(dst, psum[:, i, 0:T].rearrange("p (t n) -> p t n", n=P))\
                            .then_inc(turn_vector_step.sem, turn_vector_step.up())
                    dve.wait_ge(turn_tensor_step.sem, turn_tensor_step.at(5))
                    nc.vector.tensor_copy(g.rearrange("p t (z h) -> p z t h", z=2),
                                                psum[:, 0, 0:2 * TT * H].rearrange("p (z t h) -> p z t h", z=2, t=TT))\
                                                    .then_inc(turn_vector_step.sem, turn_vector_step.up())

                @block.scalar
                def _(act):
                    for i in (1, 3):
                        act.wait_ge(turn_tensor_step.sem, turn_tensor_step.at(i + 1))
                        dst = (k_tok, v_tok)[i // 2][:, :, P:2 * P]
                        nc.scalar.activation(dst, psum[:, i, 0:T].rearrange("p (t n) -> p t n", n=P), ACT.Copy)\
                            .then_inc(turn_scalar_step.sem, turn_scalar_step.up())
                    act.wait_ge(turn_vector_step.sem, turn_vector_step.at(3))
                    nc.scalar.activation(eg, g, ACT.Exp).then_inc(turn_scalar_step.sem, turn_scalar_step.up())
            gdn_chunks(l, feat, k_tok, v_tok, o_acc, beta, la, g, eg)
            gated_norm(l, "gdn", 10, slot["dgate"], 2 * J, at_a["gdn_norm_g"], permuted=True)

        def gdn_chunks(l, feat, k_tok, v_tok, o_acc, beta, la, g, eg):
            qf, kf = feat[0:J], feat[J:2 * J]
            rounds = [(0, 0)] + [(1 + i, TT - 1 - i) for i in range(TT - 1)]
            seen = set()
            first_visit = []
            for r in rounds:
                pair = []
                for t in r:
                    pair.append(t not in seen)
                    seen.add(t)
                first_visit.append(pair)
            flat_a = u[:, 0:6, :].rearrange("p s w -> p (s w)")
            flat_b = u[:, slot["sb"]:slot["sb"] + 6, :].rearrange("p s w -> p (s w)")
            flat_t = tmp[:].rearrange("p a t -> p (a t)")
            flat_w = wide[:].rearrange("p a t -> p (a t)")

            def bufs(f, n):
                return [f[:, i * 512:(i + 1) * 512].rearrange("p (h c) -> p h c", h=H) for i in range(n)]
            ba, bb, bt, bw = bufs(flat_a, 7), bufs(flat_b, 7), bufs(flat_t, 5), bufs(flat_w, 5)

            def rows(buffer):
                return buffer.rearrange("p h c -> p (h c)")
            side_bufs = []
            for s, own, more in ((0, ba, bt), (1, bb, bw)):
                side_bufs.append(dict(D=own[0], LT=own[1], QK=own[2], Ti=own[3], TiT=own[4], X=own[5], M=own[6],
                                      EG=more[0], VB=more[1][:, :, 0:DK], KB=more[1][:, :, DK:2 * DK],
                                      KD=more[2][:, :, 0:DK], VN=more[2][:, :, DK:2 * DK],
                                      QG=rows(more[3])[:, 0:J * P].rearrange("p (j c) -> p j c", j=J),
                                      WT=rows(more[3])[:, J * P:2 * J * P].rearrange("p (j c) -> p j c", j=J),
                                      S=rows(more[4])[:, 0:J * DK].rearrange("p (j e) -> p j e", j=J),
                                      EL=rows(more[4])[:, 200:200 + H],
                                      EK=rows(more[4])[:, 208:208 + H]))
            LV = 6
            names_ = ["decay_rows", "kk_qk", "turned_l", "x", "tx", "wt", "vn", "out", "upd"]
            tensor_done = {n: sem(f"gdnc_pe_{n}", l) for n in names_}
            vector_done = sem("gdnc_vector", l)
            scalar_done = sem("gdnc_scalar", l)
            pool_done = sem("gdnc_pool", l)
            st_in, st_out = sem("gdn_state_in", l), sem("gdn_state_out", l)

            GROUPS = [("dm", "dmin", "ek"), ("ltb", "lt", "qkm"), ("ti0", "tit0")]
            behind = [("vb", "kd"), ("kb0", "kb"), ("qg0", "qg1")]
            for b in range(LV):
                GROUPS.append((f"t{b}", f"tt{b}") if b < LV - 1 else (f"tt{b}",))
                if b < len(behind):
                    GROUPS.append(behind[b])
            GROUPS += [("vn",), ("oacc", "s0", "s1", "s2", "s3")]
            DV_ORDER = [(n, s) for group in GROUPS for s in range(2) for n in group]
            DV = {step: i for i, step in enumerate(DV_ORDER)}
            AC = {n: i for i, n in enumerate(["exp", "eg", "el", "ekx"] + [f"x{b}" for b in range(LV)] + ["wt"])}
            PO = {n: i for i, n in enumerate(["strict"] + [f"m{b}" for b in range(LV)])}

            def dn(r, n, s):
                return r * len(DV) + DV[n, s] + 1

            def an(r, n, s):
                return (r * len(AC) + AC[n]) * 2 + s + 1

            def pn(r, n, s):
                return (r * len(PO) + PO[n]) * 2 + s + 1

            def en(r, s, per=1, i=0):
                return (r * per + i) * 2 + s + 1

            with nc.Block() as block:
                @block.sync
                def _(sp):
                    for s in range(2):
                        sp.wait_ge(vector_done.sem, vector_done.at(dn(0, "s3", s)))
                        for j in range(J):
                            sp.dma_start(out["gdn"][0, l, s, 2 * j:2 * j + 2].rearrange("h d e -> (h d) e"),
                                         side_bufs[s]["S"][:, j, :]).then_inc(st_out.sem, st_out.up(16))
                    sp.wait_ge(tensor_done["out"].sem, tensor_done["out"].at(en(0, 1)))
                    sp.wait_ge(st_out.sem, st_out.at(64))
                    for s in range(2):
                        for j in range(J):
                            sp.dma_start(side_bufs[s]["S"][:, j, :],
                                         a["state_gdn"][0, l, s, 2 * j:2 * j + 2].rearrange("h d e -> (h d) e"))\
                                             .then_inc(st_in.sem, st_in.up(16))

                @block.tensor
                def _(pe):
                    for r, tiles in enumerate(rounds):
                        def decay_rows(s, t):
                            b0, b3 = bank(4 * s), bank(4 * s + 3)
                            if r:
                                pe.wait_ge(vector_done.sem, vector_done.at(dn(r - 1, "oacc", s)))
                            for hd in range(H):
                                nc.tensor.matmul(b0[:, hd * P:(hd + 1) * P],
                                                 la[:, t, s * H + hd:s * H + hd + 1].to_broadcast([P, P]),
                                                 until[:, s, :], start=True, stop=True)
                            for hd in range(H):
                                ins = nc.tensor.matmul(b3[:, hd * P:(hd + 1) * P],
                                                       beta[:, t, hd:hd + 1].to_broadcast([P, P]), ident[:],
                                                       start=True, stop=True)
                            ins.then_inc(tensor_done["decay_rows"].sem, tensor_done["decay_rows"].up())

                        def kk_qk(s, t, hp):
                            b1, b2 = bank(4 * s + 1), bank(4 * s + 2)
                            if hp == 0 and r:
                                pe.wait_ge(vector_done.sem, vector_done.at(dn(r - 1, "s3", s)))
                            if hp == 1:
                                pe.wait_ge(tensor_done["kk_qk"].sem, tensor_done["kk_qk"].at((r * 2 + s) * 2 + 1))
                            for hd in range(hp, H, 2):
                                r0, j = (hd % 2) * DK, hd // 2
                                ks = kf[j][r0:r0 + DK, t * P:(t + 1) * P]
                                nc.tensor.matmul(b1[:, hd * P:(hd + 1) * P], ks, ks, start=True, stop=True)
                                ins = nc.tensor.matmul(b2[:, hd * P:(hd + 1) * P], ks,
                                                       qf[j][r0:r0 + DK, t * P:(t + 1) * P], start=True, stop=True)
                            ins.then_inc(tensor_done["kk_qk"].sem, tensor_done["kk_qk"].up())
                        decay_rows(0, tiles[0])
                        kk_qk(0, tiles[0], 0)
                        decay_rows(1, tiles[1])
                        kk_qk(0, tiles[0], 1)
                        kk_qk(1, tiles[1], 0)
                        kk_qk(1, tiles[1], 1)
                        for s, t in enumerate(tiles):
                            B = side_bufs[s]
                            pe.wait_ge(vector_done.sem, vector_done.at(dn(r, "lt", s)))
                            for hd in range(H):
                                ins = nc.tensor.transpose(bank(4 * s + 3)[:, hd * P:(hd + 1) * P], B["LT"][:, hd, :], ident[:])
                            ins.then_inc(tensor_done["turned_l"].sem, tensor_done["turned_l"].up())
                        for b in range(LV):
                            for s, t in enumerate(tiles):
                                B = side_bufs[s]
                                b0 = bank(4 * s)
                                pe.wait_ge(pool_done.sem, pool_done.at(pn(r, f"m{b}", s)))
                                pe.wait_ge(vector_done.sem, vector_done.at(dn(r, "ti0" if b == 0 else f"tt{b - 1}", s)))
                                if b == 0:
                                    pe.wait_ge(scalar_done.sem, scalar_done.at(an(r, "ekx", s)))
                                else:
                                    pe.wait_ge(scalar_done.sem, scalar_done.at(an(r, f"x{b - 1}", s)))
                                for hd in range(H):
                                    ins = nc.tensor.matmul(b0[:, hd * P:(hd + 1) * P], B["M"][:, hd, :], B["Ti"][:, hd, :],
                                                           start=True, stop=True)
                                ins.then_inc(tensor_done["x"].sem, tensor_done["x"].up())
                            for s, t in enumerate(tiles):
                                B = side_bufs[s]
                                b1, b2 = bank(4 * s + 1), bank(4 * s + 2)
                                pe.wait_ge(scalar_done.sem, scalar_done.at(an(r, f"x{b}", s)))
                                pe.wait_ge(vector_done.sem, vector_done.at(dn(r, "tit0" if b == 0 else f"tt{b - 1}", s)))
                                for hd in range(H):
                                    if b < LV - 1:
                                        nc.tensor.matmul(b1[:, hd * P:(hd + 1) * P], B["TiT"][:, hd, :], B["X"][:, hd, :],
                                                         start=True, stop=True)
                                    ins = nc.tensor.matmul(b2[:, hd * P:(hd + 1) * P], B["X"][:, hd, :], B["TiT"][:, hd, :],
                                                           start=True, stop=True)
                                ins.then_inc(tensor_done["tx"].sem, tensor_done["tx"].up())
                        for s, t in enumerate(tiles):
                            B = side_bufs[s]
                            b3 = bank(4 * s + 3)
                            pe.wait_ge(vector_done.sem, vector_done.at(dn(r, f"tt{LV - 1}", s)))
                            for hd in range(H):
                                r0, j = (hd % 2) * DK, hd // 2
                                ins = nc.tensor.matmul(b3[r0:r0 + DK, j * P:(j + 1) * P], B["KB"][:, hd, :], B["TiT"][:, hd, :],
                                                       start=True, stop=True)
                            ins.then_inc(tensor_done["wt"].sem, tensor_done["wt"].up())
                        for s, t in enumerate(tiles):
                            B = side_bufs[s]
                            pe.wait_ge(scalar_done.sem, scalar_done.at(an(r, "wt", s)))
                            for hd in range(H):
                                r0, j = (hd % 2) * DK, hd // 2
                                vn = bank(4 * s + hd % 2)[:, j * DK:(j + 1) * DK]
                                nc.tensor.matmul(vn, B["TiT"][:, hd, :], B["VB"][:, hd, :], start=True, stop=False)
                                ins = nc.tensor.matmul(vn, B["WT"][r0:r0 + DK, j, :], B["S"][r0:r0 + DK, j, :],
                                                       start=False, stop=True)
                            ins.then_inc(tensor_done["vn"].sem, tensor_done["vn"].up())
                        for s, t in enumerate(tiles):
                            B = side_bufs[s]
                            b2, b3 = bank(4 * s + 2), bank(4 * s + 3)
                            pe.wait_ge(vector_done.sem, vector_done.at(dn(r, "vn", s)))
                            for hd in range(H):
                                r0, j = (hd % 2) * DK, hd // 2
                                o = b3[r0:r0 + DK, j * P:(j + 1) * P]
                                nc.tensor.matmul(o, B["VN"][:, hd, :], B["QK"][:, hd, :], start=True, stop=False)
                                ins = nc.tensor.matmul(o, B["S"][r0:r0 + DK, j, :], B["QG"][r0:r0 + DK, j, :],
                                                       start=False, stop=True)
                            ins.then_inc(tensor_done["out"].sem, tensor_done["out"].up())
                            for hd in range(H):
                                r0, j = (hd % 2) * DK, hd // 2
                                ins = nc.tensor.matmul(b2[r0:r0 + DK, j * DK:(j + 1) * DK], B["KD"][:, hd, :],
                                                       B["VN"][:, hd, :], start=True, stop=True)
                            ins.then_inc(tensor_done["upd"].sem, tensor_done["upd"].up())

                @block.scalar
                def _(act):
                    for r, tiles in enumerate(rounds):
                        def both(step):
                            for s, t in enumerate(tiles):
                                step(s, t, side_bufs[s])

                        def exp(s, t, B):
                            act.wait_ge(vector_done.sem, vector_done.at(dn(r, "dmin", s)))
                            nc.scalar.activation(B["D"], B["D"], ACT.Exp).then_inc(scalar_done.sem, scalar_done.up())

                        def egr(s, t, B):
                            act.wait_ge(vector_done.sem, vector_done.at(dn(r, "ek", s)))
                            if r:
                                act.wait_ge(vector_done.sem, vector_done.at(dn(r - 1, "qg1", s)))
                            nc.scalar.activation(B["EG"], bank(4 * s).rearrange("p (h c) -> p h c", h=H), ACT.Exp)\
                                .then_inc(scalar_done.sem, scalar_done.up())

                        def el(s, t, B):
                            last = bank(4 * s).rearrange("p (h c) -> p h c", h=H)[:, :, (P - 1) if s == 0 else 0]
                            if r:
                                act.wait_ge(vector_done.sem, vector_done.at(dn(r - 1, "s3", s)))
                            nc.scalar.activation(B["EL"], last, ACT.Exp).then_inc(scalar_done.sem, scalar_done.up())

                        def ekx(s, t, B):
                            act.wait_ge(vector_done.sem, vector_done.at(dn(r, "ek", s)))
                            nc.scalar.activation(B["EK"], B["EK"], ACT.Exp).then_inc(scalar_done.sem, scalar_done.up())
                        for f in (exp, egr, el, ekx):
                            both(f)
                        for b in range(LV):
                            def xcopy(s, t, B):
                                act.wait_ge(tensor_done["x"].sem, tensor_done["x"].at(en(r, s, LV, b)))
                                if b:
                                    act.wait_ge(tensor_done["tx"].sem, tensor_done["tx"].at(en(r, s, LV, b - 1)))
                                nc.scalar.activation(B["X"], bank(4 * s).rearrange("p (h c) -> p h c", h=H), ACT.Copy)\
                                    .then_inc(scalar_done.sem, scalar_done.up())
                            both(xcopy)

                        def wt(s, t, B):
                            act.wait_ge(tensor_done["wt"].sem, tensor_done["wt"].at(en(r, s)))
                            nc.scalar.mul(B["WT"], bank(4 * s + 3)[:, 0:J * P].rearrange("p (j c) -> p j c", j=J), -1.0)\
                                .then_inc(scalar_done.sem, scalar_done.up())
                        both(wt)

                @block.gpsimd
                def _(pool):
                    for r, tiles in enumerate(rounds):
                        for s, t in enumerate(tiles):
                            B = side_bufs[s]
                            pool.wait_ge(scalar_done.sem, scalar_done.at(an(r, "exp", s)))
                            nc.gpsimd.tensor_tensor(B["D"], B["D"], until[:, s:s + 1, :].to_broadcast([P, H, P]), ALU.mult)\
                                .then_inc(pool_done.sem, pool_done.up())
                        for b in range(LV):
                            for s, t in enumerate(tiles):
                                B = side_bufs[s]
                                if b == 0:
                                    pool.wait_ge(vector_done.sem, vector_done.at(dn(r, "lt", s)))
                                else:
                                    pool.wait_ge(tensor_done["x"].sem, tensor_done["x"].at(en(r, s, LV, b - 1)))
                                nc.gpsimd.tensor_tensor(B["M"], B["LT"],
                                                              level[:, b + 1, s:s + 1, :].to_broadcast([P, H, P]), ALU.mult)\
                                                                  .then_inc(pool_done.sem, pool_done.up())

                @block.vector
                def _(dve):
                    def v3(n):
                        return bank(n).rearrange("p (h c) -> p h c", h=H)

                    for r, tiles in enumerate(rounds):
                        def group(*steps):
                            for s, t in enumerate(tiles):
                                for step in steps:
                                    step(s, t, side_bufs[s])

                        if r == 0:
                            for s in range(2):
                                nc.vector.memset(side_bufs[s]["S"], 0.0)
                        if r == 1:
                            dve.wait_ge(st_in.sem, st_in.at(64))

                        def dm(s, t, B):
                            dve.wait_ge(tensor_done["decay_rows"].sem, tensor_done["decay_rows"].at(en(r, s)))
                            if r:
                                dve.wait_ge(pool_done.sem, pool_done.at(pn(r - 1, f"m{LV - 1}", s)))
                            gz = g[:, t, s * H:(s + 1) * H].unsqueeze(2).to_broadcast([P, H, P])
                            nc.vector.tensor_tensor(B["D"], v3(4 * s), gz, ALU.subtract)\
                                .then_inc(vector_done.sem, vector_done.up())

                        def dmin(s, t, B):
                            dve.wait_ge(vector_done.sem, vector_done.at(dn(r, "dm", s)))
                            nc.vector.tensor_scalar(B["D"], B["D"], 0.0, None, ALU.min)\
                                .then_inc(vector_done.sem, vector_done.up())

                        def ek(s, t, B):
                            last = v3(4 * s)[:, :, (P - 1) if s == 0 else 0]
                            nc.vector.tensor_tensor(B["EK"], last, g[:, t, s * H:(s + 1) * H], ALU.subtract)\
                                .then_inc(vector_done.sem, vector_done.up())

                        def qg(s, t, B, hp):
                            dve.wait_ge(scalar_done.sem, scalar_done.at(an(r, "eg", s)))
                            r0 = hp * DK
                            egv = B["EG"].rearrange("p (j i) c -> p j i c", i=2)[r0:r0 + DK, :, hp, :]
                            qv = u[r0:r0 + DK, slot["dq"]:slot["dq"] + J, t * P:(t + 1) * P]
                            nc.vector.tensor_tensor(B["QG"][r0:r0 + DK, :, :], qv, egv, ALU.mult)\
                                .then_inc(vector_done.sem, vector_done.up())

                        def qkm(s, t, B):
                            nc.vector.tensor_tensor(B["QK"], v3(4 * s + 2), B["D"], ALU.mult)\
                                .then_inc(vector_done.sem, vector_done.up())

                        def ltb(s, t, B):
                            dve.wait_ge(tensor_done["kk_qk"].sem, tensor_done["kk_qk"].at((r * 2 + s) * 2 + 2))
                            dve.wait_ge(pool_done.sem, pool_done.at(pn(r, "strict", s)))
                            nc.vector.tensor_tensor(B["LT"], v3(4 * s + 1), B["D"], ALU.mult)\
                                .then_inc(vector_done.sem, vector_done.up())

                        def lt(s, t, B):
                            dve.wait_ge(vector_done.sem, vector_done.at(dn(r, "ltb", s)))
                            nc.vector.tensor_tensor(B["LT"], v3(4 * s + 3), B["LT"], ALU.mult)\
                                .then_inc(vector_done.sem, vector_done.up())

                        def vb(s, t, B):
                            bt = beta[:, t, :].unsqueeze(2).to_broadcast([P, H, DK])
                            nc.vector.tensor_tensor(B["VB"], v_tok[:, t, :].rearrange("p (h e) -> p h e", h=H), bt, ALU.mult)\
                                .then_inc(vector_done.sem, vector_done.up())

                        def kdec(s, t, B):
                            dve.wait_ge(scalar_done.sem, scalar_done.at(an(r, "ekx", s)))
                            bt = B["EK"].unsqueeze(2).to_broadcast([P, H, DK])
                            nc.vector.tensor_tensor(B["KD"], k_tok[:, t, :].rearrange("p (h e) -> p h e", h=H), bt, ALU.mult)\
                                .then_inc(vector_done.sem, vector_done.up())

                        def kb0(s, t, B):
                            bt = beta[:, t, :].unsqueeze(2).to_broadcast([P, H, DK])
                            nc.vector.tensor_tensor(B["KB"], k_tok[:, t, :].rearrange("p (h e) -> p h e", h=H), bt, ALU.mult)\
                                .then_inc(vector_done.sem, vector_done.up())

                        def kb(s, t, B):
                            dve.wait_ge(vector_done.sem, vector_done.at(dn(r, "kb0", s)))
                            bt = eg[:, t, s * H:(s + 1) * H].unsqueeze(2).to_broadcast([P, H, DK])
                            nc.vector.tensor_tensor(B["KB"], B["KB"], bt, ALU.mult)\
                                .then_inc(vector_done.sem, vector_done.up())

                        def ti0(s, t, B):
                            dve.wait_ge(tensor_done["turned_l"].sem, tensor_done["turned_l"].at(en(r, s)))
                            m = level0t[:, s:s + 1, :].to_broadcast([P, H, P])
                            nc.vector.tensor_tensor(B["Ti"], v3(4 * s + 3), m, ALU.mult).then_inc(vector_inner.sem, 1)
                            vector_inner.n += 1
                            dve.wait_ge(vector_inner.sem, vector_inner.n)
                            nc.vector.scalar_tensor_tensor(out=B["Ti"], in0=B["Ti"], scalar=-1.0,
                                                                 in1=ident[:].unsqueeze(1).to_broadcast([P, H, P]),
                                                                 op0=ALU.mult, op1=ALU.add)\
                                                                     .then_inc(vector_done.sem, vector_done.up())

                        def tit0(s, t, B):
                            m = level[:, 0, s:s + 1, :].to_broadcast([P, H, P])
                            nc.vector.tensor_tensor(B["TiT"], B["LT"], m, ALU.mult).then_inc(vector_inner.sem, 1)
                            vector_inner.n += 1
                            dve.wait_ge(vector_inner.sem, vector_inner.n)
                            nc.vector.scalar_tensor_tensor(out=B["TiT"], in0=B["TiT"], scalar=-1.0,
                                                                 in1=ident[:].unsqueeze(1).to_broadcast([P, H, P]),
                                                                 op0=ALU.mult, op1=ALU.add)\
                                                                     .then_inc(vector_done.sem, vector_done.up())
                        group(dm, dmin, ek)
                        group(ltb, lt, qkm)
                        group(ti0, tit0)
                        meanwhile = [(vb, kdec), (kb0, kb), (lambda s, t, B: qg(s, t, B, 0), lambda s, t, B: qg(s, t, B, 1))]
                        for b in range(LV):
                            def ti(s, t, B):
                                dve.wait_ge(tensor_done["tx"].sem, tensor_done["tx"].at(en(r, s, LV, b)))
                                nc.vector.tensor_tensor(B["Ti"], B["Ti"], v3(4 * s + 1), ALU.subtract)\
                                    .then_inc(vector_done.sem, vector_done.up())

                            def tit(s, t, B):
                                dve.wait_ge(tensor_done["tx"].sem, tensor_done["tx"].at(en(r, s, LV, b)))
                                nc.vector.tensor_tensor(B["TiT"], B["TiT"], v3(4 * s + 2), ALU.subtract)\
                                    .then_inc(vector_done.sem, vector_done.up())
                            if b < LV - 1:
                                group(ti, tit)
                            else:
                                group(tit)
                            if b < len(meanwhile):
                                group(*meanwhile[b])

                        def vn(s, t, B):
                            dve.wait_ge(tensor_done["vn"].sem, tensor_done["vn"].at(en(r, s)))
                            nc.vector.tensor_copy(B["VN"].rearrange("p (j i) e -> p i j e", i=2),
                                                        psum[:, 2 * s, :].rearrange("p (i r) -> p i r", i=2)[:, :, 0:J * DK]
                                                        .rearrange("p i (j e) -> p i j e", j=J))\
                                                            .then_inc(vector_done.sem, vector_done.up())

                        def oacc(s, t, B):
                            dve.wait_ge(tensor_done["out"].sem, tensor_done["out"].at(en(r, s)))
                            o = u[:, 10:10 + J, t * P:(t + 1) * P]
                            src = bank(4 * s + 3)[:, 0:J * P].rearrange("p (j c) -> p j c", j=J)
                            if first_visit[r][s]:
                                ins = nc.vector.tensor_copy(o, src)
                            else:
                                dve.wait_ge(vector_done.sem, vector_done.n)
                                ins = nc.vector.tensor_tensor(o, o, src, ALU.add)
                            ins.then_inc(vector_done.sem, vector_done.up())

                        def upd(s, t, B, hd):
                            r0, j = (hd % 2) * DK, hd // 2
                            dve.wait_ge(tensor_done["upd"].sem, tensor_done["upd"].at(en(r, s)))
                            dve.wait_ge(scalar_done.sem, scalar_done.at(an(r, "el", s)))
                            Sv = B["S"][r0:r0 + DK, j, :]
                            nc.vector.scalar_tensor_tensor(out=Sv, in0=Sv, scalar=B["EL"][r0:r0 + DK, hd:hd + 1],
                                                                 in1=bank(4 * s + 2)[r0:r0 + DK, j * DK:(j + 1) * DK],
                                                                 op0=ALU.mult, op1=ALU.add)\
                                                                     .then_inc(vector_done.sem, vector_done.up())
                        group(vn)
                        group(oacc, *[lambda s, t, B, hd=hd: upd(s, t, B, hd) for hd in range(H)])

        vector_inner = sem("vector_inner")

        def close(l, name, ln_g, ln_b):
            vector_done, scalar_done, tensor_done = (sem(f"{name}_{n}", l) for n in ("vector", "scalar", "products"))
            sq = [u[:, k, 0:T] for k in range(KD)]
            rs = tmp[:, 0, :]
            with nc.Block() as block:
                @block.tensor
                def _(pe):
                    for c0, c1 in SHORT:
                        ins = nc.tensor.matmul(psum[:, 0, c0:c1], mean_d[:], x_sum[:, c0:c1], start=True, stop=True)
                    ins.then_inc(tensor_done.sem, tensor_done.up())
                    for k in range(KD):
                        pe.wait_ge(scalar_done.sem, scalar_done.at(k + 1))
                        for c0, c1 in SHORT:
                            ins = nc.tensor.matmul(psum[:, 1, c0:c1], mean_d[:], sq[k][:, c0:c1],
                                                   start=(k == 0), stop=(k == KD - 1))
                    ins.then_inc(tensor_done.sem, tensor_done.up())

                @block.vector
                def _(dve):
                    dve.wait_ge(tensor_done.sem, tensor_done.at(1))
                    for k in range(KD):
                        nc.vector.tensor_tensor(x[:, k, :], x[:, k, :], psum[:, 0, 0:T], ALU.subtract)\
                            .then_inc(vector_done.sem, vector_done.up())
                    dve.wait_ge(scalar_done.sem, scalar_done.at(KD + 2))
                    dve.wait_ge(vector_done.sem, vector_done.n)
                    for k in range(KD):
                        nc.vector.tensor_tensor(x[:, k, :], x[:, k, :], rs, ALU.mult)\
                            .then_inc(vector_done.sem, vector_done.up())

                @block.scalar
                def _(act):
                    for k in range(KD):
                        act.wait_ge(vector_done.sem, vector_done.at(k + 1))
                        nc.scalar.activation(sq[k], x[:, k, :], ACT.Square).then_inc(scalar_done.sem, scalar_done.up())
                    act.wait_ge(tensor_done.sem, tensor_done.at(2))
                    nc.scalar.activation(rs, psum[:, 1, 0:T], ACT.Ln, bias=eps_col[:, 0:1])\
                        .then_inc(scalar_done.sem, scalar_done.up())
                    act.wait_ge(scalar_done.sem, scalar_done.n)
                    nc.scalar.activation(rs, rs, ACT.Exp, scale=-0.5).then_inc(scalar_done.sem, scalar_done.up())
                    for k in range(KD):
                        act.wait_ge(vector_done.sem, vector_done.at(KD + k + 1))
                        nc.scalar.activation(x[:, k, :], x[:, k, :], ACT.Identity,
                                                  scale=pa[:, l, ln_g + k:ln_g + k + 1],
                                                  bias=pa[:, l, ln_b + k:ln_b + k + 1])\
                                                      .then_inc(scalar_done.sem, scalar_done.up())

        HALF = T // 2

        def halves(v):
            return v.rearrange("p (i c) -> p i c", c=HALF)

        def result(pair):
            return psum[:, pair, :].rearrange("p (i c) -> p i c", i=2)[:, :, 0:HALF]

        def split_products(pair, w_high, w_low, k_tiles, high, low, before=None):
            w_high, w_low = (w[:, 0:k_tiles * P].rearrange("p (k n) -> p k n", n=P) for w in (w_high, w_low))
            for k in range(k_tiles):
                if before:
                    before(k)
                for n, (w, v) in enumerate(((w_high, high), (w_high, low), (w_low, high))):
                    for b in range(2):
                        ins = nc.tensor.matmul(result(pair)[:, b, :], w[:, k, :], halves(v[:, k, :])[:, b, :],
                                               start=(k == 0 and n == 0), stop=(k == k_tiles - 1 and n == 2))
            return ins

        PIECES = ((0, 0, 0, CTX), (1, 0, CTX, HALF), (1, 1, HALF, T))

        def project_out(l):
            base, count = parts["out", l]
            added, x_scaled = sem("out_added", l), sem("out_scaled", l)
            w_split_high, w_split_low = sem("out_weights_high", l), sem("out_weights_low", l)
            mix_split_high, mix_split_low = sem("out_mix_high", l), sem("out_mix_low", l)
            summed = sem("out_summed", l)
            upper.close()
            with ExitStack() as own:
                def tensor(name, shape):
                    return own.enter_context(nc.sbuf_tensor(f"out_{name}_{l}", shape, F32R))
                mh, ml = tensor("mix_high", [P, KD, T]), tensor("mix_low", [P, KD, T])
                wh, wl = tensor("weights_high", [P, 2, KD * P]), tensor("weights_low", [P, 2, KD * P])
                with nc.Block() as block:
                    @block.sync
                    def _(sp):
                        load_ahead(sp, ("out", l))

                    @block.scalar
                    def _(act):
                        def split(m):
                            block_landed(act, base + m)
                            if m >= 2:
                                act.wait_ge(ring_used.sem, ring_used.at(base + m - 1))
                            nc.scalar.activation(wh[:, m % 2, :], ring[:, (base + m) % RING, 0:KD * P], ACT.Copy)\
                                .then_inc(w_split_high.sem, w_split_high.up())
                        split(0)
                        for k in range(KD):
                            nc.scalar.activation(mh[:, k, :], mix[:, k, :], ACT.Copy)\
                                .then_inc(mix_split_high.sem, mix_split_high.up())
                        split(1)
                        for m in range(KD):
                            nc.scalar.mul(x[:, m, :], x[:, m, :], ALPHA).then_inc(x_scaled.sem, x_scaled.up())
                            if m + 2 < KD:
                                split(m + 2)

                    @block.tensor
                    def _(pe):
                        for m in range(KD):
                            pe.wait_ge(w_split_low.sem, w_split_low.at(m + 1))
                            if m >= 4:
                                pe.wait_ge(added.sem, added.at(m - 3))

                            def before(k):
                                if m == 0:
                                    pe.wait_ge(mix_split_low.sem, mix_split_low.at(k + 1))
                            split_products(m % 4, wh[:, m % 2, :], wl[:, m % 2, :], KD, mh, ml, before)\
                                .then_inc(ring_used.sem, ring_used.up())

                    @block.vector
                    def _(dve):
                        def low(m):
                            dve.wait_ge(w_split_high.sem, w_split_high.at(m + 1))
                            nc.vector.tensor_tensor(wl[:, m % 2, :], ring[:, (base + m) % RING, 0:KD * P],
                                                    wh[:, m % 2, :].bitcast(F32), ALU.subtract)\
                                .then_inc(w_split_low.sem, w_split_low.up())
                        low(0)
                        for k in range(KD):
                            dve.wait_ge(mix_split_high.sem, mix_split_high.at(k + 1))
                            nc.vector.tensor_tensor(ml[:, k, :], mix[:, k, :], mh[:, k, :].bitcast(F32), ALU.subtract)\
                                .then_inc(mix_split_low.sem, mix_split_low.up())
                        low(1)
                        for m in range(KD):
                            if m + 2 < KD:
                                low(m + 2)
                            dve.wait_ge(ring_used.sem, ring_used.at(base + m + 1))
                            dve.wait_ge(x_scaled.sem, x_scaled.at(m + 1))
                            for s, b, t0, t1 in PIECES:
                                ins = nc.vector.scalar_tensor_tensor(
                                    out=x[:, m, t0:t1], in0=result(m % 4)[:, b, t0 - b * HALF:t1 - b * HALF],
                                    scalar=mod[:, 2 * KD + m, s:s + 1], in1=x[:, m, t0:t1],
                                    op0=ALU.mult, op1=ALU.add)
                            ins.then_inc(added.sem, added.up())

                    @block.gpsimd
                    def _(pool):
                        for m in range(1, KD):
                            pool.wait_ge(added.sem, added.at(m + 1))
                            if m > 1:
                                pool.wait_ge(summed.sem, summed.at(m - 1))
                            nc.gpsimd.tensor_tensor(x_sum[:], x[:, 0, :] if m == 1 else x_sum[:], x[:, m, :], ALU.add)\
                                .then_inc(summed.sem, summed.up())
            place_upper(f"closing_{l}")

        def route(l):
            ones = until[:, 0, P - 1:P]
            area = wide[:, 0, :]
            logits = area[:, 0:TT * NE].rearrange("p (t n) -> p t n", t=TT)
            top = area[:, 40:80].rearrange("p (t n) -> p t n", t=TT)
            index = area[:, 80:120].rearrange("p (t n) -> p t n", t=TT)
            idx = area[:, 120:160].bitcast(U32).rearrange("p (t n) -> p t n", t=TT)
            share = area[:, 160:170].rearrange("p (i t) -> p i t", i=2)
            comb = area[:, 200:240].rearrange("p (t n) -> p t n", t=TT)
            part = area[:, 240:280].rearrange("p (t n) -> p t n", t=TT)
            numbers = area[:, 280:320].rearrange("p (t n) -> p t n", t=TT)
            chosen = area[:, 320:360].rearrange("p (t n) -> p t n", t=TT)
            total = area[:, 360:360 + NE]
            steps = area[:, 368:368 + NE]
            NS = T // STEP
            over = area[:, 400:400 + NE * (NS - 1)].rearrange("p (n b) -> p n b", n=NE)
            numbers_built = sem("route_numbers", l)
            ranks = sem("route_ranks", l)
            ranks_read = sem("route_ranks_read", l)
            logits_ready = sem("route_logits", l)
            spread = sem("route_spread", l)
            spread_read = sem("route_spread_read", l)
            turned = sem("route_turned", l)
            turned_read = sem("route_turned_read", l)
            lead = sem("route_lead", l)
            lead_exp = sem("route_lead_exp", l)
            inner = sem("route_inner", l)
            chosen_ready = sem("route_chosen", l)
            with nc.Block() as block:
                @block.gpsimd
                def _(pool):
                    for n in range(NE):
                        nc.gpsimd.memset(numbers[:, :, n], float(n)).then_inc(numbers_built.sem, numbers_built.up())

                @block.tensor
                def _(pe):
                    for t in range(TT):
                        for k in range(KD):
                            ins = nc.tensor.matmul(psum[:, 0, t * NE:(t + 1) * NE], h[:, k, t * P:(t + 1) * P],
                                                   router[:, k, :], start=(k == 0), stop=(k == KD - 1))
                    ins.then_inc(logits_ready.sem, logits_ready.up())
                    for t in range(TT):
                        if t >= 3:
                            pe.wait_ge(turned_read.sem, turned_read.at(t - 2))
                        for k in range(KD):
                            ins = nc.tensor.transpose(psum[:, 1 + t % 3, k * P:(k + 1) * P], h[:, k, t * P:(t + 1) * P],
                                                      ident[:])
                        ins.then_inc(turned.sem, turned.up())
                    pe.wait_ge(chosen_ready.sem, chosen_ready.at(1))
                    for t in range(TT):
                        for s in range(t + 1):
                            nc.tensor.matmul(psum[:, 0, t * NE:(t + 1) * NE],
                                             until[:, 0, :] if s == t else ones.to_broadcast([P, P]),
                                             chosen[:, s, :], start=(s == 0), stop=(s == t))
                    for s in range(TT):
                        nc.tensor.matmul(psum[:, 0, TT * NE:(TT + 1) * NE], ones.to_broadcast([P, P]),
                                         chosen[:, s, :], start=(s == 0), stop=(s == TT - 1))
                    nc.tensor.matmul(psum[:, 0, 512:512 + P], ones.to_broadcast([P, P]), until[:, 0, :],
                                     start=True, stop=True)
                    nc.tensor.matmul(psum[:, 0, 512 + P:512 + P + 2], until[:, 0, :], ones.to_broadcast([P, 2]),
                                     start=True, stop=True).then_inc(ranks.sem, ranks.up())
                    pe.wait_ge(ranks_read.sem, ranks_read.at(1))
                    pe.wait_ge(turned_read.sem, turned_read.at(TT))
                    for i in range(2 * NE):
                        if i >= 4:
                            pe.wait_ge(spread_read.sem, spread_read.at(i - 3))
                        for t in range(TT):
                            col = comb[:, t, i // 2:i // 2 + 1] if i % 2 == 0 else places[:, i // 2, t:t + 1]
                            ins = nc.tensor.matmul(psum[:, i % 4, t * P:(t + 1) * P], col.to_broadcast([P, P]),
                                                   ident[:], start=True, stop=True)
                        ins.then_inc(spread.sem, spread.up())

                @block.vector
                def _(dve):
                    def step(ins):
                        ins.then_inc(inner.sem, inner.up())
                        dve.wait_ge(inner.sem, inner.n)
                    dve.wait_ge(logits_ready.sem, logits_ready.at(1))
                    step(nc.vector.tensor_copy(logits, psum[:, 0, 0:TT * NE].rearrange("p (t n) -> p t n", t=TT)))
                    for t in range(TT):
                        step(nc.vector.max(top[:, t, :], logits[:, t, :]))
                        step(nc.vector.max_index(idx[:, t, :], top[:, t, :], logits[:, t, :]))
                    step(nc.vector.tensor_copy(index, idx))
                    dve.wait_ge(numbers_built.sem, numbers_built.at(NE))
                    for dst, i in ((comb, 0), (part, 1)):
                        step(nc.vector.tensor_tensor(dst, numbers, index[:, :, i:i + 1].to_broadcast([P, TT, NE]),
                                                     ALU.is_equal))
                    nc.vector.tensor_tensor(chosen, comb, part, ALU.add).then_inc(chosen_ready.sem, chosen_ready.up())
                    nc.vector.tensor_tensor(share[:, 1, :], top[:, :, 1], top[:, :, 0], ALU.subtract)\
                        .then_inc(lead.sem, lead.up())
                    dve.wait_ge(lead_exp.sem, lead_exp.at(1))
                    step(nc.vector.tensor_scalar(share[:, 0, :], share[:, 1, :], 1.0, None, ALU.add))
                    step(nc.vector.reciprocal(share[:, 0, :], share[:, 0, :]))
                    step(nc.vector.tensor_tensor(share[:, 1, :], share[:, 1, :], share[:, 0, :], ALU.mult))
                    dve.wait_ge(chosen_ready.sem, chosen_ready.at(1))
                    for dst, i in ((comb, 0), (part, 1)):
                        step(nc.vector.tensor_tensor(dst, dst, share[:, i, :].unsqueeze(2).to_broadcast([P, TT, NE]),
                                                     ALU.mult))
                    step(nc.vector.tensor_tensor(comb, comb, part, ALU.add))
                    dve.wait_ge(ranks.sem, ranks.at(1))
                    nc.vector.memset(places[:, NE, :], 0.0)
                    step(nc.vector.tensor_tensor(places[:, 0:NE, :].rearrange("p e t -> p t e"),
                                                 psum[:, 0, 0:TT * NE].rearrange("p (t n) -> p t n", t=TT),
                                                 chosen, ALU.mult))
                    step(nc.vector.tensor_copy(total, psum[:, 0, TT * NE:(TT + 1) * NE]))
                    for t in range(TT):
                        step(nc.vector.tensor_scalar(counting[:, t * P:(t + 1) * P], psum[:, 0, 512:512 + P],
                                                     float(t * P), None, ALU.add))
                        step(nc.vector.tensor_scalar(slot_number[:, t:t + 1], psum[:, 0, 512 + P:512 + P + 1],
                                                     float(t * P), None, ALU.add))
                    full = counting.rearrange("p (b c) -> p b c", c=STEP)[:, 0:NS - 1, STEP - 1]
                    step(nc.vector.tensor_tensor(over, total.unsqueeze(2).to_broadcast([P, NE, NS - 1]),
                                                 full.unsqueeze(1).to_broadcast([P, NE, NS - 1]), ALU.is_gt))
                    step(nc.vector.tensor_reduce(steps, over, axis=AX.X, op=ALU.add))
                    step(nc.vector.tensor_scalar(steps, steps, 1.0, float(P // STEP), ALU.add, ALU.max))
                    nc.vector.tensor_copy(steps_used, steps).then_inc(ranks_read.sem, ranks_read.up())

                @block.scalar
                def _(act):
                    for t in range(TT):
                        act.wait_ge(turned.sem, turned.at(t + 1))
                        nc.scalar.activation(h_rows[:, t, :], psum[:, 1 + t % 3, :], ACT.Copy)\
                            .then_inc(turned_read.sem, turned_read.up())
                    act.wait_ge(lead.sem, lead.at(1))
                    nc.scalar.activation(share[:, 1, :], share[:, 1, :], ACT.Exp).then_inc(lead_exp.sem, lead_exp.up())
                    for i in range(2 * NE):
                        act.wait_ge(spread.sem, spread.at(i + 1))
                        dst = (weight_rows, place_rows)[i % 2][:, i // 2, :]
                        nc.scalar.activation(dst, psum[:, i % 4, 0:T], ACT.Copy)\
                            .then_inc(spread_read.sem, spread_read.up())

        def feed_forward(l):
            base, count = parts["ffn", l]
            turns = count // PER_EXPERT
            slot_taken = sem("ffn_slot_taken", l)
            high_done, low_done = sem("ffn_weights_high", l), sem("ffn_weights_low", l)
            modulated, m_high, m_low = (sem(f"ffn_{n}", l) for n in ("modulated", "trunk_high", "trunk_low"))
            x_scaled = sem("ffn_x_scaled", l)
            gates, hid, hid_high, hid_low = (sem(f"ffn_{n}", l) for n in ("gates", "hidden", "hidden_high", "hidden_low"))
            added = sem("ffn_added", l)
            summed = sem("ffn_summed", l)
            upper.close()
            lower.close()
            with ExitStack() as own:
                def tensor(name, shape, dt):
                    return own.enter_context(nc.sbuf_tensor(f"ffn_{name}_{l}", shape, dt))
                mh, ml = tensor("trunk_high", [P, KD, T], F32R), tensor("trunk_low", [P, KD, T], F32R)
                hh, hl = tensor("hidden_high", [P, FT, T], F32R), tensor("hidden_low", [P, FT, T], F32R)
                wh, wl = tensor("weights_high", [P, 2, RW], F32R), tensor("weights_low", [P, 2, RW], F32R)
                rows = tensor("rows", [P, 2, T], F32)
                hid_rows = tensor("hidden_rows", [P, 2, T], F32)

                def products(pair, i, k_tiles, high, low, before=None):
                    return split_products(pair, wh[:, i % 2, :], wl[:, i % 2, :], k_tiles, high, low, before)

                def width(i):
                    return (KD if i < 2 * FT else FT) * P

                with nc.Block() as block:
                    @block.sync
                    def _(sp):
                        def turn(e, last):
                            for i in range(RING, PER_EXPERT + RING):
                                n = base + i
                                sp.wait_ge(low_done.sem, e * PER_EXPERT + (low_done.base + i - RING + 1))
                                sp.sem_inc(slot_taken.sem, 1)
                                if i >= PER_EXPERT and last:
                                    if base + count + i - PER_EXPERT < len(flat):
                                        w, c, m, k = flat[base + count + i - PER_EXPERT]
                                        sp.dma_start(ring_view(n % RING, k, m), column_block(w, c, m))\
                                            .then_inc(ring_loaded[n % RING].sem, 16)
                                    continue
                                src, k = expert_block(l, e + (1 if i >= PER_EXPERT else 0), i % PER_EXPERT)
                                sp.dma_start(ring_view(n % RING, k), src).then_inc(ring_loaded[n % RING].sem, 16)
                        with sp.Fori(0, turns - 1) as e:
                            turn(e, False)
                        turn(turns - 1, True)

                    @block.tensor
                    def _(pe):
                        def trunk_split(k):
                            pe.wait_ge(m_low.sem, m_low.at(k + 1))
                        with pe.Fori(0, turns) as e:
                            for i in range(PER_EXPERT):
                                pe.wait_ge(low_done.sem, e * PER_EXPERT + (low_done.base + i + 1))
                                m = i - 2 * FT
                                if i < 2 * FT:
                                    if i >= 4:
                                        pe.wait_ge(hid.sem, e * FT + (hid.base + (i - 4) // 2 + 1))
                                    ins = products(i % 4, i, KD, mh, ml, trunk_split if i == 0 else None)
                                else:
                                    if m == 0:
                                        pe.wait_ge(hid_low.sem, e * FT + (hid_low.base + FT))
                                    if m >= 4:
                                        pe.wait_ge(added.sem, e * KD + (added.base + m - 3))
                                    ins = products(m % 4, i, FT, hh, hl)
                                ins.then_inc(ring_used.sem, 1)
                            pe.wait_ge(added.sem, e * KD + (added.base + KD))

                    @block.scalar
                    def _(act):
                        for k in range(KD):
                            act.wait_ge(modulated.sem, modulated.at(k + 1))
                            nc.scalar.activation(mh[:, k, :], rows[:, k % 2, :], ACT.Copy)\
                                .then_inc(m_high.sem, m_high.up())

                        def split(e, i):
                            n = base + i
                            act.wait_ge(ring_loaded[n % RING].sem, (e * (PER_EXPERT // RING) + (n // RING + 1)) * 16)
                            act.wait_ge(ring_used.sem, e * PER_EXPERT + (base + i - 1))
                            nc.scalar.activation(wh[:, i % 2, 0:width(i)], ring[:, n % RING, 0:width(i)], ACT.Copy)\
                                .then_inc(high_done.sem, 1)
                        with act.Fori(0, turns) as e:
                            split(e, 0)
                            split(e, 1)
                            for f in range(FT):
                                split(e, 2 * f + 2)
                                if f == 0:
                                    act.wait_ge(hid.sem, e * FT + hid.base)
                                    act.wait_ge(m_low.sem, m_low.at(KD))
                                if f >= 2:
                                    act.wait_ge(hid.sem, e * FT + (hid.base + f - 1))
                                nc.scalar.activation(halves(rows[:, f % 2, :]), result((2 * f) % 4), ACT.Silu)\
                                    .then_inc(gates.sem, 1)
                                split(e, 2 * f + 3)
                                act.wait_ge(hid.sem, e * FT + (hid.base + f + 1))
                                nc.scalar.activation(hh[:, f, :], hid_rows[:, f % 2, :], ACT.Copy)\
                                    .then_inc(hid_high.sem, 1)
                            for i in range(2 * FT + 2, PER_EXPERT):
                                split(e, i)

                    @block.vector
                    def _(dve):
                        def low_trunk(k):
                            dve.wait_ge(m_high.sem, m_high.at(k + 1))
                            nc.vector.tensor_tensor(ml[:, k, :], rows[:, k % 2, :], mh[:, k, :].bitcast(F32),
                                                    ALU.subtract).then_inc(m_low.sem, m_low.up())
                        for k in range(KD):
                            if k >= 2:
                                dve.wait_ge(m_low.sem, m_low.at(k - 1))
                            for s, (t0, t1) in enumerate(SEQS):
                                ins = nc.vector.tensor_scalar(rows[:, k % 2, t0:t1], x[:, k, t0:t1],
                                                              mod[:, 4 * KD + k, s:s + 1], mod[:, 3 * KD + k, s:s + 1],
                                                              ALU.mult, ALU.add)
                            ins.then_inc(modulated.sem, modulated.up())
                            if k >= 1:
                                low_trunk(k - 1)
                        low_trunk(KD - 1)

                        def low(e, i):
                            n = base + i
                            dve.wait_ge(high_done.sem, e * PER_EXPERT + (high_done.base + i + 1))
                            nc.vector.tensor_tensor(wl[:, i % 2, 0:width(i)], ring[:, n % RING, 0:width(i)],
                                                    wh[:, i % 2, 0:width(i)].bitcast(F32), ALU.subtract)\
                                .then_inc(low_done.sem, 1)
                        with dve.Fori(0, turns) as e:
                            low(e, 0)
                            low(e, 1)
                            for f in range(FT):
                                low(e, 2 * f + 2)
                                dve.wait_ge(gates.sem, e * FT + (gates.base + f + 1))
                                dve.wait_ge(ring_used.sem, e * PER_EXPERT + (base + 2 * f + 2))
                                nc.vector.tensor_tensor(halves(hid_rows[:, f % 2, :]), halves(rows[:, f % 2, :]),
                                                        result((2 * f + 1) % 4), ALU.mult).then_inc(hid.sem, 1)
                                low(e, 2 * f + 3)
                                dve.wait_ge(hid_high.sem, e * FT + (hid_high.base + f + 1))
                                nc.vector.tensor_tensor(hl[:, f, :], hid_rows[:, f % 2, :], hh[:, f, :].bitcast(F32),
                                                        ALU.subtract).then_inc(hid_low.sem, 1)
                            for m in range(KD):
                                if m + 2 < KD:
                                    low(e, 2 * FT + m + 2)
                                if m == 0:
                                    dve.wait_ge(x_scaled.sem, x_scaled.at(KD))
                                dve.wait_ge(summed.sem, e * (KD - 1) + summed.base)
                                dve.wait_ge(ring_used.sem, e * PER_EXPERT + (base + 2 * FT + m + 1))
                                for s, b, t0, t1 in PIECES:
                                    ins = nc.vector.scalar_tensor_tensor(
                                        out=x[:, m, t0:t1], in0=result(m % 4)[:, b, t0 - b * HALF:t1 - b * HALF],
                                        scalar=mod[:, 5 * KD + m, s:s + 1], in1=x[:, m, t0:t1],
                                        op0=ALU.mult, op1=ALU.add)
                                ins.then_inc(added.sem, 1)
                            dve.wait_ge(added.sem, e * KD + (added.base + KD))

                    @block.gpsimd
                    def _(pool):
                        for k in range(KD):
                            pool.wait_ge(modulated.sem, modulated.at(k + 1))
                            nc.gpsimd.tensor_scalar(x[:, k, :], x[:, k, :], ALPHA, None, ALU.mult)\
                                .then_inc(x_scaled.sem, x_scaled.up())
                        with pool.Fori(0, turns) as e:
                            for m in range(1, KD):
                                pool.wait_ge(added.sem, e * KD + (added.base + m + 1))
                                if m > 1:
                                    pool.wait_ge(summed.sem, e * (KD - 1) + (summed.base + m - 1))
                                nc.gpsimd.tensor_tensor(x_sum[:], x[:, 0, :] if m == 1 else x_sum[:], x[:, m, :], ALU.add)\
                                    .then_inc(summed.sem, 1)
                            pool.wait_ge(summed.sem, e * (KD - 1) + (summed.base + KD - 1))
            place_lower(f"after_{l}")
            place_upper(f"after_{l}")

        def mixture(l):
            base, count = parts["ffn", l]
            slot_taken = [sem(f"moe_slot_taken_by_{q}", l) for q in ("sync", "scalar")]
            gathered = sem("moe_gathered", l)
            tokens_in = [sem(f"moe_tokens_in_by_{e}", l) for e in ("scalar", "vector")]
            few_ready = sem("moe_few_ready", l)
            rest_ready = sem("moe_rest_ready", l)
            place_ready = sem("moe_place_ready", l)
            gates = sem("moe_gates", l)
            hid = sem("moe_hidden", l)
            outputs_in = [sem(f"moe_outputs_in_by_{e}", l) for e in ("scalar", "vector")]
            turned = sem("moe_outputs_turned", l)
            rows_in = [sem(f"moe_rows_in_by_{e}", l) for e in ("scalar", "vector")]
            spread = sem("moe_spread", l)
            added = sem("moe_added", l)
            x_scaled = sem("moe_x_scaled", l)
            summed = sem("moe_summed", l)
            HALF = KD // 2

            def pieces(width):
                return [(c0, min(c1, width)) for c0, c1 in SHORT if c0 < width]

            with nc.Block() as block:
                def load(eng, e, i, last):
                    n = base + i
                    if i + RING < PER_EXPERT or not last:
                        src, k = expert_block(l, e + (i + RING) // PER_EXPERT, (i + RING) % PER_EXPERT)
                        eng.dma_start(ring_view(n % RING, k), src).then_inc(ring_loaded[n % RING].sem, 16)

                @block.sync
                def _(sp):
                    def turn(e, last):
                        for i in range(0, PER_EXPERT, 2):
                            sp.wait_ge(ring_used.sem, e * PER_EXPERT + (base + i + 1))
                            sp.sem_inc(slot_taken[0].sem, 1)
                            load(sp, e, i, last)
                    with sp.Fori(0, NE - 1) as e:
                        turn(e, False)
                    turn(NE - 1, True)

                @block.tensor
                def _(pe):
                    def turn(e, width):
                        blocks = [(b, min(P, width - b * P)) for b in range((width + P - 1) // P)]
                        pe.wait_ge(few_ready.sem, e + 1)
                        pe.wait_ge(added.sem, e * KD)
                        if width > FEW:
                            pe.wait_ge(rest_ready.sem, e + 1)
                        picks = [(0, min(width, FEW), onehot_few)] + [(max(c0, FEW), c1, onehot)
                                                                       for c0, c1 in pieces(width) if c1 > FEW]
                        for m in range(KD):
                            if m >= 4:
                                pe.wait_ge(tokens_in[m % 2].sem, e * HALF + ((m - 4) // 2 + 1))
                            for c0, c1, pick in picks:
                                for t in range(TT):
                                    ins = nc.tensor.matmul(psum[:, m % 4, c0:c1], h_rows[:, t, m * P:(m + 1) * P],
                                                           pick[:, t, c0:c1], start=(t == 0), stop=(t == TT - 1))
                            ins.then_inc(gathered.sem, 1)
                        pe.wait_ge(tokens_in[0].sem, e * HALF + HALF - 1)
                        for i in range(2 * FT):
                            n = base + i
                            pe.wait_ge(ring_loaded[n % RING].sem, (e * (PER_EXPERT // RING) + (n // RING + 1)) * 16)
                            if i >= 4:
                                pe.wait_ge(hid.sem, e * FT + ((i - 4) // 2 + 1))
                            w = ring_view(n % RING, KD)
                            for k in range(KD):
                                if i == 0:
                                    pe.wait_ge(tokens_in[k % 2].sem, e * HALF + (k // 2 + 1))
                                for c0, c1 in pieces(width):
                                    ins = nc.tensor.matmul(psum[:, i % 4, c0:c1], w[:, k, :], h[:, k, c0:c1],
                                                           start=(k == 0), stop=(k == KD - 1))
                            ins.then_inc(ring_used.sem, 1)
                        for m in range(KD):
                            n = base + 2 * FT + m
                            pe.wait_ge(ring_loaded[n % RING].sem, (e * (PER_EXPERT // RING) + (n // RING + 1)) * 16)
                            if m == 0:
                                pe.wait_ge(gates.sem, e * FT + FT)
                            if m >= 4:
                                pe.wait_ge(outputs_in[m % 2].sem, e * HALF + ((m - 4) // 2 + 1))
                            w = ring_view(n % RING, FT)
                            for k in range(FT):
                                if m == 0:
                                    pe.wait_ge(hid.sem, e * FT + (k + 1))
                                for c0, c1 in pieces(width):
                                    ins = nc.tensor.matmul(psum[:, m % 4, c0:c1], w[:, k, :], hidden[k][:, c0:c1],
                                                           start=(k == 0), stop=(k == FT - 1))
                            ins.then_inc(ring_used.sem, 1)
                        for m in range(KD):
                            if m < 4:
                                pe.wait_ge(outputs_in[m % 2].sem, e * HALF + ((m + 4) // 2 + 1))
                            else:
                                pe.wait_ge(rows_in[m % 2].sem, e * HALF + ((m - 4) // 2 + 1))
                            for b, n in blocks:
                                ins = nc.tensor.transpose(psum[0:n, m % 4, b * P:(b + 1) * P],
                                                          h[:, m, b * P:b * P + n], ident[:])
                            ins.then_inc(turned.sem, 1)
                        pe.wait_ge(place_ready.sem, e * TT + TT)
                        for m in range(KD):
                            if m < 4:
                                pe.wait_ge(rows_in[m % 2].sem, e * HALF + ((m + 4) // 2 + 1))
                            else:
                                pe.wait_ge(added.sem, e * KD + (m - 3))
                            for b, n in blocks:
                                for c0, c1 in SHORT:
                                    ins = nc.tensor.matmul(psum[:, m % 4, c0:c1], y_rows[0:n, b, m * P:(m + 1) * P],
                                                           onehot[0:n, b, c0:c1], start=(b == 0),
                                                           stop=(b == len(blocks) - 1))
                            ins.then_inc(spread.sem, 1)
                    with pe.Fori(0, NE) as e:
                        used = pe.value_load(steps_used[0:1, bass.ds(e, 1)], min_val=P // STEP, max_val=T // STEP)
                        for n in range(P // STEP, T // STEP + 1):
                            with pe.If(used == n):
                                turn(e, n * STEP)

                @block.scalar
                def _(act):
                    for k in range(KD):
                        nc.scalar.mul(x[:, k, :], x[:, k, :], ALPHA).then_inc(x_scaled.sem, x_scaled.up())

                    def turn(e, last):
                        for m in range(0, KD, 2):
                            act.wait_ge(gathered.sem, e * KD + (m + 1))
                            nc.scalar.activation(h[:, m, :], psum[:, m % 4, 0:T], ACT.Copy)\
                                .then_inc(tokens_in[0].sem, 1)
                        for f in range(FT):
                            act.wait_ge(ring_used.sem, e * PER_EXPERT + (base + 2 * f + 1))
                            if f >= 2:
                                act.wait_ge(hid.sem, e * FT + (f - 1))
                            nc.scalar.activation(tmp[:, f % 2, :], psum[:, (2 * f) % 4, 0:T], ACT.Silu)\
                                .then_inc(gates.sem, 1)
                            if f >= 1:
                                load(act, e, 2 * f - 1, last)
                        for m in range(0, KD, 2):
                            act.wait_ge(ring_used.sem, e * PER_EXPERT + (base + 2 * FT + m + 1))
                            nc.scalar.activation(h[:, m, :], psum[:, m % 4, 0:T], ACT.Copy)\
                                .then_inc(outputs_in[0].sem, 1)
                            load(act, e, 2 * FT + m - 1, last)
                        act.wait_ge(ring_used.sem, e * PER_EXPERT + (base + PER_EXPERT))
                        act.sem_inc(slot_taken[1].sem, 1)
                        load(act, e, PER_EXPERT - 1, last)
                        for m in range(0, KD, 2):
                            act.wait_ge(turned.sem, e * KD + (m + 1))
                            nc.scalar.activation(y_rows[:, :, m * P:(m + 1) * P],
                                                 psum[:, m % 4, 0:T].rearrange("p (b f) -> p b f", b=TT),
                                                 ACT.Copy).then_inc(rows_in[0].sem, 1)

                    with act.Fori(0, NE - 1) as e:
                        turn(e, False)
                    turn(NE - 1, True)

                @block.vector
                def _(dve):
                    dve.wait_ge(x_scaled.sem, x_scaled.at(KD))

                    def pick(e, dst, c0, c1, done):
                        nc.vector.tensor_tensor(dst[:, :, c0:c1],
                                                counting[:, c0:c1].unsqueeze(1).to_broadcast([P, TT, c1 - c0]),
                                                places[:, bass.ds(e, 1), :].rearrange("p a t -> p (a t)")
                                                .unsqueeze(2).to_broadcast([P, TT, c1 - c0]),
                                                ALU.is_equal).then_inc(done.sem, 1)
                    pick(0, onehot_few, 0, FEW, few_ready)
                    with dve.Fori(0, NE) as e:
                        pick(e, onehot, FEW, T, rest_ready)
                        for m in range(1, KD, 2):
                            dve.wait_ge(gathered.sem, e * KD + (m + 1))
                            nc.vector.tensor_copy(h[:, m, :], psum[:, m % 4, 0:T]).then_inc(tokens_in[1].sem, 1)
                        for b in range(TT):
                            nc.vector.scalar_tensor_tensor(
                                out=onehot[:, b, :], in0=place_rows[:, bass.ds(e, 1), :].rearrange("p a t -> p (a t)"),
                                scalar=slot_number[:, b:b + 1],
                                in1=weight_rows[:, bass.ds(e, 1), :].rearrange("p a t -> p (a t)"),
                                op0=ALU.is_equal, op1=ALU.mult).then_inc(place_ready.sem, 1)
                        for f in range(FT):
                            dve.wait_ge(gates.sem, e * FT + f + 1)
                            dve.wait_ge(ring_used.sem, e * PER_EXPERT + (base + 2 * f + 2))
                            nc.vector.tensor_tensor(hidden[f], tmp[:, f % 2, :], psum[:, (2 * f + 1) % 4, 0:T],
                                                    ALU.mult).then_inc(hid.sem, 1)
                        for m in range(1, KD, 2):
                            dve.wait_ge(ring_used.sem, e * PER_EXPERT + (base + 2 * FT + m + 1))
                            nc.vector.tensor_copy(h[:, m, :], psum[:, m % 4, 0:T]).then_inc(outputs_in[1].sem, 1)
                        for m in range(1, KD, 2):
                            dve.wait_ge(turned.sem, e * KD + (m + 1))
                            nc.vector.tensor_copy(y_rows[:, :, m * P:(m + 1) * P],
                                                  psum[:, m % 4, 0:T].rearrange("p (b f) -> p b f", b=TT))\
                                .then_inc(rows_in[1].sem, 1)
                        pick(e + 1, onehot_few, 0, FEW, few_ready)
                        dve.wait_ge(added.sem, e * KD)
                        dve.wait_ge(summed.sem, e * (KD - 1) + summed.base)
                        for m in range(KD):
                            dve.wait_ge(spread.sem, e * KD + (m + 1))
                            for s, (t0, t1) in enumerate(SEQS):
                                ins = nc.vector.scalar_tensor_tensor(
                                    out=x[:, m, t0:t1], in0=psum[:, m % 4, t0:t1], scalar=mod[:, 5 * KD + m, s:s + 1],
                                    in1=x[:, m, t0:t1], op0=ALU.mult, op1=ALU.add)
                            ins.then_inc(added.sem, 1)

                @block.gpsimd
                def _(pool):
                    with pool.Fori(0, NE) as e:
                        for m in range(1, KD):
                            pool.wait_ge(added.sem, e * KD + (added.base + m + 1))
                            if m > 1:
                                pool.wait_ge(summed.sem, e * (KD - 1) + (summed.base + m - 1))
                            nc.gpsimd.tensor_tensor(x_sum[:], x[:, 0, :] if m == 1 else x_sum[:], x[:, m, :], ALU.add)\
                                .then_inc(summed.sem, 1)
                        pool.wait_ge(summed.sem, e * (KD - 1) + (summed.base + KD - 1))

        def finish():
            turned, copied, stored = sem("end_turned"), sem("end_copied"), sem("end_stored")
            rows = [u[:, 2 * t:2 * t + 2, :].rearrange("p s w -> p (s w)")[:, 0:D] for t in range(TT)]
            with nc.Block() as block:
                @block.tensor
                def _(pe):
                    for t in range(TT):
                        if t >= 4:
                            pe.wait_ge(copied.sem, copied.at(t - 3))
                        for k in range(KD):
                            ins = nc.tensor.transpose(psum[:, t % 4, k * P:(k + 1) * P], x[:, k, t * P:(t + 1) * P], ident[:])
                        ins.then_inc(turned.sem, turned.up())

                @block.vector
                def _(dve):
                    for t in range(TT):
                        dve.wait_ge(turned.sem, turned.at(t + 1))
                        nc.vector.tensor_copy(rows[t], psum[:, t % 4, :]).then_inc(copied.sem, copied.up())

                @block.sync
                def _(sp):
                    for t in range(TT):
                        sp.wait_ge(copied.sem, copied.at(t + 1))
                        dst = out["yp"][0] if t == 0 else out["ys"][0, (t - 1) * P:t * P, :]
                        sp.dma_start(dst, rows[t]).then_inc(stored.sem, stored.up(16))
                    sp.wait_ge(stored.sem, stored.at(16 * TT))

        start()
        for l in range(DEPTH):
            modulation(l)
            modulate(0)
            project_in(l)
            gla(l)
            gdn(l)
            project_out(l)
            close(l, "ln1", at_a["ln1_g"], at_a["ln1_b"])
            if l % 2 == 1:
                modulate(3)
                route(l)
                mixture(l)
            else:
                feed_forward(l)
            ring_used.n = sum(parts["ffn", l])
            close(l, "ln2", at_a["ln2_g"], at_a["ln2_b"])
        finish()


_INS = ["x_prompt", "x_sample", "c", "state_gla", "state_gdn", "c_ctx", "w_ada", "b_ada", "w_in", "w_out", "conv_w",
        "conv_b", "conv_ln_g", "conv_ln_b", "conv_pw", "gla_w_lr", "gla_b_lr", "gla_norm_g", "gdn_conv_w",
        "gdn_a_log", "gdn_dt_bias", "gdn_norm_g", "sc_conv_w", "ln1_g", "ln1_b", "ln2_g", "ln2_b", "ffn_w_gate",
        "ffn_w_up", "ffn_w_down", "moe_router", "moe_w_gate", "moe_w_up", "moe_w_down"]


def kernel(**inputs):
    import numpy as _np
    import concourse.bacc as _bacc
    from concourse import mybir as _mybir
    from concourse.bass_utils import run_bass_kernel_spmd as _run

    nc = _bacc.Bacc("TRN2", target_bir_lowering=False, num_devices=1)
    arrays, args = {}, {}
    for name in _INS:
        v = _np.ascontiguousarray(inputs[name])
        arrays[f"in_{name}_dram"] = v
        args[name] = nc.dram_tensor(f"in_{name}_dram", v.shape, _mybir.dt.from_np(v.dtype), kind="ExternalInput").ap()
    sp, ss = inputs["x_prompt"].shape, inputs["x_sample"].shape
    outs = {"yp": sp, "ys": ss, "gla": inputs["state_gla"].shape, "gdn": inputs["state_gdn"].shape}
    handles = {n: nc.dram_tensor(f"out_{n}_dram", tuple(s), F32, kind="ExternalOutput").ap() for n, s in outs.items()}
    trunk_kernel(nc, args, handles)
    r = _run(nc, [arrays], core_ids=[0])
    return tuple(r.results[0][f"out_{n}_dram"] for n in ("yp", "ys", "gla", "gdn"))
```
